# Optimizing a Trainium2 kernel written in Bass

```python
import jax, jax.numpy as jnp
from jax import lax
import numpy as np

D_MODEL = 1024
BATCH = 1
SEQ = 512
DEPTH = 2

CTX_LEN = 256
GRID_W = 64

POOL_WINDOWS = (2, 4, 8, 16)
POOL_GROUPS = len(POOL_WINDOWS)
POOL_GROUP_DIM = D_MODEL // 8
POOL_DIM = POOL_GROUPS * POOL_GROUP_DIM
MLA_HEADS = 8
QK_NOPE = 64
QK_ROPE = 32
V_DIM = 64
Q_LORA = D_MODEL // 4
KV_LORA = D_MODEL // 8
QK_DIM = QK_NOPE + QK_ROPE
KV_OFF = POOL_DIM + Q_LORA
MIX_IN = POOL_DIM + Q_LORA + KV_LORA + QK_ROPE
MIX_OUT = POOL_DIM + MLA_HEADS * V_DIM
ROPE_THETA = 10000.0
Q_BLOCK = 128

CONV_WIDTH = 31

N_EXPERTS = 16
EXPERT_FF = D_MODEL
CAPACITY_FACTOR = 2

EPS = 1e-6
N_EVEN = (DEPTH + 1) // 2
N_ODD = DEPTH // 2

kernel_name = "hybrid_pool_mla_conformer_ecmoe_dit"

def rms_norm(x, g):
    xf = x.astype(jnp.float32)
    y = xf * lax.rsqrt(jnp.mean(xf * xf, axis=-1, keepdims=True) + EPS)
    return (y * g.astype(jnp.float32)).astype(x.dtype)

def layer_norm(x, g, b):
    xf = x.astype(jnp.float32)
    mu = jnp.mean(xf, axis=-1, keepdims=True)
    var = jnp.mean(jnp.square(xf - mu), axis=-1, keepdims=True)
    y = (xf - mu) * lax.rsqrt(var + EPS)
    return (y * g.astype(jnp.float32) + b.astype(jnp.float32)).astype(x.dtype)

def modulate(h, shift, scale):
    return h * (1 + scale) + shift

def axial_rope_tables(n_tokens):
    rows = n_tokens // GRID_W
    row = jnp.repeat(jnp.arange(rows), GRID_W).astype(jnp.float32)
    col = jnp.tile(jnp.arange(GRID_W), rows).astype(jnp.float32)
    per_axis = QK_ROPE // 2
    inv_freq = 1.0 / (ROPE_THETA ** (jnp.arange(0, per_axis, 2, dtype=jnp.float32) / per_axis))
    ang = jnp.stack([row[:, None] * inv_freq, col[:, None] * inv_freq], axis=1)
    return jnp.cos(ang), jnp.sin(ang)

def apply_rope(x, cos, sin):
    xr = x.reshape(x.shape[:-1] + (2, 2, QK_ROPE // 4)).astype(jnp.float32)
    x1, x2 = xr[..., 0, :], xr[..., 1, :]
    out = jnp.stack([x1 * cos - x2 * sin, x1 * sin + x2 * cos], axis=-2)
    return out.reshape(x.shape).astype(x.dtype)

def multiscale_pool(u, pool_w, pool_scale):
    b, n, _ = u.shape
    uf = u.astype(jnp.float32)
    csum = jnp.concatenate([jnp.zeros_like(uf[:, :1]), jnp.cumsum(uf, axis=1)], axis=1)
    t = jnp.arange(n)
    outs = []
    for g, w in enumerate(POOL_WINDOWS):
        lo = jnp.clip(t - w // 2, 0, n)
        hi = jnp.clip(t - w // 2 + w, 0, n)
        sl = slice(g * POOL_GROUP_DIM, (g + 1) * POOL_GROUP_DIM)
        cg = csum[..., sl]
        mean = (jnp.take(cg, hi, axis=1) - jnp.take(cg, lo, axis=1)) / (hi - lo).astype(jnp.float32)[:, None]
        outs.append(mean - uf[..., sl])
    d = jnp.stack(outs, axis=2).astype(u.dtype)
    y = jnp.einsum('bngc,gcd->bngd', d, pool_w).reshape(b, n, POOL_DIM)
    return y * pool_scale

def mla_q(zq, q_norm_g, w_uq, rope):
    b, n, _ = zq.shape
    q = (rms_norm(zq, q_norm_g) @ w_uq).reshape(b, n, MLA_HEADS, QK_DIM)
    q_nope, q_rope = q[..., :QK_NOPE], q[..., QK_NOPE:]
    if rope is not None:
        cos, sin = rope
        q_rope = apply_rope(q_rope, cos[:, None], sin[:, None])
    return jnp.concatenate([q_nope, q_rope], axis=-1)

def mla_kv(zkv, kv_norm_g, w_ukv, rope):
    b, n, _ = zkv.shape
    kv = (rms_norm(zkv[..., :KV_LORA], kv_norm_g) @ w_ukv).reshape(b, n, MLA_HEADS, QK_NOPE + V_DIM)
    k_nope, v = kv[..., :QK_NOPE], kv[..., QK_NOPE:]
    k_rope = zkv[..., KV_LORA:]
    if rope is not None:
        cos, sin = rope
        k_rope = apply_rope(k_rope, cos, sin)
    k_rope = jnp.broadcast_to(k_rope[:, :, None, :], (b, n, MLA_HEADS, QK_ROPE))
    return jnp.concatenate([k_nope, k_rope], axis=-1), v

def latent_attention(q, k, v, k_ctx, v_ctx):
    b, n, h, dk = q.shape
    scale = QK_DIM ** -0.5
    lc = k_ctx.shape[1]
    qb = q.reshape(b, n // Q_BLOCK, Q_BLOCK, h, dk).swapaxes(0, 1)

    def block(qblk):
        s = jnp.concatenate([jnp.einsum('bqhd,bkhd->bhqk', qblk, k_ctx),
                             jnp.einsum('bqhd,bkhd->bhqk', qblk, k)], axis=-1)
        p = jax.nn.softmax(s.astype(jnp.float32) * scale, axis=-1).astype(v.dtype)
        return (jnp.einsum('bhqk,bkhd->bqhd', p[..., :lc], v_ctx)
                + jnp.einsum('bhqk,bkhd->bqhd', p[..., lc:], v))

    o = lax.map(block, qb)
    return o.swapaxes(0, 1).reshape(b, n, h * V_DIM)

def context_attention(q, k, v):
    b, n = q.shape[:2]
    s = jnp.einsum('bqhd,bkhd->bhqk', q, k).astype(jnp.float32) * (QK_DIM ** -0.5)
    p = jax.nn.softmax(s, axis=-1).astype(v.dtype)
    return jnp.einsum('bhqk,bkhd->bqhd', p, v).reshape(b, n, MLA_HEADS * V_DIM)

def conformer_conv(h, w_pw1, b_pw1, w_dw, b_dw, ln_g, ln_b, w_pw2, b_pw2):
    a, g = jnp.split(h @ w_pw1 + b_pw1, 2, axis=-1)
    u = a * jax.nn.sigmoid(g)
    u = lax.conv_general_dilated(u, w_dw[:, None, :], window_strides=(1,),
                                 padding=[(CONV_WIDTH // 2, CONV_WIDTH // 2)],
                                 dimension_numbers=('NWC', 'WIO', 'NWC'),
                                 feature_group_count=D_MODEL) + b_dw
    u = jax.nn.silu(layer_norm(u, ln_g, ln_b))
    return u @ w_pw2 + b_pw2

def expert_choice_moe(h, router_w, wg, wu, wd):
    b, n, d = h.shape
    cap = CAPACITY_FACTOR * n // N_EXPERTS
    aff = jax.nn.softmax((h @ router_w).astype(jnp.float32), axis=-1)
    gate, idx = lax.top_k(aff.swapaxes(1, 2), cap)
    xs = jax.vmap(lambda hb, ib: hb[ib])(h, idx)
    a = jnp.einsum('becd,edf->becf', xs, wg)
    u = jnp.einsum('becd,edf->becf', xs, wu)
    y = jnp.einsum('becf,efd->becd', jax.nn.silu(a) * u, wd) * gate[..., None].astype(h.dtype)
    return jax.vmap(lambda yb, ib: jnp.zeros((n, d), h.dtype).at[ib.reshape(-1)].add(yb.reshape(-1, d)))(y, idx)

def setup_inputs(seed: int = 0) -> dict:
    key = jax.random.key(seed)
    ks = jax.random.split(key, 32)
    nrm = lambda k, shape, s: jax.random.normal(k, shape, jnp.float32) * s
    D, L = D_MODEL, DEPTH
    return {
        "x": nrm(ks[0], (BATCH, SEQ, D), 1.0),
        "c": nrm(ks[1], (BATCH, D), 1.0),
        "ctx": nrm(ks[2], (BATCH, CTX_LEN, D), 1.0),
        "c_ctx": nrm(ks[3], (D,), 1.0),
        "ada_w": nrm(ks[4], (L, D, 6 * D), 0.5 * D ** -0.5),
        "ada_b": nrm(ks[5], (L, 6 * D), 0.02),
        "norm1_g": 1.0 + nrm(ks[6], (L, D), 0.02),
        "norm2_g": 1.0 + nrm(ks[7], (L, D), 0.02),
        "mix_w_in": nrm(ks[8], (N_EVEN, D, MIX_IN), D ** -0.5),
        "pool_w": nrm(ks[9], (N_EVEN, POOL_GROUPS, POOL_GROUP_DIM, POOL_GROUP_DIM), POOL_GROUP_DIM ** -0.5),
        "pool_scale": 1.0 + nrm(ks[10], (N_EVEN, POOL_DIM), 0.1),
        "q_norm_g": 1.0 + nrm(ks[11], (N_EVEN, Q_LORA), 0.02),
        "kv_norm_g": 1.0 + nrm(ks[12], (N_EVEN, KV_LORA), 0.02),
        "w_uq": nrm(ks[13], (N_EVEN, Q_LORA, MLA_HEADS * QK_DIM), Q_LORA ** -0.5),
        "w_ukv": nrm(ks[14], (N_EVEN, KV_LORA, MLA_HEADS * (QK_NOPE + V_DIM)), KV_LORA ** -0.5),
        "mix_w_out": nrm(ks[15], (N_EVEN, MIX_OUT, D), MIX_OUT ** -0.5),
        "conv_w_pw1": nrm(ks[16], (N_ODD, D, 2 * D), D ** -0.5),
        "conv_b_pw1": nrm(ks[17], (N_ODD, 2 * D), 0.02),
        "conv_w_dw": nrm(ks[18], (N_ODD, CONV_WIDTH, D), CONV_WIDTH ** -0.5),
        "conv_b_dw": nrm(ks[19], (N_ODD, D), 0.02),
        "conv_ln_g": 1.0 + nrm(ks[20], (N_ODD, D), 0.02),
        "conv_ln_b": nrm(ks[21], (N_ODD, D), 0.02),
        "conv_w_pw2": nrm(ks[22], (N_ODD, D, D), D ** -0.5),
        "conv_b_pw2": nrm(ks[23], (N_ODD, D), 0.02),
        "router_w": nrm(ks[24], (L, D, N_EXPERTS), D ** -0.5),
        "exp_wg": nrm(ks[25], (L, N_EXPERTS, D, EXPERT_FF), D ** -0.5),
        "exp_wu": nrm(ks[26], (L, N_EXPERTS, D, EXPERT_FF), D ** -0.5),
        "exp_wd": nrm(ks[27], (L, N_EXPERTS, EXPERT_FF, D), EXPERT_FF ** -0.5),
        "final_g": 1.0 + nrm(ks[28], (D,), 0.02),
    }

def reference(x, c, ctx, c_ctx, ada_w, ada_b, norm1_g, norm2_g, mix_w_in, pool_w, pool_scale,
              q_norm_g, kv_norm_g, w_uq, w_ukv, mix_w_out, conv_w_pw1, conv_b_pw1, conv_w_dw,
              conv_b_dw, conv_ln_g, conv_ln_b, conv_w_pw2, conv_b_pw2, router_w, exp_wg, exp_wu,
              exp_wd, final_g):
    n = x.shape[1]
    rope = axial_rope_tables(n)
    last_even = ((DEPTH - 1) // 2) * 2
    for l in range(DEPTH):
        even = (l % 2 == 0)
        ctx_update = l < last_even
        i = l // 2
        m = jax.nn.silu(c) @ ada_w[l] + ada_b[l]
        sh1, sc1, g1, sh2, sc2, g2 = [t[:, None, :] for t in jnp.split(m, 6, axis=-1)]
        if even or ctx_update:
            mc = jax.nn.silu(c_ctx) @ ada_w[l] + ada_b[l]
            csh1, csc1, cg1, csh2, csc2, cg2 = jnp.split(mc, 6, axis=-1)
            hc = modulate(rms_norm(ctx, norm1_g[l]), csh1, csc1)
        h = modulate(rms_norm(x, norm1_g[l]), sh1, sc1)
        if even:
            z = h @ mix_w_in[i]
            q = mla_q(z[..., POOL_DIM:KV_OFF], q_norm_g[i], w_uq[i], rope)
            k, v = mla_kv(z[..., KV_OFF:], kv_norm_g[i], w_ukv[i], rope)
            if ctx_update:
                zc = hc @ mix_w_in[i]
                zc_kv = zc[..., KV_OFF:]
            else:
                zc_kv = hc @ mix_w_in[i][:, KV_OFF:]
            k_c, v_c = mla_kv(zc_kv, kv_norm_g[i], w_ukv[i], None)
            attn = latent_attention(q, k, v, k_c, v_c)
            pool = multiscale_pool(z[..., :POOL_DIM], pool_w[i], pool_scale[i])
            y = jnp.concatenate([pool, attn], axis=-1) @ mix_w_out[i]
            if ctx_update:
                q_c = mla_q(zc[..., POOL_DIM:KV_OFF], q_norm_g[i], w_uq[i], None)
                attn_c = context_attention(q_c, k_c, v_c)
                pool_c = multiscale_pool(zc[..., :POOL_DIM], pool_w[i], pool_scale[i])
                yc = jnp.concatenate([pool_c, attn_c], axis=-1) @ mix_w_out[i]
        else:
            conv_args = (conv_w_pw1[i], conv_b_pw1[i], conv_w_dw[i], conv_b_dw[i],
                         conv_ln_g[i], conv_ln_b[i], conv_w_pw2[i], conv_b_pw2[i])
            y = conformer_conv(h, *conv_args)
            if ctx_update:
                yc = conformer_conv(hc, *conv_args)
        x = x + g1 * y
        h2 = modulate(rms_norm(x, norm2_g[l]), sh2, sc2)
        x = x + g2 * expert_choice_moe(h2, router_w[l], exp_wg[l], exp_wu[l], exp_wd[l])
        if ctx_update:
            ctx = ctx + cg1 * yc
            hc2 = modulate(rms_norm(ctx, norm2_g[l]), csh2, csc2)
            ctx = ctx + cg2 * expert_choice_moe(hc2, router_w[l], exp_wg[l], exp_wu[l], exp_wd[l])
    return rms_norm(x, final_g)


_drawn_inputs = setup_inputs


def setup_inputs(seed=0):
    import zlib

    import numpy as np

    out = dict(_drawn_inputs(seed))
    spreads = {}
    factors = {'ctx': 6.266,
     'c_ctx': 2.984,
     'norm1_g': 8.0,
     'norm2_g': 6.322,
     'q_norm_g': 8.0,
     'kv_norm_g': 8.0,
     'conv_b_pw1': 28.027,
     'conv_b_dw': 26.583,
     'conv_ln_g': 37.239,
     'conv_ln_b': 53.746,
     'conv_b_pw2': 28.82,
     'final_g': 7.479}
    for name, (base, spread) in spreads.items():
        noise = np.random.default_rng([zlib.crc32(name.encode()), seed]).standard_normal(out[name].shape)
        drawn = base * np.exp(spread * noise) if base else spread * noise
        out[name] = __import__('jax').numpy.asarray(drawn.astype(out[name].dtype))
    for name, factor in factors.items():
        out[name] = (out[name] * factor).astype(out[name].dtype)
    return out
```

```python
import concourse.bass as bass
from concourse import mybir
from contextlib import ExitStack

D = 1024
N = 512
NCTX = 256
T = N // 128
CT = NCTX // 128
KT = T + CT
K8 = D // 128
HEADS = 8
NOPE = 64
ROPE = 32
VD = 64
QK = NOPE + ROPE
QL = 256
KVL = 128
POOL = 512
LAT = QL + KVL + ROPE
MIX_IN = POOL + LAT
LROW = QL + KVL + 2 * ROPE
CONVW = 31
HALO = CONVW // 2
EXPERTS = 16
PAIRS = EXPERTS // 2
CAP = 2 * N // EXPERTS
SCALE = float(QK) ** -0.5
EPS = 1e-6
SLOTS = 6
SLOT_WORDS = 4096
NB = 6
VEC_ROWS = 5 * K8 + 4 + 2 + 1
PE_TAPS = 4
UNITS = HEADS * T
LAT_ORDER = [4, 5, 0, 1, 2, 3]


def l0_items():
    o = [("params", (), "V"), ("ada", (0,), "S"), ("ada", (1,), "S"), ("sel", (0,), "V"),
         ("ada", (2,), "S"), ("ada", (3,), "S"), ("sel", (1,), "V")]
    o += [("cT", (k,), "VS"[k % 2]) for k in range(K8 // 2)]
    o += [("xT", (k,), "VS"[k % 2]) for k in range(K8)]
    o += [("zlat", (4,), "V"), ("zlat", (5,), "V"), ("zlat", (0,), "V"), ("latT", (4,), "S"),
          ("zpool", (0,), "S"), ("latT", (5,), "S"), ("zlat", (1,), "V"), ("latT", (0,), "S"),
          ("zpool", (1,), "S"), ("zlat", (2,), "V"), ("latT", (1,), "S"), ("zpool", (2,), "S"),
          ("zlat", (3,), "V"), ("latT", (2,), "S"), ("zpool", (3,), "S"), ("latT", (3,), "S")]
    o += [("band", (0,), "V"), ("band", (1,), "V"), ("poolw", (0,), "S"), ("poolw", (1,), "S"),
          ("band", (2,), "V"), ("band", (3,), "V"), ("poolw", (2,), "S"), ("poolw", (3,), "S")]
    o += [("value", (k,), "VS"[k % 2]) for k in range(KT)]
    for s in range(2, 6):
        o += [("ada", (2 * s,), "S"), ("ada", (2 * s + 1,), "S"), ("sel", (s,), "V")]
    o += [("row", (2, 0), "S"), ("row", (2, 1), "V"), ("row", (5, 0), "S"), ("row", (5, 1), "V")]
    return o


def route_items(t):
    return [("hT", (t, 0), "V"), ("hT", (t, 1), "S"), ("logit", (t,), "V")]


def mix_items():
    o = [("oT", (k,), "VS"[k % 2]) for k in range(4)]
    for t in range(T):
        o += [("mix", (t, 0), "V"), ("mix", (t, 1), "V")]
        if t:
            o += route_items(t - 1)
    return o + route_items(T - 1) + [("affT", (), "S"), ("slotT", (), "V")]


def conv_items():
    o = []
    for t in range(T):
        o += [("h1T", (t, 0), "V"), ("h1T", (t, 1), "S")]
    o += [("row", (2, 0), "S"), ("row", (2, 1), "V"), ("row", (5, 0), "S"), ("row", (5, 1), "V")]
    for c in range(K8):
        o += [("pwg", (c,), "S"), ("pwa", (c,), "V")]
        if c:
            o += [("taps", (c - 1,), "V")]
    o += [("taps", (K8 - 1,), "V"), ("mean", (), "V"), ("var", (), "V")]
    for t in range(T):
        o += [("pw2", (t, 0), "V"), ("pw2", (t, 1), "V")]
        if t:
            o += route_items(t - 1)
    return o + route_items(T - 1) + [("affT", (), "S"), ("slotT", (), "V")]


L0, MIX, CONV = l0_items(), mix_items(), conv_items()
ITEMS = L0 + MIX + CONV
IN_L1 = len(L0) + len(MIX)
PLACES = {(n >= IN_L1, kind, args): n for n, (kind, args, _) in enumerate(ITEMS)}


def place(layer, kind, *args):
    return PLACES[(layer == 1, kind, args)]


def drains(engine, through):
    return sum(e == engine for _, _, e in ITEMS[:through + 1])


G_ADA = {b: b if b < 4 else b + 3 for b in range(12)}
G_MIXIN = 4
G_BAND = 6
G_MIXOUT = 15
G_MOE0 = 17
MOE_GRANULES = 12 * PAIRS
G_PW1 = G_MOE0 + MOE_GRANULES
G_PW2 = G_PW1 + 4
G_MOE1 = G_PW2 + 2
G_MOE = [G_MOE0, G_MOE1]
TWO_DMAS = {G_BAND} | {G_PW1 + q for q in range(4)}


def arrivals(g):
    return 16 * sum(1 + (n in TWO_DMAS) for n in range(g % SLOTS, g + 1, SLOTS))


def last_use(g):
    for b, n in G_ADA.items():
        if n == g:
            return place(0, "ada", b)
    if g < G_BAND:
        return place(0, "zpool", T - 1)
    if g == G_BAND:
        return place(0, "poolw", 3)
    if g < G_MOE0:
        return place(0, "mix", T - 1, 1)
    if g < G_PW2:
        return place(1, "pwa", 2 * (g - G_PW1) + 1)
    return place(1, "pw2", T - 1, 1)


class Chain:

    def __init__(self, eng, sem):
        self.eng, self.sem, self.n = eng, sem, 0

    def __call__(self, ins):
        self.n += 1
        ins.then_inc(self.sem, 1)
        self.eng.wait_ge(self.sem, self.n)


def build(nc, x_in, c_in, ctx_in, cctx_in, ada_w, ada_b, norm1_g, norm2_g, mix_w_in, pool_w, pool_scale,
          q_norm_g, kv_norm_g, w_uq, w_ukv, mix_w_out, pw1, b_pw1, w_dw, b_dw, ln_g, ln_b, pw2, b_pw2,
          router_w, exp_wg, exp_wu, exp_wd, final_g, small_tab, rope_tab, band_tab, out):
    fp32 = mybir.dt.float32
    ALU = mybir.AluOpType
    ACT = mybir.ActivationFunctionType
    AX = mybir.AxisListType
    stack = ExitStack()
    with stack:
        def sb(name, shape):
            return stack.enter_context(nc.sbuf_tensor(name, shape, fp32))

        def sem(name):
            return stack.enter_context(nc.semaphore(name))

        ring = sb("ring", [128, SLOTS, SLOT_WORDS])
        x = sb("x", [128, T, D])
        xn = sb("xn", [128, T, D])
        hT = sb("hT", [128, K8, N])
        consts = sb("consts", [128, 128 + 64 + 2])
        ident, iota, pick = consts[:, 0:128], consts[:, 128:192], consts[:, 192:194]
        ones = sb("ones", [128, 128])
        one_dth = sb("one_dth", [128, 128])
        minus_half = sb("minus_half", [128, 1])
        cond_raw = sb("cond_raw", [128, 2, K8])
        cond = sb("cond", [128, K8, 32])
        ada_bias = sb("ada_bias", [128, 2, 6, K8])
        ng = sb("ng", [128, 2, 2, K8])
        cols = sb("cols", [128, 2, 6, 2, K8])
        amp = sb("amp", [128, 2, 2, 2, K8])
        router = sb("router", [128, 2, K8, EXPERTS])
        g1_row = sb("g1_row", [128, D])
        g2_row = sb("g2_row", [128, D])
        dwT = sb("dwT", [128, K8, CONVW])
        vecT = sb("vecT", [128, VEC_ROWS])
        a_bias, g_bias, dw_bias, lng, lnb = (vecT[:, i * K8:(i + 1) * K8] for i in range(5))
        pscale, qg, kvg = vecT[:, 40:44], vecT[:, 44:46], vecT[:, 46:47]
        ssq = sb("ssq", [128, 22])
        ms = sb("ms", [128, 22])
        rstd = sb("rstd", [128, 22])
        lat_ssq = sb("lat_ssq", [128, KT, 2])
        lat_ms = sb("lat_ms", [128, KT, 2])
        lat_rstd = sb("lat_rstd", [128, KT, 2])
        ada_rows = sb("ada_rows", [128, 2, N])
        ARENA = 11450
        arena = sb("arena", [128, ARENA])

        def carver(at):
            here = [at]

            def cut(*shape):
                words = 1
                for s in shape:
                    words *= s
                v = arena[:, here[0]:here[0] + words]
                here[0] += words
                assert here[0] <= ARENA, here[0]
                if len(shape) == 2:
                    v = v.rearrange("p (a b) -> p a b", a=shape[0])
                if len(shape) == 3:
                    v = v.rearrange("p (a b c) -> p a b c", a=shape[0], b=shape[1])
                return v
            return cut

        cut = carver(0)
        qT = cut(N)
        kT = cut(KT * 128)
        kvT = cut(KT * 128)
        hcT = arena[:, 0:K8 * NCTX].rearrange("p (k n) -> p k n", k=K8)
        uq = cut(2, HEADS * QK)
        ukv = cut(HEADS * (NOPE + VD))
        wq_stage = cut(2, 128)
        wk_stage = cut(NOPE)
        qlatT = cut(2, N)
        rope_q = cut(N)
        rope_k = cut(2, T, ROPE)
        head_cols = cut(4, T)
        maxima, biases, sums, recips = (head_cols[:, i, :] for i in range(4))
        kr_tmp = cut(2, ROPE)
        values = cut(KT, HEADS * VD)
        values_flat = values.rearrange("p a b -> p (a b)")
        ctx_x = values_flat[:, 0:CT * D].rearrange("p (a b) -> p a b", a=CT)
        dw_rows = values_flat[:, CT * D:CT * D + D]
        exps = cut(2, KT * 128)
        exps_flat = exps.rearrange("p a b -> p (a b)")
        vec_rows = exps_flat[:, 1280:1408]
        lat_junk = exps_flat[:, 1024:1280]
        lat_junk2 = exps_flat[:, 1408:1536]
        diag0 = exps_flat[:, 0:D].rearrange("p (k n) -> p k n", k=K8)
        catT = hT
        hT_flat = hT[:, :, :].rearrange("p a b -> p (a b)")
        xn_flat = xn[:, :, :].rearrange("p a b -> p (a b)")
        pT = hT_flat[:, 4 * N:4 * N + 2 * KT * 128].rearrange("p (a b) -> p a b", a=2)
        diffT = hT_flat[:, 4 * N:6 * N].rearrange("p (a b) -> p a b", a=2)
        u_pool = xn_flat[:, 0:T * N].rearrange("p (a b) -> p a b", a=T)
        o_heads = xn_flat[:, T * N:2 * T * N].rearrange("p (a b) -> p a b", a=T)
        lat = xn_flat[:, T * N:T * N + 2 * LROW].rearrange("p (a b) -> p a b", a=2)

        cut = carver(0)
        onehot = cut(T, 128)
        gated = cut(T, 128)
        gatedT = cut(N)
        xsT = cut(K8, 128)
        silu_g = cut(2, N)
        act = cut(D)
        actT = cut(K8, 128)
        y_rows = cut(D)
        ada_slot = hT

        cut = carver(9700)
        aff = cut(T, EXPERTS)
        shifted = cut(T, EXPERTS)
        slot_of = cut(T, EXPERTS)
        aff_cols = cut(3, T)
        top8 = cut(8)
        affT = cut(N)
        left = cut(N)
        running = cut(N)

        cut = carver(0)
        u_pad = cut(2, N + 2 * HALO)
        conv = cut(K8, N)
        tap_diag = cut(2, PE_TAPS, 128)
        sig = cut(2, N)
        ln_sq = cut(2, N)
        ln_mean = cut(N)
        ln_rstd = cut(N)
        diag1 = sig.rearrange("p a b -> p (a b)").rearrange("p (k n) -> p k n", k=K8)
        bias_row = ln_sq.rearrange("p a b -> p (a b)")

        PS = stack.enter_context(nc.psum_tensor("PS", [128, 8, N], fp32))

        cond_in, x_arrived, ctx_arrived, consts_in, params_in, small_in, attn_w_in = map(
            sem, ("cond_in", "x_arrived", "ctx_arrived", "consts_in", "params_in", "small_in", "attn_w_in"))
        slot_in = [sem(f"slot_in{q}") for q in range(SLOTS)]
        moe_used = sem("moe_used")
        ones_set, cond_ready, filled, drained_v, drained_s = map(
            sem, ("ones_set", "cond_ready", "filled", "drained_v", "drained_s"))
        drained = {"V": drained_v, "S": drained_s}
        v_chain, s_chain, p_chain = sem("v_chain"), sem("s_chain"), sem("p_chain")
        ssq_ready, rstd_ready, xn_ready, x_updated = map(sem, ("ssq_ready", "rstd_ready", "xn_ready", "x_updated"))
        cols_ready, diag_ready = sem("cols_ready"), sem("diag_ready")
        lat_ssq_ready, lat_rstd_ready = sem("lat_ssq_ready"), sem("lat_rstd_ready")
        staged, projected, q_nope_done, k_nope_done, q_rope_done = map(
            sem, ("staged", "projected", "q_nope_done", "k_nope_done", "q_rope_done"))
        max_step, scores_ready, bias_ready, exp_done, pT_ready, pT_drained, o_ready, recip_done, o_done = map(
            sem, ("max_step", "scores_ready", "bias_ready", "exp_done", "pT_ready", "pT_drained", "o_ready", "recip_done",
                  "o_done"))
        aff_exp_done, aff_ready, slots_ready = map(
            sem, ("aff_exp_done", "aff_ready", "slots_ready"))
        onehot_built, xs_filled, xs_drained_v, xs_drained_s, gT_filled, gT_drained = map(
            sem, ("onehot_built", "xs_filled", "xs_drained_v", "xs_drained_s", "gT_filled", "gT_drained"))
        silu_done, act_done, aT_filled, aT_drained_v, aT_drained_s, y_done, scat_filled, scat_added = map(
            sem, ("silu_done", "act_done", "aT_filled", "aT_drained_v", "aT_drained_s", "y_done", "scat_filled",
                  "scat_added"))
        ada_in, rows_filled, rows_drained, sel_filled, sel_drained = map(
            sem, ("ada_in", "rows_filled", "rows_drained", "sel_filled", "sel_drained"))
        halo_set, tap_diag_ready, sq_ready, sq_used = map(
            sem, ("halo_set", "tap_diag_ready", "sq_ready", "sq_used"))
        centred, ln_rstd_ready, scaled, swish_done, bias_in, bias_added = map(
            sem, ("centred", "ln_rstd_ready", "scaled", "swish_done", "bias_in", "bias_added"))
        final_in, out_ready, out_done = sem("final_in"), sem("out_ready"), sem("out_done")

        block = stack.enter_context(nc.Block())

        NORM = {("n1", 0): 0, "ctx": 4, ("n2", 0): 6, ("n1", 1): 10, ("n2", 1): 14, "final": 18}

        def column(v):
            return v.rearrange("(p k) -> p k", k=K8)

        def slot(g):
            return ring[:, g % SLOTS, :]

        @block.sync
        def _(sp):
            sp.dma_start(cond_raw[:, 0, :], column(c_in[0, :])).then_inc(cond_in, 16)
            sp.dma_start(cond_raw[:, 1, :], column(cctx_in)).then_inc(cond_in, 16)
            sp.dma_start(consts[:, :], small_tab).then_inc(consts_in, 16)
            sp.dma_start(x[:, :, :], x_in[0, :, :].rearrange("(t p) d -> p t d", p=128)).then_inc(x_arrived, 16)
            sp.dma_start(ctx_x, ctx_in[0, :, :].rearrange("(t p) d -> p t d", p=128)).then_inc(ctx_arrived, 16)

            def slot_free(g):
                before = g - SLOTS
                if G_MOE0 <= before < G_PW1:
                    sp.wait_ge(moe_used, before - G_MOE0 + 1)
                else:
                    sp.wait_ge(filled, last_use(before) + 1)

            def load(g, parts):
                assert len(parts) == 1 + (g in TWO_DMAS)
                if g >= SLOTS:
                    slot_free(g)
                for dst, src in parts:
                    sp.dma_start(dst, src).then_inc(slot_in[g % SLOTS], 16)

            def load_ada(b):
                g = G_ADA[b]
                load(g, [(slot(g).rearrange("p (k n) -> p k n", k=K8),
                          ada_w[0, :, b * N:(b + 1) * N].rearrange("(p k) n -> p k n", k=K8))])

            for b in range(4):
                load_ada(b)
            sp.dma_start(dw_rows[0:CONVW, :], w_dw[0, :, :]).then_inc(params_in, 16)
            at = 0
            for v in (b_pw1[0, :], b_dw[0, :], ln_g[0, :], ln_b[0, :], pool_scale[0, :], q_norm_g[0, :], kv_norm_g[0, :]):
                n = v.shape[0] // 128
                sp.dma_start(vec_rows[at:at + n, :], v.rearrange("(c p) -> c p", p=128)).then_inc(params_in, 16)
                at += n
            assert at == VEC_ROWS
            for l in range(2):
                sp.dma_start(ada_bias[:, l, :, :], ada_b[l, :].rearrange("(s p k) -> p s k", s=6, k=K8))\
                  .then_inc(small_in, 16)
                sp.dma_start(ng[:, l, 0, :], column(norm1_g[l, :])).then_inc(small_in, 16)
                sp.dma_start(ng[:, l, 1, :], column(norm2_g[l, :])).then_inc(small_in, 16)
                sp.dma_start(router[:, l, :, :], router_w[l, :, :].rearrange("(p k) e -> p k e", k=K8))\
                  .then_inc(small_in, 16)
            for h in range(2):
                g = G_MIXIN + h
                load(g, [(slot(g)[:, 0:4 * MIX_IN].rearrange("p (k n) -> p k n", k=4),
                          mix_w_in[0, :, :].rearrange("(p h k) n -> p h k n", h=2, k=4)[:, h, :, :])])
            sp.dma_start(rope_q, rope_tab[:, 0:N]).then_inc(attn_w_in, 16)
            sp.dma_start(rope_k.rearrange("p a t r -> p (a t r)"), rope_tab[:, N:N + 2 * T * ROPE])\
              .then_inc(attn_w_in, 16)
            sp.dma_start(uq, w_uq[0, :, :].rearrange("(k p) n -> p k n", p=128)).then_inc(attn_w_in, 16)
            sp.dma_start(ukv, w_ukv[0, :, :]).then_inc(attn_w_in, 16)
            load(G_BAND, [(slot(G_BAND)[:, 0:20 * 128], band_tab),
                          (slot(G_BAND)[:, 20 * 128:24 * 128].rearrange("p (g n) -> p g n", g=4),
                           pool_w[0, :, :, :].rearrange("g p n -> p g n"))])
            for b in range(4, 12):
                load_ada(b)
            for h in range(2):
                g = G_MIXOUT + h
                load(g, [(slot(g).rearrange("p (k n) -> p k n", k=4),
                          mix_w_out[0, h * N:(h + 1) * N, :].rearrange("(k p) n -> p k n", p=128))])

            def load_pair(l, j, ada):
                for q in range(12):
                    if ada and q == 3:
                        sp.wait_ge(filled, place(0, "logit", T - 1) + 1)
                        if not isinstance(j, int):
                            sp.wait_ge(rows_filled, j * 2)
                        load_next_ada(j * 2)
                    if ada and q == 8:
                        sp.wait_ge(rows_filled, j * 2 + 1)
                        load_next_ada(j * 2 + 1)
                    w = (exp_wg, exp_wu, exp_wd)[q // 4]
                    src = w[l, :, :, :].rearrange("(g e) (p k) n -> g p e (k n)", e=2, k=K8)
                    s = (G_MOE[l] + q) % SLOTS
                    if isinstance(j, int) and j == 0 and q < SLOTS:
                        slot_free(G_MOE[l] + q)
                    else:
                        sp.wait_ge(moe_used, j * 12 + (MOE_GRANULES * l + q - SLOTS + 1))
                    sp.dma_start(ring[:, s, :].rearrange("p (e n) -> p e n", e=2),
                                 src[j, :, :, 2 * D * (q % 4):2 * D * (q % 4 + 1)]).then_inc(slot_in[s], 16)

            def load_next_ada(b):
                src = ada_w[1, :, :].rearrange("(p k) (b n) -> b p k n", k=K8, n=N)
                sp.dma_start(ada_slot[:, :, :], src[b, :, :, :]).then_inc(ada_in, 16)

            load_pair(0, 0, True)
            with sp.Fori(1, 6, 1) as j:
                load_pair(0, j, True)
            load_pair(0, 6, False)
            load_pair(0, 7, False)
            for q in range(4):
                g = G_PW1 + q
                dst = slot(g).rearrange("p (k h c) -> p k h c", k=K8, h=2)
                src = pw1[0, :, :].rearrange("(p k) (h q c) -> p k h q c", k=K8, h=2, q=4)
                load(g, [(dst[:, :, h, :], src[:, :, h, q, :]) for h in range(2)])
            for h in range(2):
                g = G_PW2 + h
                load(g, [(slot(g).rearrange("p (k n) -> p k n", k=4),
                          pw2[0, h * N:(h + 1) * N, :].rearrange("(k p) n -> p k n", p=128))])
            load_pair(1, 0, False)
            with sp.Fori(1, 8, 1) as j:
                load_pair(1, j, False)
            for t in range(T):
                sp.wait_ge(out_ready, t + 1)
                sp.dma_start(out[0, t * 128:(t + 1) * 128, :], xn[:, t, :]).then_inc(out_done, 16)
            sp.wait_ge(out_done, 16 * T)

        @block.tensor
        def _(pe):
            def wait_granule(g):
                pe.wait_ge(slot_in[g % SLOTS], arrivals(g))

            def transpose(o, i, rows=128):
                return nc.tensor.transpose(o, i, ident[0:rows, 0:rows])

            def drained_through(n, engines="VS"):
                for e in engines:
                    if drains(e, n):
                        pe.wait_ge(drained[e], drains(e, n))

            def ada_block(w, bank):
                for k in range(K8):
                    r = 32 * (k % 4)
                    last = nc.tensor.matmul(PS[r:r + 32, bank, :], cond[:, k, :], w[:, k, :],
                                            start=k < 4, stop=k >= 4)
                return last

            def ada_select(bank):
                for h in range(2):
                    for k in range(K8):
                        last = nc.tensor.matmul(PS[64 * h:64 * h + 64, bank, 2 * k:2 * k + 2],
                                                ada_rows[:, h, k::K8], pick, start=True, stop=True)
                return last

            def fill(n):
                l = n >= IN_L1
                kind, args, _ = ITEMS[n]
                bank = n % NB
                if n >= NB and n not in (len(L0), IN_L1):
                    e = ITEMS[n - NB][2]
                    pe.wait_ge(drained[e], drains(e, n - NB))
                B = PS[:, bank, :]
                if kind == "params":
                    pe.wait_ge(consts_in, 16)
                    pe.wait_ge(params_in, 16 * 8)
                    for c in range(K8):
                        transpose(B[:, c * CONVW:(c + 1) * CONVW], dw_rows[0:CONVW, c * 128:(c + 1) * 128], CONVW)
                    last = transpose(B[:, 256:256 + VEC_ROWS], vec_rows[0:VEC_ROWS, :], VEC_ROWS)
                elif kind == "ada":
                    g = G_ADA[args[0]]
                    pe.wait_ge(cond_ready, 2)
                    wait_granule(g)
                    w = slot(g).rearrange("p (k n) -> p k n", k=K8)
                    last = ada_block(w, bank)
                elif kind == "sel":
                    drained_through(place(0, "ada", 2 * args[0] + 1), "S")
                    last = ada_select(bank)
                elif kind in ("xT", "cT"):
                    pe.wait_ge(xn_ready, 6)
                    if kind == "xT":
                        for t in range(T):
                            last = transpose(B[:, t * 128:(t + 1) * 128], xn[:, t, args[0]::K8])
                    else:
                        for i in range(4):
                            last = transpose(B[:, i * 128:(i + 1) * 128],
                                             ctx_x[:, i % 2, 2 * args[0] + i // 2::K8])
                elif kind in ("zlat", "zpool"):
                    drained_through(place(0, "xT", K8 - 1))
                    wait_granule(G_MIXIN)
                    wait_granule(G_MIXIN + 1)
                    t = args[0]
                    a, b = (0, POOL) if kind == "zpool" else (POOL, MIX_IN) if t < T else (POOL + QL, MIX_IN)
                    for k in range(K8):
                        w = slot(G_MIXIN + k // 4)[:, (k % 4) * MIX_IN + a:(k % 4) * MIX_IN + b]
                        h = hT[:, k, t * 128:(t + 1) * 128] if t < T else hcT[:, k, (t - T) * 128:(t - T + 1) * 128]
                        last = nc.tensor.matmul(B[:, 0:b - a], h, w, start=k == 0, stop=k == K8 - 1)
                elif kind == "latT":
                    t = args[0]
                    pe.wait_ge(drained_v, drains("V", place(0, "zlat", t)))
                    row = lat[:, LAT_ORDER.index(t) % 2, :]
                    if t < T:
                        for i in range(2):
                            transpose(B[:, i * 128:(i + 1) * 128], row[:, i * 128:(i + 1) * 128])
                    transpose(B[:, 256:384], row[:, QL:QL + KVL])
                    last = transpose(B[0:64, 384:512], row[:, QL + KVL:LROW])
                elif kind == "band":
                    g = args[0]
                    drained_through(place(0, "zpool", T - 1), "S")
                    if g == 0:
                        wait_granule(G_BAND)
                    bands = slot(G_BAND)[:, 0:20 * 128].rearrange("p (g b n) -> p g b n", g=4, b=5)
                    for o in range(T):
                        near = [i for i in (o - 1, o, o + 1) if 0 <= i < T]
                        for i in near:
                            b = i - o + 1 if i != o else 3 if o == 0 else 4 if o == T - 1 else 1
                            last = nc.tensor.matmul(B[:, o * 128:(o + 1) * 128], u_pool[:, i, g * 128:(g + 1) * 128],
                                                    bands[:, g, b, :], start=i == near[0], stop=i == near[-1])
                elif kind == "poolw":
                    g = args[0]
                    pe.wait_ge(drained_v, drains("V", place(0, "band", g)))
                    w = slot(G_BAND)[:, 20 * 128:24 * 128].rearrange("p (g n) -> p g n", g=4)
                    last = nc.tensor.matmul(B, w[:, g, :], diffT[:, g % 2, :], start=True, stop=True)
                elif kind == "value":
                    kt = args[0]
                    drained_through(place(0, "latT", 3), "S")
                    pe.wait_ge(attn_w_in, 16 * 4)
                    w = ukv.rearrange("p (h e) -> p h e", h=HEADS)[:, :, NOPE:NOPE + VD]
                    last = nc.tensor.matmul(B, kvT[:, kt * 128:(kt + 1) * 128], w, start=True, stop=True)
                elif kind == "row":
                    s, half = args
                    pe.wait_ge(diag_ready, 2 * l + (1 if s == 2 else 2))
                    diag = diag1 if l else diag0
                    last = nc.tensor.matmul(B, ones[:, :], diag[:, 4 * half:4 * half + 4, :].rearrange("p a b -> p (a b)"),
                                            start=True, stop=True)
                elif kind == "oT":
                    pe.wait_ge(o_done, UNITS)
                    for t in range(T):
                        last = transpose(B[:, t * 128:(t + 1) * 128], o_heads[:, t, args[0] * 128:(args[0] + 1) * 128])
                elif kind == "mix":
                    t, half = args
                    drained_through(place(0, "oT", 3))
                    wait_granule(G_MIXOUT)
                    wait_granule(G_MIXOUT + 1)
                    for k in range(K8):
                        w = slot(G_MIXOUT + k // 4)[:, (k % 4) * D + half * N:(k % 4) * D + half * N + N]
                        last = nc.tensor.matmul(B, catT[:, k, t * 128:(t + 1) * 128], w, start=k == 0, stop=k == K8 - 1)
                elif kind in ("hT", "h1T"):
                    t, half = args
                    m = NORM[("n2", int(l))] if kind == "hT" else NORM[("n1", 1)]
                    pe.wait_ge(xn_ready, m + t + 1)
                    for i in range(4):
                        last = transpose(B[:, i * 128:(i + 1) * 128], xn[:, t, 4 * half + i::K8])
                elif kind == "logit":
                    t = args[0]
                    drained_through(n - 1)
                    for k in range(K8):
                        last = nc.tensor.matmul(B[:, 0:EXPERTS], hT[:, k, t * 128:(t + 1) * 128],
                                                router[:, int(l), k, :], start=k == 0, stop=k == K8 - 1)
                elif kind == "affT":
                    pe.wait_ge(aff_ready, T * (1 + l))
                    for t in range(T):
                        last = transpose(B[0:EXPERTS, t * 128:(t + 1) * 128], aff[:, t, :])
                elif kind == "slotT":
                    pe.wait_ge(slots_ready, 1 + l)
                    for t in range(T):
                        last = transpose(B[:, t * EXPERTS:(t + 1) * EXPERTS],
                                         left[0:EXPERTS, t * 128:(t + 1) * 128], EXPERTS)
                elif kind in ("pwg", "pwa"):
                    c = args[0]
                    drained_through(place(1, "h1T", T - 1, 1))
                    g = G_PW1 + c // 2
                    wait_granule(g)
                    w = slot(g).rearrange("p (k h c) -> p k h c", k=K8, h=2)
                    for k in range(K8):
                        last = nc.tensor.matmul(B, w[:, k, int(kind == "pwg"), (c % 2) * 128:(c % 2) * 128 + 128],
                                                hT[:, k, :], start=k == 0, stop=k == K8 - 1)
                elif kind == "taps":
                    c = args[0]
                    pe.wait_ge(drained_v, drains("V", place(1, "pwa", c)))
                    pe.wait_ge(tap_diag_ready, c + 1)
                    for i in range(PE_TAPS):
                        j = CONVW - PE_TAPS + i
                        last = nc.tensor.matmul(B, tap_diag[:, c % 2, i, :], u_pad[:, c % 2, j:j + N],
                                                start=i == 0, stop=i == PE_TAPS - 1)
                    last.then_inc(filled, 1)
                    if c:
                        pe.wait_ge(drained_v, drains("V", place(1, "taps", c - 1)))
                        nc.tensor.matmul(PS[:, 6, :], one_dth[:, :], conv[:, c - 1, :], start=c == 1, stop=False)
                    return
                elif kind == "mean":
                    pe.wait_ge(drained_v, drains("V", place(1, "taps", K8 - 1)))
                    last = nc.tensor.matmul(PS[:, 6, :], one_dth[:, :], conv[:, K8 - 1, :], start=False, stop=True)
                elif kind == "var":
                    for c in range(K8):
                        pe.wait_ge(sq_ready, c + 1)
                        last = nc.tensor.matmul(PS[:, 7, :], one_dth[:, :], ln_sq[:, c % 2, :],
                                                start=c == 0, stop=c == K8 - 1)
                        if c < K8 - 1:
                            last.then_inc(sq_used, 1)
                elif kind == "pw2":
                    t, half = args
                    wait_granule(G_PW2)
                    wait_granule(G_PW2 + 1)
                    for k in range(K8):
                        pe.wait_ge(swish_done, k + 1)
                        w = slot(G_PW2 + k // 4)[:, (k % 4) * D + half * N:(k % 4) * D + half * N + N]
                        last = nc.tensor.matmul(B, conv[:, k, t * 128:(t + 1) * 128], w, start=k == 0, stop=k == K8 - 1)
                last.then_inc(filled, 1)

            pe.wait_ge(ones_set, 3)
            for n in range(len(L0)):
                fill(n)

            drained_through(len(L0) - 1)
            S = [PS[:, 2 * b:2 * b + 2, :].rearrange("p a b -> p (a b)") for b in range(2)]
            PT = PS[:, 4:6, :].rearrange("p a b -> p (a b)")

            def project(h):
                pe.wait_ge(staged, h + 1)
                if not isinstance(h, int) or h > 0:
                    pe.wait_ge(o_done, 4 * h - 2)
                for k in range(2):
                    nc.tensor.matmul(PS[:, 7, :], wq_stage[:, k, :], qlatT[:, k, :], start=k == 0, stop=k == 1)
                nc.tensor.matmul(S[0][0:NOPE, 0:512], wk_stage, kvT[:, 0:512], start=True, stop=True)
                nc.tensor.matmul(S[0][0:NOPE, 512:768], wk_stage, kvT[:, 512:768], start=True, stop=True)\
                  .then_inc(projected, 1)

            def score(h, qt):
                if not (isinstance(h, int) and h == 0 and qt < 2):
                    pe.wait_ge(exp_done, 4 * h + qt - 1)
                pe.wait_ge(q_nope_done, h + 1)
                pe.wait_ge(k_nope_done, h + 1)
                pe.wait_ge(q_rope_done, h + 1)
                for a, b in ((0, 512), (512, 768)):
                    last = nc.tensor.matmul(S[qt % 2][:, a:b], qT[:, qt * 128:(qt + 1) * 128], kT[:, a:b],
                                            start=True, stop=True)
                last.then_inc(scores_ready, 1)

            def turn(h, qt):
                pe.wait_ge(exp_done, 4 * h + qt + 1)
                if not (isinstance(h, int) and h == 0 and qt == 0):
                    pe.wait_ge(pT_drained, 4 * h + qt)
                for k in range(KT):
                    last = transpose(PT[:, k * 128:(k + 1) * 128], exps[:, qt % 2, k * 128:(k + 1) * 128])
                last.then_inc(pT_ready, 1)

            def weigh(h, qt, v_at):
                pe.wait_ge(pT_drained, 4 * h + qt + 1)
                if not (isinstance(h, int) and h == 0 and qt < 2):
                    pe.wait_ge(o_done, 4 * h + qt - 1)
                for k in range(KT):
                    last = nc.tensor.matmul(PS[:, 6 + qt % 2, 0:VD], pT[:, qt % 2, k * 128:(k + 1) * 128],
                                            values[:, k, bass.ds(v_at, VD)], start=k == 0, stop=k == KT - 1)
                last.then_inc(o_ready, 1)

            def head(h, first, more):
                for qt in range(T):
                    prev, prev2 = (h, qt - 1) if qt else (h - 1, 3), (h, qt - 2) if qt > 1 else (h - 1, qt + 2)
                    if qt == 0:
                        if not first:
                            weigh(*prev2, prev2[0] * VD)
                            turn(*prev)
                        score(h, qt)
                    else:
                        score(h, qt)
                        if not (first and qt < 2):
                            weigh(*prev2, prev2[0] * VD)
                        turn(*prev)
                if more:
                    project(h + 1)

            project(0)
            head(0, True, True)
            with pe.Fori(1, HEADS - 1, 1) as h:
                head(h, False, True)
            head(HEADS - 1, False, False)
            weigh(HEADS - 1, 2, (HEADS - 1) * VD)
            turn(HEADS - 1, 3)
            weigh(HEADS - 1, 3, (HEADS - 1) * VD)
            pe.wait_ge(pT_drained, UNITS)
            pe.wait_ge(o_done, UNITS)
            for n in range(len(L0), IN_L1):
                fill(n)

            def gather(g):
                pe.wait_ge(onehot_built, g + 1)
                for k in range(K8):
                    for t in range(T):
                        last = nc.tensor.matmul(PS[:, k // 4, (k % 4) * 128:(k % 4 + 1) * 128], xn[:, t, k::K8],
                                                onehot[:, t, :], start=t == 0, stop=t == T - 1)
                    if k % 4 == 3:
                        last.then_inc(xs_filled, 1)

            def turn_gated(g):
                for t in range(T):
                    last = transpose(PS[:, 2, t * 128:(t + 1) * 128], gated[:, t, :])
                last.then_inc(gT_filled, 1)

            def half_products(l, g, base, q0, lhs, bank):
                for q in range(4):
                    n = G_MOE[l] + q0 + q
                    s = n % SLOTS
                    pe.wait_ge(slot_in[s], arrivals(n) + base * 32)
                    w = ring[:, s, :].rearrange("p (e k n) -> p e k n", e=2, k=2)
                    for kk in range(2):
                        k = 2 * q + kk
                        for half in range(2):
                            for e in range(2):
                                last = nc.tensor.matmul(PS[64 * e:64 * e + 64, bank + half, :],
                                                        lhs[:, k, 64 * e:64 * e + 64],
                                                        w[:, e, kk, half * N:(half + 1) * N],
                                                        start=k == 0, stop=k == K8 - 1)
                    last.then_inc(moe_used, 1)

            def pair(l, j, ada, more):
                g = j + PAIRS * l
                pe.wait_ge(xs_drained_v, g + 1)
                pe.wait_ge(xs_drained_s, g + 1)
                half_products(l, g, j, 0, xsT, 0)
                if ada:
                    pe.wait_ge(ada_in, j * 32 + 16)
                    ada_block(ada_slot, 4).then_inc(rows_filled, 1)
                pe.wait_ge(gT_drained, g + 1)
                half_products(l, g, j, 4, xsT, 2)
                if ada:
                    pe.wait_ge(ada_in, j * 32 + 32)
                    ada_block(ada_slot, 5).then_inc(rows_filled, 1)
                pe.wait_ge(act_done, 2 * g + 2)
                for k in range(K8):
                    last = transpose(PS[:, 6 + k // 4, (k % 4) * 128:(k % 4 + 1) * 128], act[:, k::K8])
                    if k % 4 == 3:
                        last.then_inc(aT_filled, 1)
                if ada:
                    pe.wait_ge(rows_drained, j * 2 + 2)
                    ada_select(4).then_inc(sel_filled, 1)
                    pe.wait_ge(sel_drained, j + 1)
                pe.wait_ge(aT_drained_v, g + 1)
                pe.wait_ge(aT_drained_s, g + 1)
                half_products(l, g, j, 8, actT, 4)
                if more:
                    gather(g + 1)
                pe.wait_ge(y_done, 2 * g + 2)
                for i in range(2 * T):
                    if i >= 2:
                        pe.wait_ge(scat_added, g * 8 + i - 1)
                    nc.tensor.matmul(PS[:, 6 + i % 2, :], gatedT[:, (i // 2) * 128:(i // 2 + 1) * 128],
                                     y_rows[:, (i % 2) * N:(i % 2 + 1) * N], start=True, stop=True)\
                      .then_inc(scat_filled, 1)
                if more:
                    turn_gated(g + 1)
                pe.wait_ge(scat_added, g * 8 + 8)

            def mixture(l):
                gather(PAIRS * l)
                turn_gated(PAIRS * l)
                if l == 0:
                    with pe.Fori(0, 6, 1) as j:
                        pair(0, j, True, True)
                    pair(0, 6, False, True)
                else:
                    with pe.Fori(0, 7, 1) as j:
                        pair(1, j, False, True)
                pair(l, 7, False, False)

            drained_through(IN_L1 - 1)
            mixture(0)
            for n in range(IN_L1, len(ITEMS)):
                fill(n)
            drained_through(len(ITEMS) - 1)
            mixture(1)

        @block.scalar
        def _(act_e):
            sc = nc.scalar
            chain = Chain(act_e, s_chain)

            def square(m, source, junk):
                sc.activation(junk, source, ACT.Square, accum_out=ssq[:, m:m + 1]).then_inc(ssq_ready, 1)

            def drain(n):
                l = int(n >= IN_L1)
                kind, args, engine = ITEMS[n]
                B = PS[:, n % NB, :]
                if engine == "S":
                    act_e.wait_ge(filled, n + 1)
                    if drains("S", n - 1):
                        act_e.wait_ge(drained_s, drains("S", n - 1))
                if kind == "zlat":
                    t = args[0]
                    act_e.wait_ge(filled, n + 1)
                    if t != LAT_ORDER[0]:
                        act_e.wait_ge(lat_ssq_ready, LAT_ORDER.index(t))
                    off = 0
                    if t < T:
                        sc.activation(lat_junk[:, 0:QL], B[:, 0:QL], ACT.Square, accum_out=lat_ssq[:, t, 0:1])
                        off = QL
                    sc.activation(lat_junk2, B[:, off:off + KVL], ACT.Square, accum_out=lat_ssq[:, t, 1:2])\
                      .then_inc(lat_ssq_ready, 1)
                    return
                if kind in ("mix", "pw2") and args[1] == 1:
                    t = args[0]
                    act_e.wait_ge(x_updated, 8 * l + 2 * t + 2)
                    m = NORM[("n2", l)] + t
                    square(m, x[:, t, :], xn[:, t, :])
                    return
                if kind == "logit":
                    t = args[0]
                    act_e.wait_ge(drained_v, drains("V", n))
                    sc.activation(shifted[:, t, :], shifted[:, t, :], ACT.Exp, accum_out=aff_cols[:, 1, t:t + 1])\
                      .then_inc(aff_exp_done, 1)
                    return
                if kind == "mean":
                    for c in range(K8):
                        act_e.wait_ge(centred, c + 1)
                        if c >= 2:
                            act_e.wait_ge(sq_used, c - 1)
                        sc.activation(ln_sq[:, c % 2, :], conv[:, c, :], ACT.Square).then_inc(sq_ready, 1)
                    return
                if kind == "var":
                    for c in range(K8):
                        act_e.wait_ge(scaled, c + 1)
                        sc.activation(conv[:, c, :], conv[:, c, :], ACT.Silu, bias=lnb[:, c:c + 1],
                                      scale=lng[:, c:c + 1]).then_inc(swish_done, 1)
                    return
                if engine != "S":
                    return
                if kind == "ada":
                    last = sc.activation(ada_rows[:, args[0] % 2, :], B, ACT.Copy)
                elif kind == "xT":
                    act_e.wait_ge(drained_v, drains("V", place(0, "sel", 1)))
                    k = args[0]
                    last = sc.activation(hT[:, k, :], B, ACT.Identity, bias=cols[:, 0, 0, 0, k:k + 1],
                                         scale=amp[:, 0, 0, 0, k:k + 1])
                elif kind == "cT":
                    act_e.wait_ge(drained_v, drains("V", place(0, "sel", 1)))
                    for i in range(2):
                        k = 2 * args[0] + i
                        last = sc.activation(hcT[:, k, :], B[:, i * NCTX:(i + 1) * NCTX], ACT.Identity,
                                             bias=cols[:, 0, 0, 1, k:k + 1], scale=amp[:, 0, 0, 1, k:k + 1])
                elif kind == "zpool":
                    last = sc.activation(u_pool[:, args[0], :], B, ACT.Copy)
                elif kind == "latT":
                    t = args[0]
                    act_e.wait_ge(attn_w_in, 16 * 4)
                    if t < T:
                        for i in range(2):
                            sc.activation(qlatT[:, i, t * 128:(t + 1) * 128], B[:, i * 128:(i + 1) * 128], ACT.Copy,
                                          scale=qg[:, i:i + 1])
                    at = (t - T if t >= T else CT + t) * 128
                    sc.activation(kvT[:, at:at + 128], B[:, 256:384], ACT.Copy, scale=kvg[:, 0:1])
                    last = sc.activation(kT[64:128, at:at + 128], B[0:64, 384:512], ACT.Copy)
                elif kind == "poolw":
                    last = sc.activation(catT[:, args[0], :], B, ACT.Copy, scale=pscale[:, args[0]:args[0] + 1])
                elif kind == "value":
                    last = sc.activation(values[:, args[0], :], B, ACT.Copy)
                elif kind == "row":
                    s, half = args
                    row = (g1_row if s == 2 else g2_row)[:, :].rearrange("p (n k) -> p k n", k=K8)
                    last = sc.activation(row[:, 4 * half:4 * half + 4, :], B.rearrange("p (k n) -> p k n", k=4), ACT.Copy)
                elif kind == "oT":
                    last = sc.activation(catT[:, 4 + args[0], :], B, ACT.Copy)
                elif kind in ("hT", "h1T"):
                    t, half = args
                    norm = int(kind == "hT")
                    if l:
                        act_e.wait_ge(cols_ready, 1)
                    for i in range(4):
                        k = 4 * half + i
                        last = sc.activation(hT[:, k, t * 128:(t + 1) * 128], B[:, i * 128:(i + 1) * 128],
                                             ACT.Identity, bias=cols[:, l, 3 * norm, 0, k:k + 1],
                                             scale=amp[:, l, norm, 0, k:k + 1])
                elif kind == "affT":
                    last = sc.activation(affT[0:EXPERTS, :], B[0:EXPERTS, :], ACT.Copy)
                elif kind == "pwg":
                    c = args[0]
                    if c >= 2:
                        act_e.wait_ge(drained_v, drains("V", place(1, "pwa", c - 2)))
                    last = sc.activation(sig[:, c % 2, :], B, ACT.Sigmoid, bias=g_bias[:, c:c + 1])
                last.then_inc(drained_s, 1)

            act_e.wait_ge(cond_in, 32)
            for v in range(2):
                sc.activation(cond[:, :, 16 * v:16 * v + 16], cond_raw[:, v, :].unsqueeze(2).to_broadcast([128, K8, 16]),
                              ACT.Silu).then_inc(cond_ready, 1)
            act_e.wait_ge(x_arrived, 16)
            for t in range(T):
                square(t, x[:, t, :], xn[:, t, :])
            act_e.wait_ge(ctx_arrived, 16)
            for t in range(CT):
                square(NORM["ctx"] + t, ctx_x[:, t, :], hT_flat[:, t * D:(t + 1) * D])
            for n in range(len(L0)):
                drain(n)

            S = [PS[:, 2 * b:2 * b + 2, :].rearrange("p a b -> p (a b)") for b in range(2)]

            def nopes(h):
                act_e.wait_ge(projected, h + 1)
                if not isinstance(h, int) or h > 0:
                    act_e.wait_ge(scores_ready, 4 * h)
                sc.activation(qT[0:NOPE, :], PS[0:NOPE, 7, :], ACT.Copy).then_inc(q_nope_done, 1)
                sc.activation(kT[0:NOPE, :], S[0][0:NOPE, 0:768], ACT.Copy).then_inc(k_nope_done, 1)

            def output(h, qt, at):
                act_e.wait_ge(o_ready, 4 * h + qt + 1)
                act_e.wait_ge(recip_done, 4 * h + qt + 1)
                sc.activation(o_heads[:, qt, bass.ds(at, VD)], PS[:, 6 + qt % 2, 0:VD], ACT.Copy,
                              scale=recips[:, qt:qt + 1]).then_inc(o_done, 1)

            def head(h, first, more):
                for qt in range(T):
                    act_e.wait_ge(bias_ready, 4 * h + qt + 1)
                    if not (first and qt < 2):
                        act_e.wait_ge(pT_ready, 4 * h + qt - 1)
                    sc.activation(exps[:, qt % 2, :], S[qt % 2][:, 0:768], ACT.Exp, bias=biases[:, qt:qt + 1],
                                  scale=SCALE, accum_out=sums[:, qt:qt + 1]).then_inc(exp_done, 1)
                    if not (first and qt < 2):
                        o = (h, qt - 2) if qt > 1 else (h - 1, qt + 2)
                        output(*o, o[0] * VD)
                if more:
                    nopes(h + 1)

            nopes(0)
            head(0, True, True)
            with act_e.Fori(1, HEADS - 1, 1) as h:
                head(h, False, True)
            head(HEADS - 1, False, False)
            output(HEADS - 1, 2, (HEADS - 1) * VD)
            output(HEADS - 1, 3, (HEADS - 1) * VD)
            for n in range(len(L0), IN_L1):
                drain(n)

            def gathered(l, g):
                act_e.wait_ge(xs_filled, g * 2 + 2)
                for i in range(4):
                    k = 4 + i
                    last = sc.activation(xsT[:, k, :], PS[:, 1, i * 128:(i + 1) * 128], ACT.Identity,
                                         bias=cols[:, l, 3, 0, k:k + 1], scale=amp[:, l, 1, 0, k:k + 1])
                last.then_inc(xs_drained_s, 1)

            def pair(l, j, ada, more):
                g = j + PAIRS * l
                act_e.wait_ge(moe_used, g * 12 + 4)
                for half in range(2):
                    sc.activation(silu_g[:, half, :], PS[:, half, :], ACT.Silu).then_inc(silu_done, 1)
                if ada:
                    for half in range(2):
                        act_e.wait_ge(rows_filled, j * 2 + half + 1)
                        sc.activation(ada_rows[:, half, :], PS[:, 4 + half, :], ACT.Copy).then_inc(rows_drained, 1)
                act_e.wait_ge(aT_filled, g * 2 + 2)
                sc.activation(actT[:, 4:8, :].rearrange("p a b -> p (a b)"), PS[:, 7, :], ACT.Copy)\
                  .then_inc(aT_drained_s, 1)
                if more:
                    gathered(l, g + 1)

            def mixture(l):
                gathered(l, PAIRS * l)
                if l == 0:
                    with act_e.Fori(0, 6, 1) as j:
                        pair(0, j, True, True)
                    pair(0, 6, False, True)
                else:
                    with act_e.Fori(0, 7, 1) as j:
                        pair(1, j, False, True)
                pair(l, 7, False, False)

            mixture(0)
            for t in range(T):
                act_e.wait_ge(scat_added, 8 * PAIRS - 8 + 2 * t + 2)
                square(NORM[("n1", 1)] + t, x[:, t, :], xn[:, t, :])
            act_e.dma_start(bias_row, b_pw2[0, :].unsqueeze(0).to_broadcast([128, D])).then_inc(bias_in, 16)
            for n in range(IN_L1, len(ITEMS)):
                drain(n)
            act_e.wait_ge(x_updated, 16)
            act_e.dma_start(g1_row[:, :], final_g.unsqueeze(0).to_broadcast([128, D])).then_inc(final_in, 16)
            mixture(1)
            for t in range(T):
                act_e.wait_ge(scat_added, 16 * PAIRS - 8 + 2 * t + 2)
                square(NORM["final"] + t, x[:, t, :], xn[:, t, :])

        @block.vector
        def _(dve):
            v = nc.vector
            chain = Chain(dve, v_chain)

            def normalise(m, dst, src):
                dve.wait_ge(rstd_ready, m + 1)
                v.tensor_scalar(dst, src, rstd[:, m:m + 1], None, ALU.mult).then_inc(xn_ready, 1)

            def amplitude(l, norm, samples=1):
                for i in range(samples):
                    last = v.scalar_tensor_tensor(amp[:, l, norm, i, :], cols[:, l, 3 * norm + 1, i, :], 1.0,
                                                  ng[:, l, norm, :], ALU.add, ALU.mult)
                return last

            def section(l, s, bank_ap):
                return v.tensor_tensor(cols[:, l, s, :, :], bank_ap.rearrange("p (k v) -> p v k", v=2),
                                       ada_bias[:, l, s, :].unsqueeze(1).to_broadcast([128, 2, K8]), ALU.add)

            def make_diag(l, s):
                v.tensor_tensor(diag1 if l else diag0, ident.unsqueeze(1).to_broadcast([128, K8, 128]),
                                cols[:, l, s, 0, :].unsqueeze(2).to_broadcast([128, K8, 128]), ALU.mult)\
                 .then_inc(diag_ready, 1)

            def residual(l, t, half, B):
                tmp = ada_rows[:, half, :]
                v.tensor_tensor(tmp, B, g1_row[:, half * N:(half + 1) * N], ALU.mult).then_inc(drained_v, 1)
                dve.wait_ge(drained_v, drains("V", place(l, "pw2" if l else "mix", t, half)))
                if l:
                    dve.wait_ge(bias_added, t + 1)
                v.tensor_tensor(x[:, t, half * N:(half + 1) * N], x[:, t, half * N:(half + 1) * N], tmp, ALU.add)\
                 .then_inc(x_updated, 1)

            def choose(l):
                dve.wait_ge(drained_s, drains("S", place(l, "affT")))
                src = affT[0:EXPERTS, :]
                for r in range(CAP // 8):
                    chain(v.max(top8[0:EXPERTS, :], src))
                    chain(v.match_replace(left[0:EXPERTS, :], top8[0:EXPERTS, :], src, -1.0))
                    src = left[0:EXPERTS, :]
                mask = affT[0:EXPERTS, :]
                chain(v.tensor_scalar(mask, src, 0.0, None, ALU.is_lt))
                chain(v.tensor_tensor_scan(running[0:EXPERTS, :], mask, mask, 0.0, ALU.add, ALU.max))
                chain(v.tensor_tensor(running[0:EXPERTS, :], running[0:EXPERTS, :], mask, ALU.mult))
                v.tensor_scalar(left[0:EXPERTS, :], running[0:EXPERTS, :], -1.0, None, ALU.add)\
                 .then_inc(slots_ready, 1)

            def drain(n):
                l = int(n >= IN_L1)
                kind, args, engine = ITEMS[n]
                B = PS[:, n % NB, :]
                if kind == "affT":
                    choose(l)
                    return
                if engine != "V":
                    return
                dve.wait_ge(filled, n + 1)
                if n:
                    dve.wait_ge(drained_v, drains("V", n - 1))
                if kind == "params":
                    v.tensor_copy(dwT[:, :, :].rearrange("p a b -> p (a b)"), B[:, 0:K8 * CONVW])
                    last = v.tensor_copy(vecT[:, :], B[:, 256:256 + VEC_ROWS])
                elif kind == "sel":
                    s = args[0]
                    if s == 0:
                        dve.wait_ge(small_in, 16 * 8)
                    if s in (1, 4):
                        chain(section(0, s, B[:, 0:16]))
                        amplitude(0, s // 3, 2).then_inc(drained_v, 1)
                    else:
                        section(0, s, B[:, 0:16]).then_inc(drained_v, 1)
                    dve.wait_ge(drained_v, drains("V", n))
                    if s == 2:
                        make_diag(0, 2)
                    return
                elif kind in ("xT", "cT"):
                    i = int(kind == "cT")
                    for j in range(1 + i):
                        k = 2 * args[0] + j if i else args[0]
                        dst, src = (hcT[:, k, :], B[:, j * NCTX:(j + 1) * NCTX]) if i else (hT[:, k, :], B)
                        last = v.tensor_scalar(dst, src, amp[:, 0, 0, i, k:k + 1], cols[:, 0, 0, i, k:k + 1],
                                               ALU.mult, ALU.add)
                elif kind == "zlat":
                    t = args[0]
                    seq = LAT_ORDER.index(t)
                    row = lat[:, seq % 2, :]
                    dve.wait_ge(lat_rstd_ready, seq + 1)
                    if seq >= 2:
                        dve.wait_ge(filled, place(0, "latT", LAT_ORDER[seq - 2]) + 1)
                    off = 0
                    if t < T:
                        v.tensor_scalar(row[:, 0:QL], B[:, 0:QL], lat_rstd[:, t, 0:1], None, ALU.mult)
                        off = QL
                    v.tensor_scalar(row[:, QL:QL + KVL], B[:, off:off + KVL], lat_rstd[:, t, 1:2], None, ALU.mult)
                    kr = B[:, off + KVL:off + KVL + ROPE]
                    if t < T:
                        if t == 0:
                            dve.wait_ge(attn_w_in, 16 * 4)
                        v.tensor_tensor(kr_tmp[:, 0, :], kr, rope_k[:, 0, t, :], ALU.mult)
                        kr4 = kr.rearrange("p (a h f) -> p a h f", a=2, h=2)
                        to4 = kr_tmp[:, 1, :].rearrange("p (a h f) -> p a h f", a=2, h=2)
                        sin4 = rope_k[:, 1, t, :].rearrange("p (a h f) -> p a h f", a=2, h=2)
                        for h in range(2):
                            last = v.tensor_tensor(to4[:, :, h, :], kr4[:, :, 1 - h, :], sin4[:, :, h, :], ALU.mult)
                        chain(last)
                        for h in range(2):
                            last = v.tensor_tensor(row[:, QL + KVL + h * ROPE:QL + KVL + (h + 1) * ROPE],
                                                   kr_tmp[:, 0, :], kr_tmp[:, 1, :], ALU.add)
                    else:
                        for h in range(2):
                            last = v.tensor_copy(row[:, QL + KVL + h * ROPE:QL + KVL + (h + 1) * ROPE], kr)
                elif kind == "band":
                    if args[0] >= 2:
                        dve.wait_ge(filled, place(0, "poolw", args[0] - 2) + 1)
                    last = v.tensor_copy(diffT[:, args[0] % 2, :], B)
                elif kind == "value":
                    last = v.tensor_copy(values[:, args[0], :], B)
                elif kind == "row":
                    s, half = args
                    row = (g1_row if s == 2 else g2_row)[:, :].rearrange("p (n k) -> p k n", k=K8)
                    v.tensor_copy(row[:, 4 * half:4 * half + 4, :], B.rearrange("p (k n) -> p k n", k=4))\
                     .then_inc(drained_v, 1)
                    if s == 2:
                        make_diag(l, 5)
                    return
                elif kind == "oT":
                    last = v.tensor_copy(catT[:, 4 + args[0], :], B)
                elif kind in ("mix", "pw2"):
                    t, half = args
                    residual(l, t, half, B)
                    if half:
                        normalise(NORM[("n2", l)] + t, xn[:, t, :], x[:, t, :])
                    return
                elif kind in ("hT", "h1T"):
                    t, half = args
                    norm = int(kind == "hT")
                    for i in range(4):
                        k = 4 * half + i
                        last = v.tensor_scalar(hT[:, k, t * 128:(t + 1) * 128], B[:, i * 128:(i + 1) * 128],
                                               amp[:, l, norm, 0, k:k + 1], cols[:, l, 3 * norm, 0, k:k + 1],
                                               ALU.mult, ALU.add)
                elif kind == "logit":
                    t = args[0]
                    chain(v.reduce_max(aff_cols[:, 0, t:t + 1], B[:, 0:EXPERTS], AX.X))
                    v.tensor_scalar(shifted[:, t, :], B[:, 0:EXPERTS], aff_cols[:, 0, t:t + 1], None, ALU.subtract)\
                     .then_inc(drained_v, 1)
                    dve.wait_ge(aff_exp_done, T * l + t + 1)
                    chain(v.reciprocal(aff_cols[:, 2, t:t + 1], aff_cols[:, 1, t:t + 1]))
                    v.tensor_scalar(aff[:, t, :], shifted[:, t, :], aff_cols[:, 2, t:t + 1], None, ALU.mult)\
                     .then_inc(aff_ready, 1)
                    return
                elif kind == "slotT":
                    last = v.tensor_copy(slot_of.rearrange("p a b -> p (a b)"), B[:, 0:T * EXPERTS])
                elif kind == "pwa":
                    c = args[0]
                    dve.wait_ge(drained_s, drains("S", place(1, "pwg", c)))
                    if c == 0:
                        dve.wait_ge(halo_set, 4)
                    if c >= 2:
                        dve.wait_ge(filled, place(1, "taps", c - 2) + 1)
                    v.scalar_tensor_tensor(u_pad[:, c % 2, HALO:HALO + N], B, a_bias[:, c:c + 1], sig[:, c % 2, :],
                                           ALU.add, ALU.mult).then_inc(drained_v, 1)
                    dve.wait_ge(drained_v, drains("V", n))
                    chain(v.tensor_scalar(conv[:, c, :], u_pad[:, c % 2, 0:N], dwT[:, c, 0:1], dw_bias[:, c:c + 1],
                                          ALU.mult, ALU.add))
                    for j in range(1, CONVW - PE_TAPS):
                        chain(v.scalar_tensor_tensor(conv[:, c, :], u_pad[:, c % 2, j:j + N], dwT[:, c, j:j + 1],
                                                     conv[:, c, :], ALU.mult, ALU.add))
                    return
                elif kind == "taps":
                    c = args[0]
                    last = v.tensor_tensor(conv[:, c, :], conv[:, c, :], B, ALU.add)
                elif kind == "mean":
                    v.tensor_copy(ln_mean, PS[:, 6, :]).then_inc(drained_v, 1)
                    dve.wait_ge(drained_v, drains("V", n))
                    for c in range(K8):
                        v.tensor_tensor(conv[:, c, :], conv[:, c, :], ln_mean, ALU.subtract).then_inc(centred, 1)
                    return
                elif kind == "var":
                    v.tensor_scalar(ln_mean, PS[:, 7, :], EPS, None, ALU.add).then_inc(drained_v, 1)
                    dve.wait_ge(drained_v, drains("V", n))
                    dve.wait_ge(ln_rstd_ready, 1)
                    for c in range(K8):
                        v.tensor_tensor(conv[:, c, :], conv[:, c, :], ln_rstd, ALU.mult).then_inc(scaled, 1)
                    return
                last.then_inc(drained_v, 1)

            v.memset(ones[:, :], 1.0).then_inc(ones_set, 1)
            v.memset(one_dth[:, :], 1.0 / D).then_inc(ones_set, 1)
            v.memset(minus_half[:, :], -0.5).then_inc(ones_set, 1)
            for t in range(T):
                normalise(t, xn[:, t, :], x[:, t, :])
            for t in range(CT):
                normalise(NORM["ctx"] + t, ctx_x[:, t, :], ctx_x[:, t, :])
            for n in range(len(L0)):
                drain(n)

            S = [PS[:, 2 * b:2 * b + 2, :].rearrange("p a b -> p (a b)") for b in range(2)]
            PT = PS[:, 4:6, :].rearrange("p a b -> p (a b)")

            def rotate(h):
                dve.wait_ge(projected, h + 1)
                if not isinstance(h, int) or h > 0:
                    dve.wait_ge(scores_ready, 4 * h)
                v.tensor_tensor(qT[64:128, :], PS[64:128, 7, :], rope_q[64:128, :], ALU.mult).then_inc(q_rope_done, 1)

            def turned(h, qt):
                dve.wait_ge(pT_ready, 4 * h + qt + 1)
                if not (isinstance(h, int) and h == 0 and qt < 2):
                    dve.wait_ge(o_ready, 4 * h + qt - 1)
                v.tensor_copy(pT[:, qt % 2, :], PT[:, 0:768]).then_inc(pT_drained, 1)
                v.reciprocal(recips[:, qt:qt + 1], sums[:, qt:qt + 1]).then_inc(recip_done, 1)

            def head(h, first, more):
                for qt in range(T):
                    dve.wait_ge(scores_ready, 4 * h + qt + 1)
                    v.reduce_max(maxima[:, qt:qt + 1], S[qt % 2][:, 0:768], AX.X).then_inc(max_step, 1)
                    dve.wait_ge(max_step, 4 * h + qt + 1)
                    v.tensor_scalar(biases[:, qt:qt + 1], maxima[:, qt:qt + 1], -SCALE, None, ALU.mult)\
                     .then_inc(bias_ready, 1)
                    if not (first and qt == 0):
                        turned(*((h, qt - 1) if qt else (h - 1, 3)))
                if more:
                    rotate(h + 1)

            rotate(0)
            head(0, True, True)
            with dve.Fori(1, HEADS - 1, 1) as h:
                head(h, False, True)
            head(HEADS - 1, False, False)
            turned(HEADS - 1, 3)
            for n in range(len(L0), IN_L1):
                drain(n)

            def choose_pair(g, j):
                for dst, scaled_by in ((onehot, False), (gated, True)):
                    for t in range(T):
                        for e in range(2):
                            s = slot_of[:, t, bass.ds(j * 2 + e, 1)]
                            if scaled_by:
                                last = v.tensor_scalar(dst[:, t, 64 * e:64 * e + 64], iota, s,
                                                       aff[:, t, bass.ds(j * 2 + e, 1)], ALU.is_equal, ALU.mult)
                            else:
                                last = v.tensor_scalar(dst[:, t, 64 * e:64 * e + 64], iota, s, None, ALU.is_equal)
                last.then_inc(onehot_built, 1)

            def gathered(l, g):
                dve.wait_ge(xs_filled, g * 2 + 1)
                for k in range(4):
                    last = v.tensor_scalar(xsT[:, k, :], PS[:, 0, k * 128:(k + 1) * 128], amp[:, l, 1, 0, k:k + 1],
                                           cols[:, l, 3, 0, k:k + 1], ALU.mult, ALU.add)
                last.then_inc(xs_drained_v, 1)

            def gated_turned(g):
                dve.wait_ge(gT_filled, g + 1)
                v.tensor_copy(gatedT, PS[:, 2, :]).then_inc(gT_drained, 1)

            def pair(l, j, ada, more):
                g = j + PAIRS * l
                if more:
                    dve.wait_ge(xs_filled, g * 2 + 2)
                    choose_pair(g + 1, j + 1)
                dve.wait_ge(moe_used, g * 12 + 8)
                for half in range(2):
                    dve.wait_ge(silu_done, g * 2 + half + 1)
                    v.tensor_tensor(act[:, half * N:(half + 1) * N], silu_g[:, half, :], PS[:, 2 + half, :], ALU.mult)\
                     .then_inc(act_done, 1)
                dve.wait_ge(aT_filled, g * 2 + 1)
                v.tensor_copy(actT[:, 0:4, :].rearrange("p a b -> p (a b)"), PS[:, 6, :]).then_inc(aT_drained_v, 1)
                if ada:
                    dve.wait_ge(sel_filled, j + 1)
                    v.tensor_tensor(cols[:, 1, bass.ds(j, 1), :, :].rearrange("p s v k -> p (s v) k"),
                                    PS[:, 4, 0:16].rearrange("p (k v) -> p v k", v=2),
                                    ada_bias[:, 1, bass.ds(j, 1), :].to_broadcast([128, 2, K8]), ALU.add)\
                     .then_inc(sel_drained, 1)
                dve.wait_ge(moe_used, g * 12 + 12)
                for half in range(2):
                    v.tensor_tensor(y_rows[:, half * N:(half + 1) * N], PS[:, 4 + half, :],
                                    g2_row[:, half * N:(half + 1) * N], ALU.mult).then_inc(y_done, 1)
                if more:
                    gathered(l, g + 1)
                for i in range(2 * T):
                    dve.wait_ge(scat_filled, g * 8 + i + 1)
                    part = x[:, i // 2, (i % 2) * N:(i % 2 + 1) * N]
                    v.tensor_tensor(part, part, PS[:, 6 + i % 2, :], ALU.add).then_inc(scat_added, 1)
                if more:
                    gated_turned(g + 1)

            def mixture(l):
                choose_pair(PAIRS * l, 0)
                gathered(l, PAIRS * l)
                gated_turned(PAIRS * l)
                if l == 0:
                    with dve.Fori(0, 6, 1) as j:
                        pair(0, j, True, True)
                    pair(0, 6, False, True)
                else:
                    with dve.Fori(0, 7, 1) as j:
                        pair(1, j, False, True)
                pair(l, 7, False, False)

            dve.wait_ge(drained_v, drains("V", IN_L1 - 1))
            mixture(0)
            dve.wait_ge(sel_drained, 6)
            amplitude(1, 0)
            amplitude(1, 1).then_inc(cols_ready, 1)
            dve.wait_ge(cols_ready, 1)
            make_diag(1, 2)
            for t in range(T):
                normalise(NORM[("n1", 1)] + t, xn[:, t, :], x[:, t, :])
            for n in range(IN_L1, len(ITEMS)):
                drain(n)
            dve.wait_ge(drained_v, drains("V", len(ITEMS) - 1))
            mixture(1)
            dve.wait_ge(final_in, 16)
            for t in range(T):
                m = NORM["final"] + t
                dve.wait_ge(rstd_ready, m + 1)
                v.scalar_tensor_tensor(xn[:, t, :], x[:, t, :], rstd[:, m:m + 1], g1_row[:, :], ALU.mult, ALU.mult)\
                 .then_inc(out_ready, 1)

        @block.gpsimd
        def _(pool):
            p = nc.gpsimd
            chain = Chain(pool, p_chain)

            def reciprocal_root(m):
                pool.wait_ge(ssq_ready, m + 1)
                chain(p.tensor_scalar(ms[:, m:m + 1], ssq[:, m:m + 1], 1.0 / D, EPS, ALU.mult, ALU.add))
                p.tensor_tensor(rstd[:, m:m + 1], ms[:, m:m + 1], minus_half[:, :], ALU.pow).then_inc(rstd_ready, 1)

            pool.wait_ge(ones_set, 3)
            for m in range(6):
                reciprocal_root(m)
            for seq, t in enumerate(LAT_ORDER):
                pool.wait_ge(lat_ssq_ready, seq + 1)
                a = 0 if t < T else 1
                if t < T:
                    p.tensor_scalar(lat_ms[:, t, 0:1], lat_ssq[:, t, 0:1], 1.0 / QL, EPS, ALU.mult, ALU.add)
                chain(p.tensor_scalar(lat_ms[:, t, 1:2], lat_ssq[:, t, 1:2], 1.0 / KVL, EPS, ALU.mult, ALU.add))
                p.tensor_tensor(lat_rstd[:, t, a:2], lat_ms[:, t, a:2], minus_half[:, :].to_broadcast([128, 2 - a]),
                                ALU.pow).then_inc(lat_rstd_ready, 1)

            pool.wait_ge(attn_w_in, 16 * 4)

            def stage(h):
                if not isinstance(h, int) or h > 0:
                    pool.wait_ge(projected, h)
                p.tensor_copy(wq_stage[:, :, 0:QK], uq[:, :, bass.ds(h * QK, QK)])
                for half in range(2):
                    for axis in range(2):
                        to = QK + axis * 16 + half * 8
                        fr = NOPE + axis * 16 + (1 - half) * 8
                        p.tensor_copy(wq_stage[:, :, to:to + 8], uq[:, :, bass.ds(h * QK + fr, 8)])
                p.tensor_copy(wk_stage, ukv[:, bass.ds(h * (NOPE + VD), NOPE)]).then_inc(staged, 1)

            stage(0)
            with pool.Fori(1, HEADS, 1) as h:
                stage(h)
            for t in range(T):
                reciprocal_root(NORM[("n2", 0)] + t)
            for t in range(T):
                reciprocal_root(NORM[("n1", 1)] + t)
            for b in range(2):
                for a in (0, HALO + N):
                    p.memset(u_pad[:, b, a:a + HALO], 0.0).then_inc(halo_set, 1)
            pool.wait_ge(filled, place(1, "row", 5, 1) + 1)
            for c in range(K8):
                if c >= 2:
                    pool.wait_ge(filled, place(1, "taps", c - 2) + 1)
                for i in range(PE_TAPS):
                    j = CONVW - PE_TAPS + i
                    last = p.tensor_scalar(tap_diag[:, c % 2, i, :], ident, dwT[:, c, j:j + 1], None, ALU.mult)
                last.then_inc(tap_diag_ready, 1)
                if c == 1:
                    pool.wait_ge(bias_in, 16)
                    pool.wait_ge(drained_s, drains("S", place(1, "row", 2, 0)))
                    pool.wait_ge(drained_v, drains("V", place(1, "row", 2, 1)))
                    chain(p.tensor_tensor(bias_row, bias_row, g1_row[:, :], ALU.mult))
                    pool.wait_ge(xn_ready, NORM[("n1", 1)] + T)
                    for t in range(T):
                        p.tensor_tensor(x[:, t, :], x[:, t, :], bias_row, ALU.add).then_inc(bias_added, 1)
            pool.wait_ge(drained_v, drains("V", place(1, "var")))
            p.tensor_tensor(ln_rstd, ln_mean, minus_half[:, :].to_broadcast([128, N]), ALU.pow).then_inc(ln_rstd_ready, 1)
            for t in range(T):
                reciprocal_root(NORM[("n2", 1)] + t)
            for t in range(T):
                reciprocal_root(NORM["final"] + t)


_INS = ["x", "c", "ctx", "c_ctx", "ada_w", "ada_b", "norm1_g", "norm2_g", "mix_w_in", "pool_w", "pool_scale",
        "q_norm_g", "kv_norm_g", "w_uq", "w_ukv", "mix_w_out", "conv_w_pw1", "conv_b_pw1", "conv_w_dw", "conv_b_dw",
        "conv_ln_g", "conv_ln_b", "conv_w_pw2", "conv_b_pw2", "router_w", "exp_wg", "exp_wu", "exp_wd", "final_g"]


def tables():
    import numpy as np
    small = np.zeros((128, 194), np.float32)
    small[:, 0:128] = np.eye(128, dtype=np.float32)
    small[:, 128:192] = np.arange(64, dtype=np.float32)
    small[0::32, 192] = 1.0
    small[16::32, 193] = 1.0
    tok = np.arange(N)
    inv = (1.0 / (10000.0 ** (np.arange(0, 16, 2, dtype=np.float32) / 16))).astype(np.float32)
    pos = np.stack([tok // 64, tok % 64], 1).astype(np.float32)
    ang = (pos[:, :, None] * inv).astype(np.float32)
    cos = np.repeat(np.cos(ang)[:, :, None, :], 2, axis=2).reshape(N, ROPE).astype(np.float32)
    sin = (np.repeat(np.sin(ang)[:, :, None, :], 2, axis=2)
           * np.array([-1.0, 1.0])[None, None, :, None]).reshape(N, ROPE).astype(np.float32)
    rope = np.zeros((128, N + 2 * T * ROPE), np.float32)
    rope[64:96, 0:N] = cos.T
    rope[96:128, 0:N] = sin.T
    rope[:, N:N + T * ROPE] = cos.reshape(T, 128, ROPE).transpose(1, 0, 2).reshape(128, T * ROPE)
    rope[:, N + T * ROPE:] = sin.reshape(T, 128, ROPE).transpose(1, 0, 2).reshape(128, T * ROPE)
    band = np.zeros((128, 4, 5, 128), np.float32)
    for g, w in enumerate((2, 4, 8, 16)):
        lo, hi = np.clip(tok - w // 2, 0, N), np.clip(tok - w // 2 + w, 0, N)
        inside = (tok[:, None] >= lo) & (tok[:, None] < hi)
        full = inside / (hi - lo).astype(np.float32) - np.eye(N)
        for b, (i, o) in enumerate(((0, 1), (1, 1), (2, 1), (0, 0), (3, 3))):
            band[:, g, b, :] = full[i * 128:(i + 1) * 128, o * 128:(o + 1) * 128]
    return {"small_tab": small, "rope_tab": rope, "band_tab": band.reshape(128, 20 * 128)}


def kernel(**inputs):
    import numpy as _np
    import concourse.bacc as _bacc
    from concourse import mybir as _mybir
    from concourse.bass_utils import run_bass_kernel_spmd as _run

    nc = _bacc.Bacc("TRN2", target_bir_lowering=False, num_devices=1)
    given = {n: _np.ascontiguousarray(inputs[n]) for n in _INS}
    given.update(tables())
    arrays, args = {}, []
    for name, a in given.items():
        arrays[f"in_{name}_dram"] = a
        args.append(nc.dram_tensor(f"in_{name}_dram", a.shape, _mybir.dt.from_np(a.dtype), kind="ExternalInput").ap())
    args.append(nc.dram_tensor("out_0_dram", (1, N, D), _mybir.dt.float32, kind="ExternalOutput").ap())
    build(nc, *args)
    r = _run(nc, [arrays], core_ids=[0])
    return r.results[0]["out_0_dram"]
```

```python
import concourse.bass as bass
from concourse import mybir
from contextlib import ExitStack

D = 1024
N = 512
NCTX = 256
T = N // 128
CT = NCTX // 128
KT = T + CT
K8 = D // 128
HEADS = 8
NOPE = 64
ROPE = 32
VD = 64
QK = NOPE + ROPE
QL = 256
KVL = 128
POOL = 512
LATE = HEADS - 1
LAT = QL + KVL + ROPE
MIX_IN = POOL + LAT
LROW = QL + KVL + 2 * ROPE
CONVW = 31
HALO = CONVW // 2
EXPERTS = 16
PAIRS = EXPERTS // 2
CAP = 2 * N // EXPERTS
SCALE = float(QK) ** -0.5
EPS = 1e-6
SLOTS = 6
SLOT_WORDS = 4096
NB = 6
VEC_ROWS = 5 * K8 + 4 + 2 + 1
PE_TAPS = 4
PE_TAPS_LAST = 14
UNITS = HEADS * T
LAT_ORDER = [4, 5, 0, 1, 2, 3]


def conditioning(s):
    return [("ada", (2 * s,), "S"), ("ada", (2 * s + 1,), "S"), ("sel", (s,), "V")]


def l0_items():
    o = [("params", (), "V")] + conditioning(0) + conditioning(1)
    o += [("cT", (k,), "VS"[k % 2]) for k in range(K8 // 2)]
    o += [("xT", (k,), "VS"[k % 2]) for k in range(K8)]
    o += [("zlat", (4,), "V"), ("zlat", (5,), "V"), ("zlat", (0,), "V"), ("latT", (4,), "S"),
          ("zpool", (0,), "S"), ("latT", (5,), "S"), ("zlat", (1,), "V"), ("latT", (0,), "S"),
          ("zpool", (1,), "S"), ("zlat", (2,), "V"), ("latT", (1,), "S"), ("zpool", (2,), "S"),
          ("zlat", (3,), "V"), ("latT", (2,), "S"), ("zpool", (3,), "S"), ("latT", (3,), "S")]
    o += [("band", (0,), "V"), ("band", (1,), "V"), ("poolw", (0,), "S"), ("poolw", (1,), "S"),
          ("band", (2,), "V"), ("band", (3,), "V"), ("poolw", (2,), "S"), ("poolw", (3,), "S")]
    o += [("value", (k,), "VS"[k % 2]) for k in range(KT)]
    for s in range(2, 5):
        o += conditioning(s)
    return o + [("row", (2, 0), "S"), ("row", (2, 1), "V")]


def product_and_route(kind):
    o = []
    for t in range(T):
        o += [(kind, (t, 0), "V")]
        if t:
            o += [("hT", (t - 1, 0), "V"), ("hT", (t - 1, 1), "S")]
        o += [(kind, (t, 1), "V")]
        if t:
            o += [("logit", (t - 1,), "V")]
    if kind == "mix":
        o += [("row", (5, 0), "S"), ("row", (5, 1), "S")]
    o += [("hT", (T - 1, 0), "V"), ("hT", (T - 1, 1), "S"), ("logit", (T - 1,), "V")]
    return o + [("affT", (), "S"), ("slotT", (), "V")]


def mix_items():
    return product_and_route("mix")


def conv_items():
    o = []
    for t in range(T):
        o += [("h1T", (t, 0), "V"), ("h1T", (t, 1), "S")]
    for c in range(K8):
        o += [("pwg", (c,), "S"), ("pwa", (c,), "V")]
        if c:
            o += [("taps", (c - 1,), "V")]
        if c == 2:
            o += [("shift", (), "V")]
    o += [("taps", (K8 - 1,), "V"), ("row", (2, 0), "S"), ("row", (2, 1), "V"), ("moments", (), "V"),
          ("row", (5, 0), "S"), ("row", (5, 1), "S")]
    return o + product_and_route("pw2")


L0, MIX, CONV = l0_items(), mix_items(), conv_items()
ITEMS = L0 + MIX + CONV
IN_L1 = len(L0) + len(MIX)
PLACES = {(n >= IN_L1, kind, args): n for n, (kind, args, _) in enumerate(ITEMS)}


def place(layer, kind, *args):
    return PLACES[(layer == 1, kind, args)]


def drains(engine, through):
    return sum(e == engine for _, _, e in ITEMS[:through + 1])


ORDER = ([("ada", b) for b in range(4)] + [("mixin", 0), ("mixin", 1), ("band", 0)] + [("ada", b) for b in range(4, 10)]
         + [("late", 0), ("late", 1), ("mixout", 0), ("mixout", 1)] + [("moe0", n) for n in range(12 * PAIRS)]
         + [("pw1", q) for q in range(4)] + [("pw2", 0), ("pw2", 1)] + [("moe1", n) for n in range(12 * PAIRS)])
GRANULE = {name: g for g, name in enumerate(ORDER)}
G_MIXIN, G_BAND, G_MIXOUT, G_PW1, G_PW2 = (GRANULE[(name, 0)] for name in ("mixin", "band", "mixout", "pw1", "pw2"))
G_MOE = [GRANULE[("moe0", 0)], GRANULE[("moe1", 0)]]
MOE_GRANULES = 12 * PAIRS
G_LATE = GRANULE[("late", 0)]
TWO_DMAS = {G_BAND} | {G_PW1 + q for q in range(4)}


def arrivals(g):
    return 16 * sum(LATE if ORDER[n][0] == "late" else 1 + (n in TWO_DMAS) for n in range(g % SLOTS, g + 1, SLOTS))


def last_use(g):
    name, i = ORDER[g]
    if name == "ada":
        return place(0, "ada", i)
    if name == "pw1":
        return place(1, "pwa", 2 * i + 1)
    return {"mixin": place(0, "zpool", T - 1), "band": place(0, "poolw", 3), "mixout": place(0, "mix", T - 1, 1),
            "pw2": place(1, "pw2", T - 1, 1)}[name]


def pe_taps(c):
    return PE_TAPS_LAST if c == K8 - 1 else PE_TAPS


def dve_steps(parity, c):
    return sum((CONVW - pe_taps(i) + 1 - parity) // 2 for i in range(c))


class Chain:

    def __init__(self, eng, sem):
        self.eng, self.sem, self.n = eng, sem, 0

    def __call__(self, ins):
        self.n += 1
        ins.then_inc(self.sem, 1)
        self.eng.wait_ge(self.sem, self.n)


def build(nc, x_in, c_in, ctx_in, cctx_in, ada_w, ada_b, norm1_g, norm2_g, mix_w_in, pool_w, pool_scale,
          q_norm_g, kv_norm_g, w_uq, w_ukv, mix_w_out, pw1, b_pw1, w_dw, b_dw, ln_g, ln_b, pw2, b_pw2,
          router_w, exp_wg, exp_wu, exp_wd, final_g, small_tab, rope_tab, band_tab, out):
    fp32 = mybir.dt.float32
    ALU = mybir.AluOpType
    ACT = mybir.ActivationFunctionType
    AX = mybir.AxisListType
    stack = ExitStack()
    with stack:
        def sb(name, shape):
            return stack.enter_context(nc.sbuf_tensor(name, shape, fp32))

        def sem(name):
            return stack.enter_context(nc.semaphore(name))

        ring = sb("ring", [128, SLOTS, SLOT_WORDS])
        x = sb("x", [128, T, D])
        xn = sb("xn", [128, T, D])
        hT = sb("hT", [128, K8, N])
        consts = sb("consts", [128, 128 + 64 + 2])
        ident, iota, pick = consts[:, 0:128], consts[:, 128:192], consts[:, 192:194]
        ones = sb("ones", [128, 128])
        one_dth = sb("one_dth", [128, 128])
        minus_half = sb("minus_half", [128, 1])
        cond_raw = sb("cond_raw", [128, 2, K8])
        cond = sb("cond", [128, K8, 32])
        ada_bias = sb("ada_bias", [128, 2, 6, K8])
        ng = sb("ng", [128, 2, 2, K8])
        cols = sb("cols", [128, 2, 6, 2, K8])
        amp = sb("amp", [128, 2, 2, 2, K8])
        router = sb("router", [128, 2, K8, EXPERTS])
        g1_row = sb("g1_row", [128, D])
        g2_row = sb("g2_row", [128, D])
        dwT = sb("dwT", [128, K8, CONVW])
        vecT = sb("vecT", [128, VEC_ROWS])
        a_bias, g_bias, dw_bias, lng, lnb = (vecT[:, i * K8:(i + 1) * K8] for i in range(5))
        pscale, qg, kvg = vecT[:, 40:44], vecT[:, 44:46], vecT[:, 46:47]
        ssq = sb("ssq", [128, 22])
        ms = sb("ms", [128, 22])
        rstd = sb("rstd", [128, 22])
        lat_ssq = sb("lat_ssq", [128, KT, 2])
        lat_ms = sb("lat_ms", [128, KT, 2])
        lat_rstd = sb("lat_rstd", [128, KT, 2])
        ada_rows = sb("ada_rows", [128, 2, N])
        ARENA = 11450
        arena = sb("arena", [128, ARENA])

        def carver(at):
            here = [at]

            def cut(*shape):
                words = 1
                for s in shape:
                    words *= s
                v = arena[:, here[0]:here[0] + words]
                here[0] += words
                assert here[0] <= ARENA, here[0]
                if len(shape) == 2:
                    v = v.rearrange("p (a b) -> p a b", a=shape[0])
                if len(shape) == 3:
                    v = v.rearrange("p (a b c) -> p a b c", a=shape[0], b=shape[1])
                return v
            return cut

        cut = carver(0)
        qT = cut(N)
        kT = cut(KT * 128)
        kvT = cut(KT * 128)
        hcT = arena[:, 0:K8 * NCTX].rearrange("p (k n) -> p k n", k=K8)
        uq = cut(2, HEADS * QK)
        ukv = cut(HEADS * (NOPE + VD))
        wq_stage = cut(2, 128)
        qlatT = cut(2, N)
        rope_q = cut(N)
        rope_k = cut(2, T, ROPE)
        head_cols = cut(4, T)
        maxima, biases, sums, recips = (head_cols[:, i, :] for i in range(4))
        kr_tmp = cut(2, ROPE)
        values = cut(KT, HEADS * VD)
        values_flat = values.rearrange("p a b -> p (a b)")
        ctx_x = values_flat[:, 0:CT * D].rearrange("p (a b) -> p a b", a=CT)
        dw_rows = values_flat[:, CT * D:CT * D + D]
        exps = cut(2, KT * 128)
        exps_flat = exps.rearrange("p a b -> p (a b)")
        vec_rows = exps_flat[:, 1280:1408]
        lat_junk = exps_flat[:, 1024:1280]
        lat_junk2 = exps_flat[:, 1408:1536]
        catT = hT
        hT_flat = hT[:, :, :].rearrange("p a b -> p (a b)")
        diffT = hT_flat[:, 4 * N:6 * N].rearrange("p (a b) -> p a b", a=2)
        xn_flat = xn[:, :, :].rearrange("p a b -> p (a b)")
        u_pool = xn_flat[:, 0:T * N].rearrange("p (a b) -> p a b", a=T)
        pT = xn_flat[:, 0:T * KT * 128].rearrange("p (a b) -> p a b", a=T)
        kT_odd = xn_flat[:, T * KT * 128:(T + 1) * KT * 128]
        wk_stage = xn_flat[:, (T + 1) * KT * 128:(T + 1) * KT * 128 + 2 * NOPE]
        assert T * N + 2 * LROW <= T * KT * 128
        keys = (kT, kT_odd)
        v_stage = [g2_row[:, i * KT * VD:(i + 1) * KT * VD].rearrange("p (a b) -> p a b", a=KT) for i in range(2)]
        lat = xn_flat[:, T * N:T * N + 2 * LROW].rearrange("p (a b) -> p a b", a=2)

        cut = carver(0)
        onehot = cut(T, 128)
        gated = cut(T, 128)
        gatedT = cut(N)
        xsT = cut(K8, 128)
        silu_g = cut(2, N)
        act = cut(D)
        actT = cut(K8, 128)
        y_rows = cut(D)

        ROUTE = ARENA - 224
        cut = carver(ROUTE)
        aff = cut(T, EXPERTS)
        shifted = cut(T, EXPERTS)
        slot_of = cut(T, EXPERTS)
        aff_cols = cut(3, T)
        top8 = cut(8)
        cut = carver(0)
        affT = cut(N)
        left = cut(N)
        running = cut(N)

        cut = carver(0)
        u_pad = cut(2, N + 2 * HALO)
        conv = cut(K8, N)
        tap_diag = cut(2, PE_TAPS, 128)
        sig = cut(2, N)
        ln_sq = cut(2, N)
        odd_taps = cut(2, N)
        shift = cut(N)
        ln_mean = cut(N)
        ln_rstd = cut(N)
        assert ln_rstd.offset + N <= arena[:, ROUTE:].offset

        bias_row = xn_flat[:, 2 * D:3 * D]
        last_diag = xn_flat[:, 0:PE_TAPS_LAST * 128].rearrange("p (a b) -> p a b", a=PE_TAPS_LAST)
        diags = {(0, 2): exps_flat[:, 0:D], (0, 5): exps_flat[:, 0:D], (1, 2): xn_flat[:, 3 * D:4 * D],
                 (1, 5): tap_diag.rearrange("p a b c -> p (a b c)")}
        assert exps_flat[:, 0:D].offset + D <= arena[:, ROUTE:].offset
        diags = {key: v.rearrange("p (k n) -> p k n", k=K8) for key, v in diags.items()}

        PS = stack.enter_context(nc.psum_tensor("PS", [128, 8, N], fp32))

        cond_in, x_arrived, ctx_arrived, consts_in, params_in, small_in, attn_w_in = map(
            sem, ("cond_in", "x_arrived", "ctx_arrived", "consts_in", "params_in", "small_in", "attn_w_in"))
        slot_in = [sem(f"slot_in{q}") for q in range(SLOTS)]
        moe_used = sem("moe_used")
        ones_set, cond_ready, filled, drained_v, drained_s = map(
            sem, ("ones_set", "cond_ready", "filled", "drained_v", "drained_s"))
        drained = {"V": drained_v, "S": drained_s}
        v_chain, s_chain, p_chain = sem("v_chain"), sem("s_chain"), sem("p_chain")
        ssq_ready, rstd_ready, xn_ready, x_updated = map(sem, ("ssq_ready", "rstd_ready", "xn_ready", "x_updated"))
        cols_ready, diag_ready = sem("cols_ready"), sem("diag_ready")
        late_filled, late_rows, late_selected, late_added = map(
            sem, ("late_filled", "late_rows", "late_selected", "late_added"))
        lat_ssq_ready, lat_rstd_ready = sem("lat_ssq_ready"), sem("lat_rstd_ready")
        q_staged, k_staged, v_staged, q_projected, k_projected, q_nope_done, k_nope_done, q_rope_done = map(
            sem, ("q_staged", "k_staged", "v_staged", "q_projected", "k_projected", "q_nope_done", "k_nope_done",
                  "q_rope_done"))
        max_step, scores_ready, bias_ready, exp_done, recip_done, exp_scaled, pT_ready, pT_drained, o_ready, o_done = map(
            sem, ("max_step", "scores_ready", "bias_ready", "exp_done", "recip_done", "exp_scaled", "pT_ready",
                  "pT_drained", "o_ready", "o_done"))
        odd_keys_set = sem("odd_keys_set")
        aff_exp_done, aff_ready, slots_ready = map(
            sem, ("aff_exp_done", "aff_ready", "slots_ready"))
        onehot_built, xs_filled, xs_drained_v, xs_drained_s, gT_filled, gT_drained = map(
            sem, ("onehot_built", "xs_filled", "xs_drained_v", "xs_drained_s", "gT_filled", "gT_drained"))
        silu_done, act_done, aT_filled, aT_drained_v, aT_drained_s, y_done, scat_filled, scat_added = map(
            sem, ("silu_done", "act_done", "aT_filled", "aT_drained_v", "aT_drained_s", "y_done", "scat_filled",
                  "scat_added"))
        even_step, odd_step = sem("even_step"), sem("odd_step")
        halo_set, tap_diag_ready, conv_done, centred, sq_ready, moments_added = map(
            sem, ("halo_set", "tap_diag_ready", "conv_done", "centred", "sq_ready", "moments_added"))
        ln_root_done, scaled, swish_done, bias_in, bias_added = map(
            sem, ("ln_root_done", "scaled", "swish_done", "bias_in", "bias_added"))
        final_in, out_ready, out_done = sem("final_in"), sem("out_ready"), sem("out_done")

        block = stack.enter_context(nc.Block())

        NORM = {("n1", 0): 0, "ctx": 4, ("n2", 0): 6, ("n1", 1): 10, ("n2", 1): 14, "final": 18}

        def column(v):
            return v.rearrange("(p k) -> p k", k=K8)

        def slot(g):
            return ring[:, g % SLOTS, :]

        @block.sync
        def _(sp):
            sp.dma_start(cond_raw[:, 0, :], column(c_in[0, :])).then_inc(cond_in, 16)
            sp.dma_start(cond_raw[:, 1, :], column(cctx_in)).then_inc(cond_in, 16)
            sp.dma_start(consts[:, :], small_tab).then_inc(consts_in, 16)
            sp.dma_start(x[:, :, :], x_in[0, :, :].rearrange("(t p) d -> p t d", p=128)).then_inc(x_arrived, 16)
            sp.dma_start(ctx_x, ctx_in[0, :, :].rearrange("(t p) d -> p t d", p=128)).then_inc(ctx_arrived, 16)

            def slot_free(g):
                before = g - SLOTS
                if ORDER[before][0] == "moe0":
                    sp.wait_ge(moe_used, ORDER[before][1] + 1)
                elif ORDER[before][0] == "late":
                    sp.wait_ge(late_filled, 2 * LATE)
                else:
                    sp.wait_ge(filled, last_use(before) + 1)

            def load(g, parts):
                assert len(parts) == 1 + (g in TWO_DMAS)
                if g >= SLOTS:
                    slot_free(g)
                for dst, src in parts:
                    sp.dma_start(dst, src).then_inc(slot_in[g % SLOTS], 16)

            def load_ada(b):
                g = GRANULE[("ada", b)]
                load(g, [(slot(g).rearrange("p (k n) -> p k n", k=K8),
                          ada_w[0, :, b * N:(b + 1) * N].rearrange("(p k) n -> p k n", k=K8))])

            def late_slot(b):
                return slot(G_LATE + b).rearrange("p (k n) -> p k n", k=K8)

            sp.dma_start(dw_rows[0:CONVW, :], w_dw[0, :, :]).then_inc(params_in, 16)
            at = 0
            for v in (b_pw1[0, :], b_dw[0, :], ln_g[0, :], ln_b[0, :], pool_scale[0, :], q_norm_g[0, :], kv_norm_g[0, :]):
                n = v.shape[0] // 128
                sp.dma_start(vec_rows[at:at + n, :], v.rearrange("(c p) -> c p", p=128)).then_inc(params_in, 16)
                at += n
            assert at == VEC_ROWS
            for b in range(4):
                load_ada(b)
            for l in range(2):
                sp.dma_start(ada_bias[:, l, :, :], ada_b[l, :].rearrange("(s p k) -> p s k", s=6, k=K8))\
                  .then_inc(small_in, 16)
                sp.dma_start(ng[:, l, 0, :], column(norm1_g[l, :])).then_inc(small_in, 16)
                sp.dma_start(ng[:, l, 1, :], column(norm2_g[l, :])).then_inc(small_in, 16)
                sp.dma_start(router[:, l, :, :], router_w[l, :, :].rearrange("(p k) e -> p k e", k=K8))\
                  .then_inc(small_in, 16)
            for h in range(2):
                g = G_MIXIN + h
                load(g, [(slot(g)[:, 0:4 * MIX_IN].rearrange("p (k n) -> p k n", k=4),
                          mix_w_in[0, :, :].rearrange("(p h k) n -> p h k n", h=2, k=4)[:, h, :, :])])
            sp.dma_start(rope_q, rope_tab[:, 0:N]).then_inc(attn_w_in, 16)
            sp.dma_start(rope_k.rearrange("p a t r -> p (a t r)"), rope_tab[:, N:N + 2 * T * ROPE])\
              .then_inc(attn_w_in, 16)
            sp.dma_start(uq, w_uq[0, :, :].rearrange("(k p) n -> p k n", p=128)).then_inc(attn_w_in, 16)
            sp.dma_start(ukv, w_ukv[0, :, :]).then_inc(attn_w_in, 16)
            load(G_BAND, [(slot(G_BAND)[:, 0:20 * 128], band_tab),
                          (slot(G_BAND)[:, 20 * 128:24 * 128].rearrange("p (g n) -> p g n", g=4),
                           pool_w[0, :, :, :].rearrange("g p n -> p g n"))])
            for b in range(4, 10):
                load_ada(b)
            for b in range(2):
                slot_free(G_LATE + b)
                sp.dma_start(late_slot(b), ada_w[0, :, (10 + b) * N:(11 + b) * N].rearrange("(p k) n -> p k n", k=K8))\
                  .then_inc(slot_in[(G_LATE + b) % SLOTS], 16)
            for h in range(2):
                g = G_MIXOUT + h
                load(g, [(slot(g).rearrange("p (k n) -> p k n", k=4),
                          mix_w_out[0, h * N:(h + 1) * N, :].rearrange("(k p) n -> p k n", p=128))])

            def load_pair(l, j, quarters=range(12)):
                for q in quarters:
                    w = (exp_wg, exp_wu, exp_wd)[q // 4]
                    src = w[l, :, :, :].rearrange("(g e) (p k) n -> g p e (k n)", e=2, k=K8)
                    s = (G_MOE[l] + q) % SLOTS
                    if isinstance(j, int) and j == 0 and q < SLOTS:
                        slot_free(G_MOE[l] + q)
                    else:
                        sp.wait_ge(moe_used, j * 12 + (MOE_GRANULES * l + q - SLOTS + 1))
                    sp.dma_start(ring[:, s, :].rearrange("p (e n) -> p e n", e=2),
                                 src[j, :, :, 2 * D * (q % 4):2 * D * (q % 4 + 1)]).then_inc(slot_in[s], 16)

            load_pair(0, 0, range(2))
            with sp.Fori(0, LATE - 1, 1) as s:
                for b in range(2):
                    sp.wait_ge(late_filled, 2 * s + b + 1)
                    src = ada_w[1, :, :].rearrange("(p k) (s b n) -> s b p k n", k=K8, b=2, n=N)
                    sp.dma_start(late_slot(b), src[s, b, :, :, :]).then_inc(slot_in[(G_LATE + b) % SLOTS], 16)
            load_pair(0, 0, range(2, 12))
            with sp.Fori(1, PAIRS, 1) as j:
                load_pair(0, j)
            for q in range(4):
                g = G_PW1 + q
                dst = slot(g).rearrange("p (k h c) -> p k h c", k=K8, h=2)
                src = pw1[0, :, :].rearrange("(p k) (h q c) -> p k h q c", k=K8, h=2, q=4)
                load(g, [(dst[:, :, h, :], src[:, :, h, q, :]) for h in range(2)])
            for h in range(2):
                g = G_PW2 + h
                load(g, [(slot(g).rearrange("p (k n) -> p k n", k=4),
                          pw2[0, h * N:(h + 1) * N, :].rearrange("(k p) n -> p k n", p=128))])
            load_pair(1, 0)
            with sp.Fori(1, PAIRS, 1) as j:
                load_pair(1, j)
            for t in range(T):
                sp.wait_ge(out_ready, t + 1)
                sp.dma_start(out[0, t * 128:(t + 1) * 128, :], xn[:, t, :]).then_inc(out_done, 16)
            sp.wait_ge(out_done, 16 * T)

        @block.tensor
        def _(pe):
            def wait_granule(g):
                pe.wait_ge(slot_in[g % SLOTS], arrivals(g))

            def transpose(o, i, rows=128):
                return nc.tensor.transpose(o, i, ident[0:rows, 0:rows])

            def drained_through(n, engines="VS"):
                for e in engines:
                    if drains(e, n):
                        pe.wait_ge(drained[e], drains(e, n))

            def ada_block(w, bank):
                for k in range(K8):
                    r = 32 * (k % 4)
                    last = nc.tensor.matmul(PS[r:r + 32, bank, :], cond[:, k, :], w[:, k, :],
                                            start=k < 4, stop=k >= 4)
                return last

            def ada_select(bank):
                for h in range(2):
                    for k in range(K8):
                        last = nc.tensor.matmul(PS[64 * h:64 * h + 64, bank, 2 * k:2 * k + 2],
                                                ada_rows[:, h, k::K8], pick, start=True, stop=True)
                return last

            def moments(c):
                pe.wait_ge(centred, c + 1)
                nc.tensor.matmul(PS[:, 6, :], one_dth[:, :], conv[:, c, :], start=c == 0, stop=c == K8 - 1)
                pe.wait_ge(sq_ready, c + 1)
                last = nc.tensor.matmul(PS[:, 7, :], one_dth[:, :], ln_sq[:, c % 2, :], start=c == 0, stop=c == K8 - 1)
                if c < K8 - 1:
                    last.then_inc(moments_added, 1)
                return last

            def fill(n):
                l = n >= IN_L1
                kind, args, _ = ITEMS[n]
                bank = n % NB
                if n >= NB and n not in (len(L0), IN_L1):
                    e = ITEMS[n - NB][2]
                    pe.wait_ge(drained[e], drains(e, n - NB))
                B = PS[:, bank, :]
                if kind == "params":
                    pe.wait_ge(consts_in, 16)
                    pe.wait_ge(params_in, 16 * 8)
                    for c in range(K8):
                        transpose(B[:, c * CONVW:(c + 1) * CONVW], dw_rows[0:CONVW, c * 128:(c + 1) * 128], CONVW)
                    last = transpose(B[:, 256:256 + VEC_ROWS], vec_rows[0:VEC_ROWS, :], VEC_ROWS)
                elif kind == "ada":
                    g = GRANULE[(kind, args[0])]
                    pe.wait_ge(cond_ready, 2)
                    wait_granule(g)
                    w = slot(g).rearrange("p (k n) -> p k n", k=K8)
                    last = ada_block(w, bank)
                elif kind == "sel":
                    drained_through(n - 1, "S")
                    last = ada_select(bank)
                elif kind in ("xT", "cT"):
                    pe.wait_ge(xn_ready, 6)
                    if kind == "xT":
                        for t in range(T):
                            last = transpose(B[:, t * 128:(t + 1) * 128], xn[:, t, args[0]::K8])
                    else:
                        for i in range(4):
                            last = transpose(B[:, i * 128:(i + 1) * 128],
                                             ctx_x[:, i % 2, 2 * args[0] + i // 2::K8])
                elif kind in ("zlat", "zpool"):
                    drained_through(place(0, "xT", K8 - 1))
                    wait_granule(G_MIXIN)
                    wait_granule(G_MIXIN + 1)
                    t = args[0]
                    a, b = (0, POOL) if kind == "zpool" else (POOL, MIX_IN) if t < T else (POOL + QL, MIX_IN)
                    for k in range(K8):
                        w = slot(G_MIXIN + k // 4)[:, (k % 4) * MIX_IN + a:(k % 4) * MIX_IN + b]
                        h = hT[:, k, t * 128:(t + 1) * 128] if t < T else hcT[:, k, (t - T) * 128:(t - T + 1) * 128]
                        last = nc.tensor.matmul(B[:, 0:b - a], h, w, start=k == 0, stop=k == K8 - 1)
                elif kind == "latT":
                    t = args[0]
                    pe.wait_ge(drained_v, drains("V", place(0, "zlat", t)))
                    row = lat[:, LAT_ORDER.index(t) % 2, :]
                    if t < T:
                        for i in range(2):
                            transpose(B[:, i * 128:(i + 1) * 128], row[:, i * 128:(i + 1) * 128])
                    transpose(B[:, 256:384], row[:, QL:QL + KVL])
                    last = transpose(B[0:64, 384:512], row[:, QL + KVL:LROW])
                elif kind == "band":
                    g = args[0]
                    drained_through(place(0, "zpool", T - 1), "S")
                    if g == 0:
                        wait_granule(G_BAND)
                    bands = slot(G_BAND)[:, 0:20 * 128].rearrange("p (g b n) -> p g b n", g=4, b=5)
                    for o in range(T):
                        near = [i for i in (o - 1, o, o + 1) if 0 <= i < T]
                        for i in near:
                            b = i - o + 1 if i != o else 3 if o == 0 else 4 if o == T - 1 else 1
                            last = nc.tensor.matmul(B[:, o * 128:(o + 1) * 128], u_pool[:, i, g * 128:(g + 1) * 128],
                                                    bands[:, g, b, :], start=i == near[0], stop=i == near[-1])
                elif kind == "poolw":
                    g = args[0]
                    pe.wait_ge(drained_v, drains("V", place(0, "band", g)))
                    w = slot(G_BAND)[:, 20 * 128:24 * 128].rearrange("p (g n) -> p g n", g=4)
                    last = nc.tensor.matmul(B, w[:, g, :], diffT[:, g % 2, :], start=True, stop=True)
                elif kind == "value":
                    kt = args[0]
                    drained_through(place(0, "latT", 3), "S")
                    pe.wait_ge(attn_w_in, 16 * 4)
                    w = ukv.rearrange("p (h e) -> p h e", h=HEADS)[:, :, NOPE:NOPE + VD]
                    last = nc.tensor.matmul(B, kvT[:, kt * 128:(kt + 1) * 128], w, start=True, stop=True)
                elif kind == "row":
                    s, half = args
                    pe.wait_ge(diag_ready, 2 * l + (1 if s == 2 else 2))
                    diag = diags[(int(l), s)]
                    last = nc.tensor.matmul(B, ones[:, :], diag[:, 4 * half:4 * half + 4, :].rearrange("p a b -> p (a b)"),
                                            start=True, stop=True)
                elif kind == "mix":
                    t, half = args
                    pe.wait_ge(o_done, UNITS // 2)
                    wait_granule(G_MIXOUT)
                    wait_granule(G_MIXOUT + 1)
                    for k in range(K8):
                        w = slot(G_MIXOUT + k // 4)[:, (k % 4) * D + half * N:(k % 4) * D + half * N + N]
                        last = nc.tensor.matmul(B, catT[:, k, t * 128:(t + 1) * 128], w, start=k == 0, stop=k == K8 - 1)
                elif kind in ("hT", "h1T"):
                    t, half = args
                    m = NORM[("n2", int(l))] if kind == "hT" else NORM[("n1", 1)]
                    pe.wait_ge(xn_ready, m + t + 1)
                    for i in range(4):
                        last = transpose(B[:, i * 128:(i + 1) * 128], xn[:, t, 4 * half + i::K8])
                elif kind == "logit":
                    t = args[0]
                    drained_through(place(l, "hT", t, 1))
                    for k in range(K8):
                        last = nc.tensor.matmul(B[:, 0:EXPERTS], hT[:, k, t * 128:(t + 1) * 128],
                                                router[:, int(l), k, :], start=k == 0, stop=k == K8 - 1)
                elif kind == "affT":
                    pe.wait_ge(aff_ready, T * (1 + l))
                    for t in range(T):
                        last = transpose(B[0:EXPERTS, t * 128:(t + 1) * 128], aff[:, t, :])
                elif kind == "slotT":
                    pe.wait_ge(slots_ready, 1 + l)
                    for t in range(T):
                        last = transpose(B[:, t * EXPERTS:(t + 1) * EXPERTS],
                                         left[0:EXPERTS, t * 128:(t + 1) * 128], EXPERTS)
                elif kind in ("pwg", "pwa"):
                    c = args[0]
                    drained_through(place(1, "h1T", T - 1, 1))
                    g = G_PW1 + c // 2
                    wait_granule(g)
                    w = slot(g).rearrange("p (k h c) -> p k h c", k=K8, h=2)
                    for k in range(K8):
                        last = nc.tensor.matmul(B, w[:, k, int(kind == "pwg"), (c % 2) * 128:(c % 2) * 128 + 128],
                                                hT[:, k, :], start=k == 0, stop=k == K8 - 1)
                elif kind == "taps":
                    c = args[0]
                    pe.wait_ge(drained_v, drains("V", place(1, "pwa", c)))
                    pe.wait_ge(tap_diag_ready, c + 2 if c < K8 - 1 else 1)
                    for b in {3: (0, 1)}.get(c, (c - 2,) if c > 3 else ()):
                        moments(b)
                    many = pe_taps(c)
                    for i in range(many):
                        j = CONVW - many + i
                        w = last_diag[:, i, :] if c == K8 - 1 else tap_diag[:, c % 2, i, :]
                        last = nc.tensor.matmul(B, w, u_pad[:, c % 2, j:j + N], start=i == 0, stop=i == many - 1)
                elif kind == "shift":
                    pe.wait_ge(conv_done, 1)
                    last = nc.tensor.matmul(B, ones[:, :], conv[:, 0, :], start=True, stop=True)
                elif kind == "moments":
                    moments(K8 - 2)
                    last = moments(K8 - 1)
                elif kind == "pw2":
                    t, half = args
                    wait_granule(G_PW2)
                    wait_granule(G_PW2 + 1)
                    for k in range(K8):
                        pe.wait_ge(swish_done, K8 * t + k + 1)
                        w = slot(G_PW2 + k // 4)[:, (k % 4) * D + half * N:(k % 4) * D + half * N + N]
                        last = nc.tensor.matmul(B, conv[:, k, t * 128:(t + 1) * 128], w, start=k == 0, stop=k == K8 - 1)
                last.then_inc(filled, 1)

            pe.wait_ge(ones_set, 3)
            for n in range(len(L0)):
                fill(n)

            drained_through(len(L0) - 1)
            S = [PS[:, 2 * b:2 * b + 2, :].rearrange("p a b -> p (a b)") for b in range(2)]
            PT = PS[:, 4:6, :].rearrange("p a b -> p (a b)")

            def project_queries(h):
                pe.wait_ge(q_staged, h + 1)
                if not isinstance(h, int) or h > 0:
                    pe.wait_ge(late_added, h)
                for k in range(2):
                    last = nc.tensor.matmul(PS[:, 7, :], wq_stage[:, k, :], qlatT[:, k, :], start=k == 0, stop=k == 1)
                last.then_inc(q_projected, 1)

            def project_keys(j):
                pe.wait_ge(k_staged, j + 1)
                if not isinstance(j, int) or j > 0:
                    pe.wait_ge(exp_done, 8 * j - 1)
                nc.tensor.matmul(S[0][:, 0:512], wk_stage, kvT[:, 0:512], start=True, stop=True)
                nc.tensor.matmul(S[0][:, 512:768], wk_stage, kvT[:, 512:768], start=True, stop=True)\
                  .then_inc(k_projected, 1)

            def score(h, odd, qt):
                if not (isinstance(h, int) and h == 0 and qt < 2):
                    pe.wait_ge(exp_done, 4 * h + qt - 1)
                pe.wait_ge(q_nope_done, h + 1)
                pe.wait_ge(q_rope_done, h + 1)
                pe.wait_ge(k_nope_done, h + 1 if odd or qt else h + 2)
                for a, b in ((0, 512), (512, 768)):
                    last = nc.tensor.matmul(S[qt % 2][:, a:b], qT[:, qt * 128:(qt + 1) * 128], keys[odd][:, a:b],
                                            start=True, stop=True)
                last.then_inc(scores_ready, 1)

            def turn(h, qt):
                pe.wait_ge(exp_scaled, 4 * h + qt + 1)
                if not (isinstance(h, int) and h == 0 and qt == 0):
                    pe.wait_ge(pT_drained, 4 * h + qt)
                for k in range(KT):
                    last = transpose(PT[:, k * 128:(k + 1) * 128], exps[:, qt % 2, k * 128:(k + 1) * 128])
                last.then_inc(pT_ready, 1)

            def weigh(h, odd, half):
                pe.wait_ge(v_staged, h + 1)
                pe.wait_ge(pT_drained, 4 * h + 2 * half + 2)
                if not (isinstance(h, int) and h == 0 and half == 0):
                    pe.wait_ge(o_done, 2 * h + half)
                for k in range(KT):
                    for i in range(2):
                        last = nc.tensor.matmul(PS[64 * i:64 * i + 64, 6, 0:128], v_stage[odd][:, k, :],
                                                pT[:, 2 * half + i, k * 128:(k + 1) * 128],
                                                start=k == 0, stop=k == KT - 1)
                last.then_inc(o_ready, 1)

            def late_block(h, b):
                g = G_LATE + b
                pe.wait_ge(slot_in[g % SLOTS], arrivals(g) - 16 * (LATE - 1) + 16 * h)
                if b == 0:
                    pe.wait_ge(q_nope_done, h + 1)
                    pe.wait_ge(q_rope_done, h + 1)
                else:
                    pe.wait_ge(late_rows, 2 * h + 1)
                ada_block(slot(g).rearrange("p (k n) -> p k n", k=K8), 7).then_inc(late_filled, 1)

            def late_select(h):
                pe.wait_ge(late_rows, 2 * h + 2)
                ada_select(7).then_inc(late_selected, 1)

            def head(h, odd, first, more):
                if not first:
                    turn(h - 1, 3)
                if more:
                    late_block(h, 0)
                score(h, odd, 0)
                score(h, odd, 1)
                if more:
                    late_block(h, 1)
                turn(h, 0)
                if not first:
                    weigh(h - 1, 1 - odd, 1)
                score(h, odd, 2)
                if more:
                    late_select(h)
                turn(h, 1)
                score(h, odd, 3)
                turn(h, 2)
                weigh(h, odd, 0)
                if more:
                    project_queries(h + 1)

            def two_heads(j, first=False, more=True):
                head(2 * j, 0, first, True)
                head(2 * j + 1, 1, False, more)
                if more:
                    project_keys(j + 1)

            project_queries(0)
            project_keys(0)
            pe.wait_ge(odd_keys_set, 1)
            two_heads(0, first=True)
            with pe.Fori(1, HEADS // 2 - 1, 1) as j:
                two_heads(j)
            two_heads(HEADS // 2 - 1, more=False)
            turn(HEADS - 1, 3)
            weigh(HEADS - 1, 1, 1)
            pe.wait_ge(pT_drained, UNITS)
            pe.wait_ge(o_done, UNITS // 2)
            for n in range(len(L0), IN_L1):
                fill(n)

            def gather(g):
                pe.wait_ge(onehot_built, g + 1)
                for k in range(K8):
                    for t in range(T):
                        last = nc.tensor.matmul(PS[:, k // 4, (k % 4) * 128:(k % 4 + 1) * 128], xn[:, t, k::K8],
                                                onehot[:, t, :], start=t == 0, stop=t == T - 1)
                    if k % 4 == 3:
                        last.then_inc(xs_filled, 1)

            def turn_gated(g):
                for t in range(T):
                    last = transpose(PS[:, 2, t * 128:(t + 1) * 128], gated[:, t, :])
                last.then_inc(gT_filled, 1)

            def half_products(l, g, base, q0, lhs, bank):
                for q in range(4):
                    n = G_MOE[l] + q0 + q
                    s = n % SLOTS
                    pe.wait_ge(slot_in[s], arrivals(n) + base * 32)
                    w = ring[:, s, :].rearrange("p (e k n) -> p e k n", e=2, k=2)
                    for kk in range(2):
                        k = 2 * q + kk
                        for half in range(2):
                            for e in range(2):
                                last = nc.tensor.matmul(PS[64 * e:64 * e + 64, bank + half, :],
                                                        lhs[:, k, 64 * e:64 * e + 64],
                                                        w[:, e, kk, half * N:(half + 1) * N],
                                                        start=k == 0, stop=k == K8 - 1)
                    last.then_inc(moe_used, 1)

            def pair(l, j, more):
                g = j + PAIRS * l
                pe.wait_ge(xs_drained_v, g + 1)
                pe.wait_ge(xs_drained_s, g + 1)
                half_products(l, g, j, 0, xsT, 0)
                pe.wait_ge(gT_drained, g + 1)
                half_products(l, g, j, 4, xsT, 2)
                pe.wait_ge(act_done, 2 * g + 2)
                for k in range(K8):
                    last = transpose(PS[:, 6 + k // 4, (k % 4) * 128:(k % 4 + 1) * 128], act[:, k::K8])
                    if k % 4 == 3:
                        last.then_inc(aT_filled, 1)
                pe.wait_ge(aT_drained_v, g + 1)
                pe.wait_ge(aT_drained_s, g + 1)
                half_products(l, g, j, 8, actT, 4)
                if more:
                    gather(g + 1)
                pe.wait_ge(y_done, 2 * g + 2)
                for i in range(2 * T):
                    if i >= 2:
                        pe.wait_ge(scat_added, g * 8 + i - 1)
                    nc.tensor.matmul(PS[:, 6 + i % 2, :], gatedT[:, (i // 2) * 128:(i // 2 + 1) * 128],
                                     y_rows[:, (i % 2) * N:(i % 2 + 1) * N], start=True, stop=True)\
                      .then_inc(scat_filled, 1)
                if more:
                    turn_gated(g + 1)
                pe.wait_ge(scat_added, g * 8 + 8)

            def mixture(l):
                gather(PAIRS * l)
                turn_gated(PAIRS * l)
                with pe.Fori(0, PAIRS - 1, 1) as j:
                    pair(l, j, True)
                pair(l, PAIRS - 1, False)

            drained_through(IN_L1 - 1)
            mixture(0)
            for n in range(IN_L1, len(ITEMS)):
                fill(n)
            drained_through(len(ITEMS) - 1)
            mixture(1)

        @block.scalar
        def _(act_e):
            sc = nc.scalar
            chain = Chain(act_e, s_chain)

            def square(m, source, junk):
                sc.activation(junk, source, ACT.Square, accum_out=ssq[:, m:m + 1]).then_inc(ssq_ready, 1)

            def drain(n):
                l = int(n >= IN_L1)
                kind, args, engine = ITEMS[n]
                B = PS[:, n % NB, :]
                if engine == "S":
                    act_e.wait_ge(filled, n + 1)
                    if drains("S", n - 1):
                        act_e.wait_ge(drained_s, drains("S", n - 1))
                if kind == "zlat":
                    t = args[0]
                    act_e.wait_ge(filled, n + 1)
                    if t != LAT_ORDER[0]:
                        act_e.wait_ge(lat_ssq_ready, LAT_ORDER.index(t))
                    off = 0
                    if t < T:
                        sc.activation(lat_junk[:, 0:QL], B[:, 0:QL], ACT.Square, accum_out=lat_ssq[:, t, 0:1])
                        off = QL
                    sc.activation(lat_junk2, B[:, off:off + KVL], ACT.Square, accum_out=lat_ssq[:, t, 1:2])\
                      .then_inc(lat_ssq_ready, 1)
                    return
                if kind in ("mix", "pw2") and args[1] == 1:
                    t = args[0]
                    act_e.wait_ge(x_updated, 8 * l + 2 * t + 2)
                    if l and t == 2:
                        act_e.wait_ge(bias_added, T)
                    m = NORM[("n2", l)] + t
                    square(m, x[:, t, :], xn[:, t, :])
                    return
                if kind == "logit":
                    t = args[0]
                    act_e.wait_ge(drained_v, drains("V", n))
                    sc.activation(shifted[:, t, :], shifted[:, t, :], ACT.Exp, accum_out=aff_cols[:, 1, t:t + 1])\
                      .then_inc(aff_exp_done, 1)
                    return
                ready = ()
                if kind == "moments":
                    ready = (K8 - 1,)
                elif kind == "taps" and args[0] >= 2:
                    ready = (0, 1) if args[0] == 2 else (args[0] - 1,)
                for c in ready:
                    act_e.wait_ge(centred, c + 1)
                    if c >= 2:
                        act_e.wait_ge(moments_added, c - 1)
                    sc.activation(ln_sq[:, c % 2, :], conv[:, c, :], ACT.Square).then_inc(sq_ready, 1)
                if kind == "moments":
                    act_e.wait_ge(drained_v, drains("V", n))
                    sc.activation(ln_rstd, ln_rstd, ACT.Sqrt).then_inc(ln_root_done, 1)
                    for t in range(T):
                        act_e.wait_ge(scaled, t + 1)
                        for c in range(K8):
                            part = conv[:, c, t * 128:(t + 1) * 128]
                            sc.activation(part, part, ACT.Silu, bias=lnb[:, c:c + 1], scale=lng[:, c:c + 1])\
                              .then_inc(swish_done, 1)
                    return
                if engine != "S":
                    return
                if kind == "ada":
                    last = sc.activation(ada_rows[:, args[0] % 2, :], B, ACT.Copy)
                elif kind == "xT":
                    act_e.wait_ge(drained_v, drains("V", place(0, "sel", 1)))
                    k = args[0]
                    last = sc.activation(hT[:, k, :], B, ACT.Identity, bias=cols[:, 0, 0, 0, k:k + 1],
                                         scale=amp[:, 0, 0, 0, k:k + 1])
                elif kind == "cT":
                    act_e.wait_ge(drained_v, drains("V", place(0, "sel", 1)))
                    for i in range(2):
                        k = 2 * args[0] + i
                        last = sc.activation(hcT[:, k, :], B[:, i * NCTX:(i + 1) * NCTX], ACT.Identity,
                                             bias=cols[:, 0, 0, 1, k:k + 1], scale=amp[:, 0, 0, 1, k:k + 1])
                elif kind == "zpool":
                    last = sc.activation(u_pool[:, args[0], :], B, ACT.Copy)
                elif kind == "latT":
                    t = args[0]
                    act_e.wait_ge(attn_w_in, 16 * 4)
                    if t < T:
                        for i in range(2):
                            sc.activation(qlatT[:, i, t * 128:(t + 1) * 128], B[:, i * 128:(i + 1) * 128], ACT.Copy,
                                          scale=qg[:, i:i + 1])
                    at = (t - T if t >= T else CT + t) * 128
                    sc.activation(kvT[:, at:at + 128], B[:, 256:384], ACT.Copy, scale=kvg[:, 0:1])
                    last = sc.activation(kT[64:128, at:at + 128], B[0:64, 384:512], ACT.Copy)
                elif kind == "poolw":
                    last = sc.activation(catT[:, args[0], :], B, ACT.Copy, scale=pscale[:, args[0]:args[0] + 1])
                elif kind == "value":
                    last = sc.activation(values[:, args[0], :], B, ACT.Copy)
                elif kind == "row":
                    s, half = args
                    row = (g1_row if s == 2 else g2_row)[:, :].rearrange("p (n k) -> p k n", k=K8)
                    last = sc.activation(row[:, 4 * half:4 * half + 4, :], B.rearrange("p (k n) -> p k n", k=4), ACT.Copy)
                elif kind in ("hT", "h1T"):
                    t, half = args
                    norm = int(kind == "hT")
                    if l:
                        act_e.wait_ge(cols_ready, 1)
                    for i in range(4):
                        k = 4 * half + i
                        last = sc.activation(hT[:, k, t * 128:(t + 1) * 128], B[:, i * 128:(i + 1) * 128],
                                             ACT.Identity, bias=cols[:, l, 3 * norm, 0, k:k + 1],
                                             scale=amp[:, l, norm, 0, k:k + 1])
                elif kind == "affT":
                    last = sc.activation(affT[0:EXPERTS, :], B[0:EXPERTS, :], ACT.Copy)
                elif kind == "pwg":
                    c = args[0]
                    if c >= 2:
                        act_e.wait_ge(drained_v, drains("V", place(1, "pwa", c - 2)))
                    last = sc.activation(sig[:, c % 2, :], B, ACT.Sigmoid, bias=g_bias[:, c:c + 1])
                last.then_inc(drained_s, 1)
                if (kind, args) == ("pwg", (0,)):
                    act_e.dma_start(bias_row, b_pw2[0, :].unsqueeze(0).to_broadcast([128, D])).then_inc(bias_in, 16)

            act_e.wait_ge(cond_in, 32)
            for v in range(2):
                sc.activation(cond[:, :, 16 * v:16 * v + 16], cond_raw[:, v, :].unsqueeze(2).to_broadcast([128, K8, 16]),
                              ACT.Silu).then_inc(cond_ready, 1)
            act_e.wait_ge(x_arrived, 16)
            for t in range(T):
                square(t, x[:, t, :], xn[:, t, :])
            act_e.wait_ge(ctx_arrived, 16)
            for t in range(CT):
                square(NORM["ctx"] + t, ctx_x[:, t, :], hT_flat[:, t * D:(t + 1) * D])
            for n in range(len(L0)):
                drain(n)

            S = [PS[:, 2 * b:2 * b + 2, :].rearrange("p a b -> p (a b)") for b in range(2)]

            def queries(h):
                act_e.wait_ge(q_projected, h + 1)
                if not isinstance(h, int) or h > 0:
                    act_e.wait_ge(scores_ready, 4 * h)
                sc.activation(qT[0:NOPE, :], PS[0:NOPE, 7, :], ACT.Copy).then_inc(q_nope_done, 1)

            def two_keys(j):
                act_e.wait_ge(k_projected, j + 1)
                if not isinstance(j, int) or j > 0:
                    act_e.wait_ge(scores_ready, 8 * j)
                for odd in range(2):
                    sc.activation(keys[odd][0:NOPE, :], S[0][64 * odd:64 * odd + NOPE, 0:768], ACT.Copy)\
                      .then_inc(k_nope_done, 1)

            def output(j, odd, half):
                act_e.wait_ge(o_ready, 4 * j + 2 * odd + half + 1)
                for i in range(2):
                    at = (2 * half + i) * 128
                    last = sc.activation(hT_flat[64 * odd:64 * odd + VD, bass.ds(j * N + (4 * N + at), 128)],
                                         PS[64 * i:64 * i + VD, 6, 0:128], ACT.Copy)
                last.then_inc(o_done, 1)

            def late_rows_out(h, b):
                act_e.wait_ge(late_filled, 2 * h + b + 1)
                sc.activation(ada_rows[:, b, :], PS[:, 7, :], ACT.Copy).then_inc(late_rows, 1)

            def head(j, odd, first, more):
                h = 2 * j + odd
                for qt in range(T):
                    if more and qt == 0:
                        late_rows_out(h, 0)
                    act_e.wait_ge(bias_ready, 4 * h + qt + 1)
                    if not (first and qt < 2):
                        act_e.wait_ge(pT_ready, 4 * h + qt - 1)
                    sc.activation(exps[:, qt % 2, :], S[qt % 2][:, 0:768], ACT.Exp, bias=biases[:, qt:qt + 1],
                                  scale=SCALE, accum_out=sums[:, qt:qt + 1]).then_inc(exp_done, 1)
                    if more and qt == 1:
                        late_rows_out(h, 1)
                    if qt == 1 and not first:
                        output(*((j, 0) if odd else (j - 1, 1)), 1)
                    if qt == 3:
                        output(j, odd, 0)
                if more:
                    queries(h + 1)

            def two_heads(j, first=False, more=True):
                head(j, 0, first, True)
                head(j, 1, False, more)
                if more:
                    two_keys(j + 1)

            act_e.wait_ge(drained_s, drains("S", len(L0) - 1))
            sc.activation(kT_odd[64:128, :], kT[64:128, :], ACT.Copy).then_inc(odd_keys_set, 1)
            queries(0)
            two_keys(0)
            two_heads(0, first=True)
            with act_e.Fori(1, HEADS // 2 - 1, 1) as j:
                two_heads(j)
            two_heads(HEADS // 2 - 1, more=False)
            output(HEADS // 2 - 1, 1, 1)
            for n in range(len(L0), IN_L1):
                drain(n)

            def gathered(l, g):
                act_e.wait_ge(xs_filled, g * 2 + 2)
                for i in range(4):
                    k = 4 + i
                    last = sc.activation(xsT[:, k, :], PS[:, 1, i * 128:(i + 1) * 128], ACT.Identity,
                                         bias=cols[:, l, 3, 0, k:k + 1], scale=amp[:, l, 1, 0, k:k + 1])
                last.then_inc(xs_drained_s, 1)

            def pair(l, j, more):
                g = j + PAIRS * l
                act_e.wait_ge(moe_used, g * 12 + 4)
                for half in range(2):
                    sc.activation(silu_g[:, half, :], PS[:, half, :], ACT.Silu).then_inc(silu_done, 1)
                act_e.wait_ge(aT_filled, g * 2 + 2)
                sc.activation(actT[:, 4:8, :].rearrange("p a b -> p (a b)"), PS[:, 7, :], ACT.Copy)\
                  .then_inc(aT_drained_s, 1)
                if more:
                    gathered(l, g + 1)

            def mixture(l):
                gathered(l, PAIRS * l)
                with act_e.Fori(0, PAIRS - 1, 1) as j:
                    pair(l, j, True)
                pair(l, PAIRS - 1, False)

            mixture(0)
            for t in range(T):
                act_e.wait_ge(scat_added, 8 * PAIRS - 8 + 2 * t + 2)
                square(NORM[("n1", 1)] + t, x[:, t, :], xn[:, t, :])
            for n in range(IN_L1, len(ITEMS)):
                drain(n)
            act_e.wait_ge(x_updated, 16)
            act_e.dma_start(g1_row[:, :], final_g.unsqueeze(0).to_broadcast([128, D])).then_inc(final_in, 16)
            mixture(1)
            for t in range(T):
                act_e.wait_ge(scat_added, 16 * PAIRS - 8 + 2 * t + 2)
                square(NORM["final"] + t, x[:, t, :], xn[:, t, :])

        @block.vector
        def _(dve):
            v = nc.vector
            chain = Chain(dve, v_chain)

            def normalise(m, dst, src):
                dve.wait_ge(rstd_ready, m + 1)
                v.tensor_scalar(dst, src, rstd[:, m:m + 1], None, ALU.mult).then_inc(xn_ready, 1)

            def amplitude(l, norm, samples=1):
                for i in range(samples):
                    last = v.scalar_tensor_tensor(amp[:, l, norm, i, :], cols[:, l, 3 * norm + 1, i, :], 1.0,
                                                  ng[:, l, norm, :], ALU.add, ALU.mult)
                return last

            cols_flat = cols[:, :, :, :, :].rearrange("p a b v k -> p (a b v k)")
            bias_flat = ada_bias[:, :, :, :].rearrange("p a b k -> p (a b k)")

            def section(n, B):
                return v.tensor_tensor(cols_flat[:, bass.ds(n * 2 * K8, 2 * K8)].rearrange("p (v k) -> p v k", v=2),
                                       B[:, 0:2 * K8].rearrange("p (k v) -> p v k", v=2),
                                       bias_flat[:, bass.ds(n * K8, K8)].unsqueeze(1).to_broadcast([128, 2, K8]), ALU.add)

            def make_diag(l, s):
                v.tensor_tensor(diags[(l, s)], ident.unsqueeze(1).to_broadcast([128, K8, 128]),
                                cols[:, l, s, 0, :].unsqueeze(2).to_broadcast([128, K8, 128]), ALU.mult)\
                 .then_inc(diag_ready, 1)

            def residual(l, t, half, B):
                tmp = (odd_taps if l else ada_rows)[:, half, :]
                if t == 0 and half == 0:
                    dve.wait_ge(drained_s, drains("S", place(l, "row", 2, 0)))
                v.tensor_tensor(tmp, B, g1_row[:, half * N:(half + 1) * N], ALU.mult).then_inc(drained_v, 1)
                dve.wait_ge(drained_v, drains("V", place(l, "pw2" if l else "mix", t, half)))
                if l:
                    dve.wait_ge(bias_added, t + 1)
                v.tensor_tensor(x[:, t, half * N:(half + 1) * N], x[:, t, half * N:(half + 1) * N], tmp, ALU.add)\
                 .then_inc(x_updated, 1)

            def choose(l):
                dve.wait_ge(drained_s, drains("S", place(l, "affT")))
                src = affT[0:EXPERTS, :]
                for r in range(CAP // 8):
                    chain(v.max(top8[0:EXPERTS, :], src))
                    chain(v.match_replace(left[0:EXPERTS, :], top8[0:EXPERTS, :], src, -1.0))
                    src = left[0:EXPERTS, :]
                mask = affT[0:EXPERTS, :]
                chain(v.tensor_scalar(mask, src, 0.0, None, ALU.is_lt))
                chain(v.tensor_tensor_scan(running[0:EXPERTS, :], mask, mask, 0.0, ALU.add, ALU.max))
                chain(v.tensor_tensor(running[0:EXPERTS, :], running[0:EXPERTS, :], mask, ALU.mult))
                v.tensor_scalar(left[0:EXPERTS, :], running[0:EXPERTS, :], -1.0, None, ALU.add)\
                 .then_inc(slots_ready, 1)

            def drain(n):
                l = int(n >= IN_L1)
                kind, args, engine = ITEMS[n]
                B = PS[:, n % NB, :]
                if kind == "affT":
                    choose(l)
                    return
                if engine != "V":
                    return
                dve.wait_ge(filled, n + 1)
                if n:
                    dve.wait_ge(drained_v, drains("V", n - 1))
                if kind == "params":
                    v.tensor_copy(dwT[:, :, :].rearrange("p a b -> p (a b)"), B[:, 0:K8 * CONVW])
                    last = v.tensor_copy(vecT[:, :], B[:, 256:256 + VEC_ROWS])
                elif kind == "sel":
                    s = args[0]
                    if s == 0:
                        dve.wait_ge(small_in, 16 * 8)
                    if s in (1, 4):
                        chain(section(s, B))
                        amplitude(0, s // 3, 2).then_inc(drained_v, 1)
                    else:
                        section(s, B).then_inc(drained_v, 1)
                    dve.wait_ge(drained_v, drains("V", n))
                    if s == 2:
                        make_diag(0, 2)
                    return
                elif kind in ("xT", "cT"):
                    i = int(kind == "cT")
                    for j in range(1 + i):
                        k = 2 * args[0] + j if i else args[0]
                        dst, src = (hcT[:, k, :], B[:, j * NCTX:(j + 1) * NCTX]) if i else (hT[:, k, :], B)
                        last = v.tensor_scalar(dst, src, amp[:, 0, 0, i, k:k + 1], cols[:, 0, 0, i, k:k + 1],
                                               ALU.mult, ALU.add)
                elif kind == "zlat":
                    t = args[0]
                    seq = LAT_ORDER.index(t)
                    row = lat[:, seq % 2, :]
                    dve.wait_ge(lat_rstd_ready, seq + 1)
                    if seq >= 2:
                        dve.wait_ge(filled, place(0, "latT", LAT_ORDER[seq - 2]) + 1)
                    off = 0
                    if t < T:
                        v.tensor_scalar(row[:, 0:QL], B[:, 0:QL], lat_rstd[:, t, 0:1], None, ALU.mult)
                        off = QL
                    v.tensor_scalar(row[:, QL:QL + KVL], B[:, off:off + KVL], lat_rstd[:, t, 1:2], None, ALU.mult)
                    kr = B[:, off + KVL:off + KVL + ROPE]
                    if t < T:
                        if t == 0:
                            dve.wait_ge(attn_w_in, 16 * 4)
                        v.tensor_tensor(kr_tmp[:, 0, :], kr, rope_k[:, 0, t, :], ALU.mult)
                        kr4 = kr.rearrange("p (a h f) -> p a h f", a=2, h=2)
                        to4 = kr_tmp[:, 1, :].rearrange("p (a h f) -> p a h f", a=2, h=2)
                        sin4 = rope_k[:, 1, t, :].rearrange("p (a h f) -> p a h f", a=2, h=2)
                        for h in range(2):
                            last = v.tensor_tensor(to4[:, :, h, :], kr4[:, :, 1 - h, :], sin4[:, :, h, :], ALU.mult)
                        chain(last)
                        for h in range(2):
                            last = v.tensor_tensor(row[:, QL + KVL + h * ROPE:QL + KVL + (h + 1) * ROPE],
                                                   kr_tmp[:, 0, :], kr_tmp[:, 1, :], ALU.add)
                    else:
                        for h in range(2):
                            last = v.tensor_copy(row[:, QL + KVL + h * ROPE:QL + KVL + (h + 1) * ROPE], kr)
                elif kind == "band":
                    if args[0] >= 2:
                        dve.wait_ge(filled, place(0, "poolw", args[0] - 2) + 1)
                    last = v.tensor_copy(diffT[:, args[0] % 2, :], B)
                elif kind == "value":
                    last = v.tensor_copy(values[:, args[0], :], B)
                elif kind == "row":
                    s, half = args
                    row = (g1_row if s == 2 else g2_row)[:, :].rearrange("p (n k) -> p k n", k=K8)
                    last = v.tensor_copy(row[:, 4 * half:4 * half + 4, :], B.rearrange("p (k n) -> p k n", k=4))
                elif kind in ("mix", "pw2"):
                    t, half = args
                    residual(l, t, half, B)
                    if half and t == 0:
                        normalise(NORM[("n2", l)], xn[:, 0, :], x[:, 0, :])
                    return
                elif kind in ("hT", "h1T"):
                    t, half = args
                    norm = int(kind == "hT")
                    for i in range(4):
                        k = 4 * half + i
                        last = v.tensor_scalar(hT[:, k, t * 128:(t + 1) * 128], B[:, i * 128:(i + 1) * 128],
                                               amp[:, l, norm, 0, k:k + 1], cols[:, l, 3 * norm, 0, k:k + 1],
                                               ALU.mult, ALU.add)
                elif kind == "logit":
                    t = args[0]
                    chain(v.reduce_max(aff_cols[:, 0, t:t + 1], B[:, 0:EXPERTS], AX.X))
                    v.tensor_scalar(shifted[:, t, :], B[:, 0:EXPERTS], aff_cols[:, 0, t:t + 1], None, ALU.subtract)\
                     .then_inc(drained_v, 1)
                    if t < T - 1:
                        normalise(NORM[("n2", l)] + t + 1, xn[:, t + 1, :], x[:, t + 1, :])
                    dve.wait_ge(aff_exp_done, T * l + t + 1)
                    chain(v.reciprocal(aff_cols[:, 2, t:t + 1], aff_cols[:, 1, t:t + 1]))
                    v.tensor_scalar(aff[:, t, :], shifted[:, t, :], aff_cols[:, 2, t:t + 1], None, ALU.mult)\
                     .then_inc(aff_ready, 1)
                    return
                elif kind == "slotT":
                    v.tensor_copy(slot_of.rearrange("p a b -> p (a b)"), B[:, 0:T * EXPERTS]).then_inc(drained_v, 1)
                    return
                elif kind == "pwa":
                    c = args[0]
                    dve.wait_ge(drained_s, drains("S", place(1, "pwg", c)))
                    if c == 0:
                        dve.wait_ge(halo_set, 4)
                    if c >= 2:
                        dve.wait_ge(filled, place(1, "taps", c - 2) + 1)
                    v.scalar_tensor_tensor(u_pad[:, c % 2, HALO:HALO + N], B, a_bias[:, c:c + 1], sig[:, c % 2, :],
                                           ALU.add, ALU.mult).then_inc(drained_v, 1)
                    dve.wait_ge(drained_v, drains("V", n))
                    if c > 1:
                        dve.wait_ge(conv_done, c - 1)
                    for j in range(CONVW - pe_taps(c)):
                        to = (conv[:, c, :], odd_taps[:, c % 2, :])[j % 2]
                        step = (even_step, odd_step)[j % 2]
                        u = u_pad[:, c % 2, j:j + N]
                        if j == 0:
                            ins = v.tensor_scalar(to, u, dwT[:, c, 0:1], dw_bias[:, c:c + 1], ALU.mult, ALU.add)
                        elif j == 1:
                            ins = v.tensor_scalar(to, u, dwT[:, c, 1:2], None, ALU.mult)
                        else:
                            dve.wait_ge(step, dve_steps(j % 2, c) + j // 2)
                            ins = v.scalar_tensor_tensor(to, u, dwT[:, c, j:j + 1], to, ALU.mult, ALU.add)
                        ins.then_inc(step, 1)
                    return
                elif kind == "taps":
                    c = args[0]
                    dve.wait_ge(odd_step, dve_steps(1, c + 1))
                    last = v.tensor_tensor(odd_taps[:, c % 2, :], odd_taps[:, c % 2, :], B, ALU.add)
                elif kind == "shift":
                    last = v.tensor_scalar(shift, B, 1.0 / 128, None, ALU.mult)
                elif kind == "moments":
                    chain(v.tensor_copy(ln_mean, PS[:, 6, :]))
                    chain(v.tensor_tensor(shift, ln_mean, ln_mean, ALU.mult))
                    v.scalar_tensor_tensor(ln_rstd, PS[:, 7, :], EPS, shift, ALU.add, ALU.subtract)\
                     .then_inc(drained_v, 1)
                    dve.wait_ge(ln_root_done, 1)
                    chain(v.reciprocal(ln_rstd, ln_rstd))
                    for t in range(T):
                        part = conv[:, :, t * 128:(t + 1) * 128]
                        mean, root = (a[:, t * 128:(t + 1) * 128].unsqueeze(1).to_broadcast([128, K8, 128])
                                      for a in (ln_mean, ln_rstd))
                        chain(v.tensor_tensor(part, part, mean, ALU.subtract))
                        v.tensor_tensor(part, part, root, ALU.mult).then_inc(scaled, 1)
                    return
                last.then_inc(drained_v, 1)

            v.memset(ones[:, :], 1.0).then_inc(ones_set, 1)
            v.memset(one_dth[:, :], 1.0 / D).then_inc(ones_set, 1)
            v.memset(minus_half[:, :], -0.5).then_inc(ones_set, 1)
            for t in range(T):
                normalise(t, xn[:, t, :], x[:, t, :])
            for t in range(CT):
                normalise(NORM["ctx"] + t, ctx_x[:, t, :], ctx_x[:, t, :])
            for n in range(len(L0)):
                drain(n)

            S = [PS[:, 2 * b:2 * b + 2, :].rearrange("p a b -> p (a b)") for b in range(2)]
            PT = PS[:, 4:6, :].rearrange("p a b -> p (a b)")

            def rotate(h):
                dve.wait_ge(q_projected, h + 1)
                if not isinstance(h, int) or h > 0:
                    dve.wait_ge(scores_ready, 4 * h)
                v.tensor_tensor(qT[64:128, :], PS[64:128, 7, :], rope_q[64:128, :], ALU.mult).then_inc(q_rope_done, 1)

            def turned(h, qt):
                dve.wait_ge(pT_ready, 4 * h + qt + 1)
                if not (isinstance(h, int) and h == 0):
                    dve.wait_ge(o_ready, 2 * h - 1 + qt // 2)
                v.tensor_copy(pT[:, qt, :], PT[:, 0:768]).then_inc(pT_drained, 1)

            def head(h, first, more):
                for qt in range(T):
                    if more and qt == 3:
                        dve.wait_ge(late_selected, h + 1)
                        section(h + 5, PS[:, 7, :]).then_inc(late_added, 1)
                    unit = 4 * h + qt
                    dve.wait_ge(scores_ready, unit + 1)
                    v.reduce_max(maxima[:, qt:qt + 1], S[qt % 2][:, 0:768], AX.X).then_inc(max_step, 1)
                    dve.wait_ge(max_step, unit + 1)
                    v.tensor_scalar(biases[:, qt:qt + 1], maxima[:, qt:qt + 1], -SCALE, None, ALU.mult)\
                     .then_inc(bias_ready, 1)
                    if not (first and qt == 0):
                        turned(*((h, qt - 1) if qt else (h - 1, 3)))
                    dve.wait_ge(exp_done, unit + 1)
                    v.reciprocal(recips[:, qt:qt + 1], sums[:, qt:qt + 1]).then_inc(recip_done, 1)
                    dve.wait_ge(recip_done, unit + 1)
                    v.tensor_scalar(exps[:, qt % 2, :], exps[:, qt % 2, :], recips[:, qt:qt + 1], None, ALU.mult)\
                     .then_inc(exp_scaled, 1)
                if more:
                    rotate(h + 1)

            rotate(0)
            head(0, True, True)
            with dve.Fori(1, HEADS - 1, 1) as h:
                head(h, False, True)
            head(HEADS - 1, False, False)
            turned(HEADS - 1, 3)
            dve.wait_ge(late_added, LATE)
            make_diag(0, 5)
            for n in range(len(L0), IN_L1):
                drain(n)

            def choose_pair(g, j):
                for dst, scaled_by in ((onehot, False), (gated, True)):
                    for t in range(T):
                        for e in range(2):
                            s = slot_of[:, t, bass.ds(j * 2 + e, 1)]
                            if scaled_by:
                                last = v.tensor_scalar(dst[:, t, 64 * e:64 * e + 64], iota, s,
                                                       aff[:, t, bass.ds(j * 2 + e, 1)], ALU.is_equal, ALU.mult)
                            else:
                                last = v.tensor_scalar(dst[:, t, 64 * e:64 * e + 64], iota, s, None, ALU.is_equal)
                last.then_inc(onehot_built, 1)

            def gathered(l, g):
                dve.wait_ge(xs_filled, g * 2 + 1)
                for k in range(4):
                    last = v.tensor_scalar(xsT[:, k, :], PS[:, 0, k * 128:(k + 1) * 128], amp[:, l, 1, 0, k:k + 1],
                                           cols[:, l, 3, 0, k:k + 1], ALU.mult, ALU.add)
                last.then_inc(xs_drained_v, 1)

            def gated_turned(g):
                dve.wait_ge(gT_filled, g + 1)
                v.tensor_copy(gatedT, PS[:, 2, :]).then_inc(gT_drained, 1)

            def pair(l, j, more):
                g = j + PAIRS * l
                if more:
                    dve.wait_ge(xs_filled, g * 2 + 2)
                    choose_pair(g + 1, j + 1)
                dve.wait_ge(moe_used, g * 12 + 8)
                for half in range(2):
                    dve.wait_ge(silu_done, g * 2 + half + 1)
                    v.tensor_tensor(act[:, half * N:(half + 1) * N], silu_g[:, half, :], PS[:, 2 + half, :], ALU.mult)\
                     .then_inc(act_done, 1)
                dve.wait_ge(aT_filled, g * 2 + 1)
                v.tensor_copy(actT[:, 0:4, :].rearrange("p a b -> p (a b)"), PS[:, 6, :]).then_inc(aT_drained_v, 1)
                dve.wait_ge(moe_used, g * 12 + 12)
                for half in range(2):
                    v.tensor_tensor(y_rows[:, half * N:(half + 1) * N], PS[:, 4 + half, :],
                                    g2_row[:, half * N:(half + 1) * N], ALU.mult).then_inc(y_done, 1)
                if more:
                    gathered(l, g + 1)
                for i in range(2 * T):
                    dve.wait_ge(scat_filled, g * 8 + i + 1)
                    part = x[:, i // 2, (i % 2) * N:(i % 2 + 1) * N]
                    v.tensor_tensor(part, part, PS[:, 6 + i % 2, :], ALU.add).then_inc(scat_added, 1)
                if more:
                    gated_turned(g + 1)

            def mixture(l):
                choose_pair(PAIRS * l, 0)
                gathered(l, PAIRS * l)
                gated_turned(PAIRS * l)
                with dve.Fori(0, PAIRS - 1, 1) as j:
                    pair(l, j, True)
                pair(l, PAIRS - 1, False)

            dve.wait_ge(drained_v, drains("V", IN_L1 - 1))
            mixture(0)
            amplitude(1, 0)
            amplitude(1, 1).then_inc(cols_ready, 1)
            dve.wait_ge(cols_ready, 1)
            for t in range(T):
                normalise(NORM[("n1", 1)] + t, xn[:, t, :], x[:, t, :])
            for n in range(IN_L1, len(ITEMS)):
                drain(n)
            dve.wait_ge(drained_v, drains("V", len(ITEMS) - 1))
            mixture(1)
            dve.wait_ge(final_in, 16)
            for t in range(T):
                m = NORM["final"] + t
                dve.wait_ge(rstd_ready, m + 1)
                v.scalar_tensor_tensor(xn[:, t, :], x[:, t, :], rstd[:, m:m + 1], g1_row[:, :], ALU.mult, ALU.mult)\
                 .then_inc(out_ready, 1)

        @block.gpsimd
        def _(pool):
            p = nc.gpsimd
            chain = Chain(pool, p_chain)

            def reciprocal_root(m):
                pool.wait_ge(ssq_ready, m + 1)
                chain(p.tensor_scalar(ms[:, m:m + 1], ssq[:, m:m + 1], 1.0 / D, EPS, ALU.mult, ALU.add))
                p.tensor_tensor(rstd[:, m:m + 1], ms[:, m:m + 1], minus_half[:, :], ALU.pow).then_inc(rstd_ready, 1)

            pool.wait_ge(ones_set, 3)
            for m in range(6):
                reciprocal_root(m)
            for seq, t in enumerate(LAT_ORDER):
                pool.wait_ge(lat_ssq_ready, seq + 1)
                a = 0 if t < T else 1
                if t < T:
                    p.tensor_scalar(lat_ms[:, t, 0:1], lat_ssq[:, t, 0:1], 1.0 / QL, EPS, ALU.mult, ALU.add)
                chain(p.tensor_scalar(lat_ms[:, t, 1:2], lat_ssq[:, t, 1:2], 1.0 / KVL, EPS, ALU.mult, ALU.add))
                p.tensor_tensor(lat_rstd[:, t, a:2], lat_ms[:, t, a:2], minus_half[:, :].to_broadcast([128, 2 - a]),
                                ALU.pow).then_inc(lat_rstd_ready, 1)

            pool.wait_ge(attn_w_in, 16 * 4)

            def stage_queries(h):
                if not isinstance(h, int) or h > 0:
                    pool.wait_ge(q_projected, h)
                p.tensor_copy(wq_stage[:, :, 0:QK], uq[:, :, bass.ds(h * QK, QK)])
                for half in range(2):
                    for axis in range(2):
                        to = QK + axis * 16 + half * 8
                        fr = NOPE + axis * 16 + (1 - half) * 8
                        last = p.tensor_copy(wq_stage[:, :, to:to + 8], uq[:, :, bass.ds(h * QK + fr, 8)])
                last.then_inc(q_staged, 1)

            def stage_values(h, odd):
                if not isinstance(h, int) or h > 1:
                    pool.wait_ge(o_ready, 2 * h - 2)
                p.tensor_copy(v_stage[odd], values[:, :, bass.ds(h * VD, VD)]).then_inc(v_staged, 1)

            def stage_two_heads(j):
                stage_queries(2 * j)
                if not isinstance(j, int) or j > 0:
                    pool.wait_ge(k_projected, j)
                p.tensor_copy(wk_stage.rearrange("p (a b) -> p a b", a=2),
                              ukv_heads[:, bass.ds(2 * j, 2), 0:NOPE]).then_inc(k_staged, 1)
                if isinstance(j, int):
                    pool.wait_ge(drained_v, drains("V", len(L0) - 1))
                    pool.wait_ge(drained_s, drains("S", len(L0) - 1))
                stage_values(2 * j, 0)
                stage_queries(2 * j + 1)
                stage_values(2 * j + 1, 1)

            ukv_heads = ukv.rearrange("p (h e) -> p h e", h=HEADS)
            stage_two_heads(0)
            with pool.Fori(1, HEADS // 2, 1) as j:
                stage_two_heads(j)
            for t in range(T):
                reciprocal_root(NORM[("n2", 0)] + t)
            for t in range(T):
                reciprocal_root(NORM[("n1", 1)] + t)
            for b in range(2):
                for a in (0, HALO + N):
                    p.memset(u_pad[:, b, a:a + HALO], 0.0).then_inc(halo_set, 1)
            pool.wait_ge(filled, place(1, "h1T", T - 1, 1) + 1)

            def whole(c):
                pool.wait_ge(drained_v, drains("V", place(1, "taps", c)))
                pool.wait_ge(even_step, dve_steps(0, c + 1))
                p.tensor_tensor(conv[:, c, :], conv[:, c, :], odd_taps[:, c % 2, :], ALU.add).then_inc(conv_done, 1)
                pool.wait_ge(conv_done, c + 1)

            def centre(c):
                pool.wait_ge(drained_v, drains("V", place(1, "shift")))
                p.tensor_tensor(conv[:, c, :], conv[:, c, :], shift, ALU.subtract).then_inc(centred, 1)

            def make_diag(s):
                p.tensor_tensor(diags[(1, s)], ident.unsqueeze(1).to_broadcast([128, K8, 128]),
                                cols[:, 1, s, 0, :].unsqueeze(2).to_broadcast([128, K8, 128]), ALU.mult)\
                 .then_inc(diag_ready, 1)

            for c in [K8 - 1] + list(range(K8 - 1)):
                many = pe_taps(c)
                if 2 <= c < K8 - 1:
                    pool.wait_ge(filled, place(1, "taps", c - 2) + 1)
                for i in range(many):
                    j = CONVW - many + i
                    w = last_diag[:, i, :] if c == K8 - 1 else tap_diag[:, c % 2, i, :]
                    last = p.tensor_scalar(w, ident, dwT[:, c, j:j + 1], None, ALU.mult)
                last.then_inc(tap_diag_ready, 1)
                if 2 <= c < K8 - 1:
                    whole(c - 2)
                if c == 3:
                    centre(0)
                if 3 <= c < K8 - 1:
                    centre(c - 2)
            whole(K8 - 3)
            centre(K8 - 3)
            whole(K8 - 2)
            centre(K8 - 2)
            make_diag(2)
            pool.wait_ge(filled, place(1, "taps", K8 - 2) + 1)
            make_diag(5)
            whole(K8 - 1)
            centre(K8 - 1)
            pool.wait_ge(bias_in, 16)
            pool.wait_ge(drained_s, drains("S", place(1, "row", 2, 0)))
            pool.wait_ge(drained_v, drains("V", place(1, "row", 2, 1)))
            chain(p.tensor_tensor(bias_row, bias_row, g1_row[:, :], ALU.mult))
            for t in range(T):
                p.tensor_tensor(x[:, t, :], x[:, t, :], bias_row, ALU.add).then_inc(bias_added, 1)
            for t in range(T):
                reciprocal_root(NORM[("n2", 1)] + t)
            for t in range(T):
                reciprocal_root(NORM["final"] + t)


_INS = ["x", "c", "ctx", "c_ctx", "ada_w", "ada_b", "norm1_g", "norm2_g", "mix_w_in", "pool_w", "pool_scale",
        "q_norm_g", "kv_norm_g", "w_uq", "w_ukv", "mix_w_out", "conv_w_pw1", "conv_b_pw1", "conv_w_dw", "conv_b_dw",
        "conv_ln_g", "conv_ln_b", "conv_w_pw2", "conv_b_pw2", "router_w", "exp_wg", "exp_wu", "exp_wd", "final_g"]


def tables():
    import numpy as np
    small = np.zeros((128, 194), np.float32)
    small[:, 0:128] = np.eye(128, dtype=np.float32)
    small[:, 128:192] = np.arange(64, dtype=np.float32)
    small[0::32, 192] = 1.0
    small[16::32, 193] = 1.0
    tok = np.arange(N)
    inv = (1.0 / (10000.0 ** (np.arange(0, 16, 2, dtype=np.float32) / 16))).astype(np.float32)
    pos = np.stack([tok // 64, tok % 64], 1).astype(np.float32)
    ang = (pos[:, :, None] * inv).astype(np.float32)
    cos = np.repeat(np.cos(ang)[:, :, None, :], 2, axis=2).reshape(N, ROPE).astype(np.float32)
    sin = (np.repeat(np.sin(ang)[:, :, None, :], 2, axis=2)
           * np.array([-1.0, 1.0])[None, None, :, None]).reshape(N, ROPE).astype(np.float32)
    rope = np.zeros((128, N + 2 * T * ROPE), np.float32)
    rope[64:96, 0:N] = cos.T
    rope[96:128, 0:N] = sin.T
    rope[:, N:N + T * ROPE] = cos.reshape(T, 128, ROPE).transpose(1, 0, 2).reshape(128, T * ROPE)
    rope[:, N + T * ROPE:] = sin.reshape(T, 128, ROPE).transpose(1, 0, 2).reshape(128, T * ROPE)
    band = np.zeros((128, 4, 5, 128), np.float32)
    for g, w in enumerate((2, 4, 8, 16)):
        lo, hi = np.clip(tok - w // 2, 0, N), np.clip(tok - w // 2 + w, 0, N)
        inside = (tok[:, None] >= lo) & (tok[:, None] < hi)
        full = inside / (hi - lo).astype(np.float32) - np.eye(N)
        for b, (i, o) in enumerate(((0, 1), (1, 1), (2, 1), (0, 0), (3, 3))):
            band[:, g, b, :] = full[i * 128:(i + 1) * 128, o * 128:(o + 1) * 128]
    return {"small_tab": small, "rope_tab": rope, "band_tab": band.reshape(128, 20 * 128)}


def kernel(**inputs):
    import numpy as _np
    import concourse.bacc as _bacc
    from concourse import mybir as _mybir
    from concourse.bass_utils import run_bass_kernel_spmd as _run

    nc = _bacc.Bacc("TRN2", target_bir_lowering=False, num_devices=1)
    given = {n: _np.ascontiguousarray(inputs[n]) for n in _INS}
    given.update(tables())
    arrays, args = {}, []
    for name, a in given.items():
        arrays[f"in_{name}_dram"] = a
        args.append(nc.dram_tensor(f"in_{name}_dram", a.shape, _mybir.dt.from_np(a.dtype), kind="ExternalInput").ap())
    args.append(nc.dram_tensor("out_0_dram", (1, N, D), _mybir.dt.float32, kind="ExternalOutput").ap())
    build(nc, *args)
    r = _run(nc, [arrays], core_ids=[0])
    return r.results[0]["out_0_dram"]
```

```python
import concourse.bass as bass
from concourse import mybir
from contextlib import ExitStack

D = 1024
N = 512
NCTX = 256
T = N // 128
CT = NCTX // 128
KT = T + CT
K8 = D // 128
HEADS = 8
NOPE = 64
ROPE = 32
VD = 64
QK = NOPE + ROPE
QL = 256
KVL = 128
POOL = 512
SECTIONS = 12
EARLY = 4
LATE = HEADS - 2
LAT = QL + KVL + ROPE
MIX_IN = POOL + LAT
LROW = QL + KVL + 2 * ROPE
CONVW = 31
HALO = CONVW // 2
EXPERTS = 16
PAIRS = EXPERTS // 2
CAP = 2 * N // EXPERTS
SCALE = float(QK) ** -0.5
EPS = 1e-6
SLOTS = 6
SLOT_WORDS = 4096
NB = 6
VEC_ROWS = 5 * K8 + 4 + 2 + 1
PE_TAPS = 2
POOL_TAPS = 8
PE_TAPS_LAST = 12
UNITS = HEADS * T
LAT_ORDER = [4, 5, 0, 1, 2, 3]


def conditioning(s):
    return [("ada", (2 * s,), "S"), ("ada", (2 * s + 1,), "S"), ("sel", (s,), "V")]


def l0_items():
    o = [("params", (), "V")] + conditioning(0) + conditioning(1)
    o += [("cT", (k,), "VS"[k % 2]) for k in range(K8 // 2)]
    o += [("xT", (k,), "VS"[k % 2]) for k in range(K8)]
    o += [("zlat", (4,), "V"), ("zlat", (5,), "V"), ("zlat", (0,), "V"), ("latT", (4,), "S"),
          ("zpool", (0,), "S"), ("latT", (5,), "S"), ("zlat", (1,), "V"), ("latT", (0,), "S"),
          ("zpool", (1,), "S"), ("zlat", (2,), "V"), ("latT", (1,), "S"), ("zpool", (2,), "S"),
          ("zlat", (3,), "V"), ("latT", (2,), "S"), ("zpool", (3,), "S"), ("latT", (3,), "S")]
    o += [("band", (0,), "V"), ("band", (1,), "V"), ("poolw", (0,), "S"), ("poolw", (1,), "S"),
          ("band", (2,), "V"), ("band", (3,), "V"), ("poolw", (2,), "S"), ("poolw", (3,), "S")]
    o += [("value", (k,), "VS"[k % 2]) for k in range(KT)]
    for s in range(2, EARLY):
        o += conditioning(s)
    return o + [("row", (2, 0), "S"), ("row", (2, 1), "S")]


def product_and_route(kind):
    o = []
    for t in range(T):
        o += [(kind, (t, 0), "V")]
        if t:
            o += [("hT", (t - 1, 0), "V"), ("hT", (t - 1, 1), "S")]
        o += [(kind, (t, 1), "V")]
        if t:
            o += [("logit", (t - 1,), "V")]
    if kind == "mix":
        o += [("row", (5, 0), "S"), ("row", (5, 1), "S")]
    o += [("hT", (T - 1, 0), "V"), ("hT", (T - 1, 1), "S"), ("logit", (T - 1,), "V")]
    o += [("affT", (), "S")]
    if kind == "mix":
        for s in range(EARLY + LATE, SECTIONS):
            o += conditioning(s)
    return o + [("slotT", (), "V")]


def mix_items():
    return product_and_route("mix")


def conv_items():
    o = []
    for t in range(T):
        o += [("h1T", (t, 0), "V"), ("h1T", (t, 1), "S")]
    for c in range(K8):
        o += [("pwg", (c,), "S")]
        if c == 3:
            o += [("shift", (), "V")]
        o += [("pwa", (c,), "V")]
        if c:
            o += [("taps", (c - 1,), "V")]
    o += [("taps", (K8 - 1,), "V"), ("row", (2, 0), "S"), ("row", (2, 1), "S"), ("moments", (), "V"),
          ("row", (5, 0), "S"), ("row", (5, 1), "S")]
    return o + product_and_route("pw2")


L0, MIX, CONV = l0_items(), mix_items(), conv_items()
ITEMS = L0 + MIX + CONV
IN_L1 = len(L0) + len(MIX)
PLACES = {(n >= IN_L1, kind, args): n for n, (kind, args, _) in enumerate(ITEMS)}


def place(layer, kind, *args):
    return PLACES[(layer == 1, kind, args)]


def bank_of(n):
    start = max(s for s in (0, len(L0), IN_L1) if s <= n)
    return (n - start) % NB, n - NB if n - NB >= start else None


def drains(engine, through):
    return sum(e == engine for _, _, e in ITEMS[:through + 1])


SPARE = (SLOTS, SLOTS + 1)
ORDER = ([("ada", b) for b in range(4)] + [("mixin", 0), ("mixin", 1), ("band", 0)]
         + [("ada", b) for b in range(4, 2 * EARLY)] + [("late", 0), ("late", 1), ("mixout", 0), ("mixout", 1)]
         + [("ada", b) for b in range(2 * (EARLY + LATE), 2 * SECTIONS)]
         + [("moe0", n) for n in range(12 * PAIRS) if n not in SPARE]
         + [("pw1", q) for q in range(4)] + [("pw2", 0), ("pw2", 1)]
         + [("moe1", n) for n in range(12 * PAIRS) if n not in SPARE])
GRANULE = {name: g for g, name in enumerate(ORDER)}
G_MIXIN, G_BAND, G_MIXOUT, G_PW1, G_PW2 = (GRANULE[(name, 0)] for name in ("mixin", "band", "mixout", "pw1", "pw2"))
MOE_GRANULES = 12 * PAIRS
G_LATE = GRANULE[("late", 0)]
TWO_DMAS = {G_BAND} | {G_PW1 + q for q in range(4)}


def arrivals(g):
    return 16 * sum(LATE if ORDER[n][0] == "late" else 1 + (n in TWO_DMAS) for n in range(g % SLOTS, g + 1, SLOTS))


def last_use(g):
    name, i = ORDER[g]
    if name == "ada":
        return place(0, "ada", i)
    if name == "pw1":
        return place(1, "pwa", 2 * i + 1)
    return {"mixin": place(0, "zpool", T - 1), "band": place(0, "poolw", 3), "mixout": place(0, "mix", T - 1, 1),
            "pw2": place(1, "pw2", T - 1, 1)}[name]


def pe_taps(c):
    return PE_TAPS_LAST if c == K8 - 1 else PE_TAPS


def dve_taps(c):
    return CONVW - pe_taps(c) - POOL_TAPS


def dve_steps(parity, c):
    return sum((dve_taps(i) + 1 - parity) // 2 for i in range(c))


class Chain:

    def __init__(self, eng, sem):
        self.eng, self.sem, self.n = eng, sem, 0

    def __call__(self, ins):
        self.n += 1
        ins.then_inc(self.sem, 1)
        self.eng.wait_ge(self.sem, self.n)


def build(nc, x_in, c_in, ctx_in, cctx_in, ada_w, ada_b, norm1_g, norm2_g, mix_w_in, pool_w, pool_scale,
          q_norm_g, kv_norm_g, w_uq, w_ukv, mix_w_out, pw1, b_pw1, w_dw, b_dw, ln_g, ln_b, pw2, b_pw2,
          router_w, exp_wg, exp_wu, exp_wd, final_g, small_tab, rope_tab, band_tab, out):
    fp32 = mybir.dt.float32
    ALU = mybir.AluOpType
    ACT = mybir.ActivationFunctionType
    AX = mybir.AxisListType
    stack = ExitStack()
    with stack:
        def sb(name, shape):
            return stack.enter_context(nc.sbuf_tensor(name, shape, fp32))

        def sem(name):
            return stack.enter_context(nc.semaphore(name))

        ring = sb("ring", [128, SLOTS, SLOT_WORDS])
        x = sb("x", [128, T, D])
        xn = sb("xn", [128, T, D])
        hT = sb("hT", [128, K8, N])
        consts = sb("consts", [128, 128 + 64 + 2])
        ident, iota, pick = consts[:, 0:128], consts[:, 128:192], consts[:, 192:194]
        ones = sb("ones", [128, 128])
        one_dth = sb("one_dth", [128, 128])
        minus_half = sb("minus_half", [128, 1])
        cond_raw = sb("cond_raw", [128, 2, K8])
        cond = sb("cond", [128, K8, 32])
        ada_bias = sb("ada_bias", [128, 2, 6, K8])
        ng = sb("ng", [128, 2, 2, K8])
        cols = sb("cols", [128, 2, 6, 2, K8])
        amp = sb("amp", [128, 2, 2, 2, K8])
        router = sb("router", [128, 2, K8, EXPERTS])
        g1_row = sb("g1_row", [128, D])
        g2_row = sb("g2_row", [128, D])
        dwT = sb("dwT", [128, K8, CONVW])
        vecT = sb("vecT", [128, VEC_ROWS])
        a_bias, g_bias, dw_bias, lng, lnb = (vecT[:, i * K8:(i + 1) * K8] for i in range(5))
        pscale, qg, kvg = vecT[:, 40:44], vecT[:, 44:46], vecT[:, 46:47]
        ssq = sb("ssq", [128, 22])
        ms = sb("ms", [128, 22])
        rstd = sb("rstd", [128, 22])
        lat_ssq = sb("lat_ssq", [128, KT, 2])
        lat_ms = sb("lat_ms", [128, KT, 2])
        lat_rstd = sb("lat_rstd", [128, KT, 2])
        ada_rows = sb("ada_rows", [128, 2, N])
        ARENA = 11450
        arena = sb("arena", [128, ARENA])

        def carver(at):
            here = [at]

            def cut(*shape):
                words = 1
                for s in shape:
                    words *= s
                v = arena[:, here[0]:here[0] + words]
                here[0] += words
                assert here[0] <= ARENA, here[0]
                if len(shape) == 2:
                    v = v.rearrange("p (a b) -> p a b", a=shape[0])
                if len(shape) == 3:
                    v = v.rearrange("p (a b c) -> p a b c", a=shape[0], b=shape[1])
                return v
            return cut

        cut = carver(0)
        qT = cut(N)
        kT = cut(KT * 128)
        kvT = cut(KT * 128)
        hcT = arena[:, 0:K8 * NCTX].rearrange("p (k n) -> p k n", k=K8)
        uq = cut(2, HEADS * QK)
        ukv = cut(HEADS * (NOPE + VD))
        wq_stage = cut(2, 128)
        qlatT = cut(2, N)
        rope_q = cut(N)
        rope_k = cut(2, T, ROPE)
        head_cols = cut(4, T)
        maxima, biases, sums, recips = (head_cols[:, i, :] for i in range(4))
        kr_tmp = cut(2, ROPE)
        values = cut(KT, HEADS * VD)
        values_flat = values.rearrange("p a b -> p (a b)")
        ctx_x = values_flat[:, 0:CT * D].rearrange("p (a b) -> p a b", a=CT)
        dw_rows = values_flat[:, CT * D:CT * D + D]
        exps = cut(2, KT * 128)
        exps_flat = exps.rearrange("p a b -> p (a b)")
        vec_rows = exps_flat[:, 1280:1408]
        lat_junk = exps_flat[:, 1024:1280]
        lat_junk2 = exps_flat[:, 1408:1536]
        catT = hT
        hT_flat = hT[:, :, :].rearrange("p a b -> p (a b)")
        diffT = hT_flat[:, 4 * N:6 * N].rearrange("p (a b) -> p a b", a=2)
        xn_flat = xn[:, :, :].rearrange("p a b -> p (a b)")
        u_pool = xn_flat[:, 0:T * N].rearrange("p (a b) -> p a b", a=T)
        pT = xn_flat[:, 0:T * KT * 128].rearrange("p (a b) -> p a b", a=T)
        kT_odd = xn_flat[:, T * KT * 128:(T + 1) * KT * 128]
        wk_stage = xn_flat[:, (T + 1) * KT * 128:(T + 1) * KT * 128 + 2 * NOPE]
        assert T * N + 2 * LROW <= T * KT * 128
        keys = (kT, kT_odd)
        v_stage = [g2_row[:, i * KT * VD:(i + 1) * KT * VD].rearrange("p (a b) -> p a b", a=KT) for i in range(2)]
        lat = xn_flat[:, T * N:T * N + 2 * LROW].rearrange("p (a b) -> p a b", a=2)

        cut = carver(0)
        onehot = cut(T, 128)
        gated = cut(T, 128)
        gatedT = cut(N)
        xsT = cut(K8, 128)
        silu_g = cut(2, N)
        act = cut(D)
        actT = cut(K8, 128)
        y_rows = cut(D)
        spare = [cut(SLOT_WORDS), hT[:, :, :].rearrange("p a b -> p (a b)")]

        ROUTE = ARENA - 224
        assert spare[0].offset + SLOT_WORDS <= arena[:, ROUTE:].offset
        cut = carver(ROUTE)
        aff = cut(T, EXPERTS)
        shifted = cut(T, EXPERTS)
        slot_of = cut(T, EXPERTS)
        aff_cols = cut(3, T)
        top8 = cut(8)
        cut = carver(0)
        affT = cut(N)
        left = cut(N)
        running = cut(N)

        cut = carver(0)
        u_pad = cut(2, N + 2 * HALO)
        conv = cut(K8, N)
        tap_diag = cut(2, PE_TAPS, 128)
        sig = cut(2, N)
        ln_sq = cut(2, N)
        odd_taps = cut(2, N)
        shift = cut(N)
        pool_taps = cut(2, N)
        ln_mean, ln_rstd = pool_taps[:, 0, :], pool_taps[:, 1, :]
        assert ln_rstd.offset + N <= arena[:, ROUTE:].offset

        bias_row = xn_flat[:, 2 * D:3 * D]
        last_diag = xn_flat[:, 0:PE_TAPS_LAST * 128].rearrange("p (a b) -> p a b", a=PE_TAPS_LAST)
        products = [xn_flat[:, PE_TAPS_LAST * 128:PE_TAPS_LAST * 128 + N], cut(N)]
        assert PE_TAPS_LAST * 128 + N <= 2 * D
        diags = {(0, 2): exps_flat[:, 0:D], (0, 5): exps_flat[:, 0:D], (1, 2): xn_flat[:, 3 * D:4 * D],
                 (1, 5): sig.rearrange("p a b -> p (a b)")}
        assert exps_flat[:, 0:D].offset + D <= arena[:, ROUTE:].offset
        diags = {key: v.rearrange("p (k n) -> p k n", k=K8) for key, v in diags.items()}

        PS = stack.enter_context(nc.psum_tensor("PS", [128, 8, N], fp32))

        cond_in, x_arrived, ctx_arrived, consts_in, params_in, small_in, attn_w_in = map(
            sem, ("cond_in", "x_arrived", "ctx_arrived", "consts_in", "params_in", "small_in", "attn_w_in"))
        slot_in = [sem(f"slot_in{q}") for q in range(SLOTS)]
        spare_in = [sem(f"spare_in{i}") for i in range(2)]
        moe_used = sem("moe_used")
        ones_set, cond_ready, filled, drained_v, drained_s = map(
            sem, ("ones_set", "cond_ready", "filled", "drained_v", "drained_s"))
        drained = {"V": drained_v, "S": drained_s}
        v_chain, p_chain = sem("v_chain"), sem("p_chain")
        ssq_ready, rstd_ready, xn_ready, x_updated = map(sem, ("ssq_ready", "rstd_ready", "xn_ready", "x_updated"))
        cols_ready, diag_ready = sem("cols_ready"), sem("diag_ready")
        late_filled, late_rows, late_selected, late_added = map(
            sem, ("late_filled", "late_rows", "late_selected", "late_added"))
        lat_ssq_ready, lat_rstd_ready = sem("lat_ssq_ready"), sem("lat_rstd_ready")
        q_staged, k_staged, v_staged, q_projected, k_projected, q_nope_done, k_nope_done, q_rope_done = map(
            sem, ("q_staged", "k_staged", "v_staged", "q_projected", "k_projected", "q_nope_done", "k_nope_done",
                  "q_rope_done"))
        max_step, scores_ready, bias_ready, exp_done, recip_done, exp_scaled, pT_ready, pT_drained, o_ready, o_done = map(
            sem, ("max_step", "scores_ready", "bias_ready", "exp_done", "recip_done", "exp_scaled", "pT_ready",
                  "pT_drained", "o_ready", "o_done"))
        odd_keys_set = sem("odd_keys_set")
        aff_exp_done, aff_ready, slots_ready = map(sem, ("aff_exp_done", "aff_ready", "slots_ready"))
        gated_built = sem("gated_built")
        onehot_built, xs_filled, xs_drained_v, xs_drained_s, gT_filled, gT_drained = map(
            sem, ("onehot_built", "xs_filled", "xs_drained_v", "xs_drained_s", "gT_filled", "gT_drained"))
        silu_done, act_done, aT_filled, aT_drained_v, aT_drained_s, y_done, scat_filled, scat_added = map(
            sem, ("silu_done", "act_done", "aT_filled", "aT_drained_v", "aT_drained_s", "y_done", "scat_filled",
                  "scat_added"))
        even_step, odd_step = sem("even_step"), sem("odd_step")
        product_ready, product_added = sem("product_ready"), sem("product_added")
        halo_set, tap_diag_ready, conv_done, centred, sq_ready, moments_added = map(
            sem, ("halo_set", "tap_diag_ready", "conv_done", "centred", "sq_ready", "moments_added"))
        ln_root_done, scaled, swish_done, bias_in, bias_added = map(
            sem, ("ln_root_done", "scaled", "swish_done", "bias_in", "bias_added"))
        final_in, out_ready, out_done = sem("final_in"), sem("out_ready"), sem("out_done")

        block = stack.enter_context(nc.Block())

        NORM = {("n1", 0): 0, "ctx": 4, ("n2", 0): 6, ("n1", 1): 10, ("n2", 1): 14, "final": 18}

        def column(v):
            return v.rearrange("(p k) -> p k", k=K8)

        def slot(g):
            return ring[:, g % SLOTS, :]

        @block.sync
        def _(sp):
            sp.dma_start(cond_raw[:, 0, :], column(c_in[0, :])).then_inc(cond_in, 16)
            sp.dma_start(cond_raw[:, 1, :], column(cctx_in)).then_inc(cond_in, 16)
            sp.dma_start(consts[:, :], small_tab).then_inc(consts_in, 16)
            sp.dma_start(x[:, :, :], x_in[0, :, :].rearrange("(t p) d -> p t d", p=128)).then_inc(x_arrived, 16)
            sp.dma_start(ctx_x, ctx_in[0, :, :].rearrange("(t p) d -> p t d", p=128)).then_inc(ctx_arrived, 16)

            def slot_free(g):
                before = g - SLOTS
                if ORDER[before][0] == "moe0":
                    sp.wait_ge(moe_used, ORDER[before][1] + 1)
                elif ORDER[before][0] == "moe1":
                    sp.wait_ge(moe_used, MOE_GRANULES + ORDER[before][1] + 1)
                elif ORDER[before][0] == "late":
                    sp.wait_ge(late_filled, 2 * LATE)
                else:
                    sp.wait_ge(filled, last_use(before) + 1)

            def load(g, parts):
                assert len(parts) == 1 + (g in TWO_DMAS)
                if g >= SLOTS:
                    slot_free(g)
                for dst, src in parts:
                    sp.dma_start(dst, src).then_inc(slot_in[g % SLOTS], 16)

            def load_ada(b):
                g = GRANULE[("ada", b)]
                l, s = divmod(b // 2, SECTIONS // 2)
                load(g, [(slot(g).rearrange("p (k n) -> p k n", k=K8), ada_blocks(l)[s, b % 2, :, :, :])])

            def ada_blocks(l):
                return ada_w[l, :, :].rearrange("(p k) (s b n) -> s b p k n", k=K8, b=2, n=N)

            def late_slot(b):
                return slot(G_LATE + b).rearrange("p (k n) -> p k n", k=K8)

            sp.dma_start(dw_rows[0:CONVW, :], w_dw[0, :, :]).then_inc(params_in, 16)
            at = 0
            for v in (b_pw1[0, :], b_dw[0, :], ln_g[0, :], ln_b[0, :], pool_scale[0, :], q_norm_g[0, :], kv_norm_g[0, :]):
                n = v.shape[0] // 128
                sp.dma_start(vec_rows[at:at + n, :], v.rearrange("(c p) -> c p", p=128)).then_inc(params_in, 16)
                at += n
            assert at == VEC_ROWS
            for b in range(4):
                load_ada(b)
            for l in range(2):
                sp.dma_start(ada_bias[:, l, :, :], ada_b[l, :].rearrange("(s p k) -> p s k", s=6, k=K8))\
                  .then_inc(small_in, 16)
                sp.dma_start(ng[:, l, 0, :], column(norm1_g[l, :])).then_inc(small_in, 16)
                sp.dma_start(ng[:, l, 1, :], column(norm2_g[l, :])).then_inc(small_in, 16)
                sp.dma_start(router[:, l, :, :], router_w[l, :, :].rearrange("(p k) e -> p k e", k=K8))\
                  .then_inc(small_in, 16)
            for h in range(2):
                g = G_MIXIN + h
                load(g, [(slot(g)[:, 0:4 * MIX_IN].rearrange("p (k n) -> p k n", k=4),
                          mix_w_in[0, :, :].rearrange("(p h k) n -> p h k n", h=2, k=4)[:, h, :, :])])
            sp.dma_start(rope_q, rope_tab[:, 0:N]).then_inc(attn_w_in, 16)
            sp.dma_start(rope_k.rearrange("p a t r -> p (a t r)"), rope_tab[:, N:N + 2 * T * ROPE])\
              .then_inc(attn_w_in, 16)
            sp.dma_start(uq, w_uq[0, :, :].rearrange("(k p) n -> p k n", p=128)).then_inc(attn_w_in, 16)
            sp.dma_start(ukv, w_ukv[0, :, :]).then_inc(attn_w_in, 16)
            load(G_BAND, [(slot(G_BAND)[:, 0:20 * 128], band_tab),
                          (slot(G_BAND)[:, 20 * 128:24 * 128].rearrange("p (g n) -> p g n", g=4),
                           pool_w[0, :, :, :].rearrange("g p n -> p g n"))])
            for b in range(4, 2 * EARLY):
                load_ada(b)
            for b in range(2):
                slot_free(G_LATE + b)
                sp.dma_start(late_slot(b), ada_blocks(0)[EARLY, b, :, :, :]).then_inc(slot_in[(G_LATE + b) % SLOTS], 16)
            for h in range(2):
                g = G_MIXOUT + h
                load(g, [(slot(g).rearrange("p (k n) -> p k n", k=4),
                          mix_w_out[0, h * N:(h + 1) * N, :].rearrange("(k p) n -> p k n", p=128))])

            def load_quarter(l, j, q, dst, arrived):
                w = (exp_wg, exp_wu, exp_wd)[q // 4]
                src = w[l, :, :, :].rearrange("(g e) (p k) n -> g p e (k n)", e=2, k=K8)
                sp.dma_start(dst.rearrange("p (e n) -> p e n", e=2),
                             src[j, :, :, 2 * D * (q % 4):2 * D * (q % 4 + 1)]).then_inc(arrived, 16)

            def load_pair(l, j):
                for q in range(12):
                    if isinstance(j, int) and j == 0 and q in SPARE:
                        if q == SPARE[0] and l == 0:
                            sp.wait_ge(filled, place(0, "row", 5, 1) + 1)
                        elif q == SPARE[0]:
                            sp.wait_ge(x_updated, 4 * T)
                        else:
                            sp.wait_ge(filled, place(l, "logit", T - 1) + 1)
                        load_quarter(l, j, q, spare[q - SPARE[0]], spare_in[q - SPARE[0]])
                        continue
                    if isinstance(j, int):
                        g = GRANULE[(f"moe{l}", 12 * j + q)]
                        slot_free(g)
                    else:
                        g = GRANULE[(f"moe{l}", 24 + q)]
                        sp.wait_ge(moe_used, j * 12 + (MOE_GRANULES * l + ORDER[g - SLOTS][1] + 1 - 24))
                    load_quarter(l, j, q, slot(g), slot_in[g % SLOTS])

            for b in range(2 * (EARLY + LATE), 2 * SECTIONS - 2):
                load_ada(b)
            for b in range(2):
                sp.wait_ge(late_filled, b + 1)
                sp.dma_start(late_slot(b), ada_blocks(0)[EARLY + 1, b, :, :, :])\
                  .then_inc(slot_in[(G_LATE + b) % SLOTS], 16)
            with sp.Fori(0, LATE - 2, 1) as s:
                for b in range(2):
                    sp.wait_ge(late_filled, 2 * s + (b + 3))
                    sp.dma_start(late_slot(b), ada_blocks(1)[s, b, :, :, :])\
                      .then_inc(slot_in[(G_LATE + b) % SLOTS], 16)
            for b in range(2 * SECTIONS - 2, 2 * SECTIONS):
                load_ada(b)
            load_pair(0, 0)
            load_pair(0, 1)
            with sp.Fori(2, PAIRS, 1) as j:
                load_pair(0, j)
            for q in range(4):
                g = G_PW1 + q
                dst = slot(g).rearrange("p (k h c) -> p k h c", k=K8, h=2)
                src = pw1[0, :, :].rearrange("(p k) (h q c) -> p k h q c", k=K8, h=2, q=4)
                load(g, [(dst[:, :, h, :], src[:, :, h, q, :]) for h in range(2)])
            for h in range(2):
                g = G_PW2 + h
                load(g, [(slot(g).rearrange("p (k n) -> p k n", k=4),
                          pw2[0, h * N:(h + 1) * N, :].rearrange("(k p) n -> p k n", p=128))])
            load_pair(1, 0)
            load_pair(1, 1)
            with sp.Fori(2, PAIRS, 1) as j:
                load_pair(1, j)
            for t in range(T):
                sp.wait_ge(out_ready, t + 1)
                sp.dma_start(out[0, t * 128:(t + 1) * 128, :], xn[:, t, :]).then_inc(out_done, 16)
            sp.wait_ge(out_done, 16 * T)

        @block.tensor
        def _(pe):
            def wait_granule(g):
                pe.wait_ge(slot_in[g % SLOTS], arrivals(g))

            def transpose(o, i, rows=128):
                return nc.tensor.transpose(o, i, ident[0:rows, 0:rows])

            def drained_through(n, engines="VS"):
                for e in engines:
                    if drains(e, n):
                        pe.wait_ge(drained[e], drains(e, n))

            def ada_block(w, bank):
                for k in range(K8):
                    r = 32 * (k % 4)
                    last = nc.tensor.matmul(PS[r:r + 32, bank, :], cond[:, k, :], w[:, k, :],
                                            start=k < 4, stop=k >= 4)
                return last

            def ada_select(bank):
                for h in range(2):
                    for k in range(K8):
                        last = nc.tensor.matmul(PS[64 * h:64 * h + 64, bank, 2 * k:2 * k + 2],
                                                ada_rows[:, h, k::K8], pick, start=True, stop=True)
                return last

            def moments(c):
                pe.wait_ge(centred, c + 1)
                nc.tensor.matmul(PS[:, 6, :], one_dth[:, :], conv[:, c, :], start=c == 0, stop=c == K8 - 1)
                pe.wait_ge(sq_ready, c + 1)
                last = nc.tensor.matmul(PS[:, 7, :], one_dth[:, :], ln_sq[:, c % 2, :], start=c == 0, stop=c == K8 - 1)
                if c < K8 - 1:
                    last.then_inc(moments_added, 1)
                return last

            def mix_part(n, k0, k1):
                t, half = ITEMS[n][1]
                wait_granule(G_MIXOUT)
                wait_granule(G_MIXOUT + 1)
                for k in range(k0, k1):
                    w = slot(G_MIXOUT + k // 4)[:, (k % 4) * D + half * N:(k % 4) * D + half * N + N]
                    last = nc.tensor.matmul(PS[:, bank_of(n)[0], :], catT[:, k, t * 128:(t + 1) * 128], w,
                                            start=k == 0, stop=k == K8 - 1)
                return last

            def fill(n):
                l = n >= IN_L1
                kind, args, _ = ITEMS[n]
                bank, before = bank_of(n)
                if before is not None:
                    e = ITEMS[before][2]
                    pe.wait_ge(drained[e], drains(e, before))
                B = PS[:, bank, :]
                if kind == "params":
                    pe.wait_ge(consts_in, 16)
                    pe.wait_ge(params_in, 16 * 8)
                    for c in range(K8):
                        transpose(B[:, c * CONVW:(c + 1) * CONVW], dw_rows[0:CONVW, c * 128:(c + 1) * 128], CONVW)
                    last = transpose(B[:, 256:256 + VEC_ROWS], vec_rows[0:VEC_ROWS, :], VEC_ROWS)
                elif kind == "ada":
                    g = GRANULE[(kind, args[0])]
                    pe.wait_ge(cond_ready, 2)
                    wait_granule(g)
                    w = slot(g).rearrange("p (k n) -> p k n", k=K8)
                    last = ada_block(w, bank)
                elif kind == "sel":
                    drained_through(n - 1, "S")
                    last = ada_select(bank)
                elif kind in ("xT", "cT"):
                    pe.wait_ge(xn_ready, 6)
                    if kind == "xT":
                        for t in range(T):
                            last = transpose(B[:, t * 128:(t + 1) * 128], xn[:, t, args[0]::K8])
                    else:
                        for i in range(4):
                            last = transpose(B[:, i * 128:(i + 1) * 128],
                                             ctx_x[:, i % 2, 2 * args[0] + i // 2::K8])
                elif kind in ("zlat", "zpool"):
                    t = args[0]
                    drained_through(place(0, "xT", K8 - 1))
                    a, b = (0, POOL) if kind == "zpool" else (POOL, MIX_IN) if t < T else (POOL + QL, MIX_IN)
                    for k in range(K8):
                        if k % 4 == 0:
                            wait_granule(G_MIXIN + k // 4)
                        w = slot(G_MIXIN + k // 4)[:, (k % 4) * MIX_IN + a:(k % 4) * MIX_IN + b]
                        h = hT[:, k, t * 128:(t + 1) * 128] if t < T else hcT[:, k, (t - T) * 128:(t - T + 1) * 128]
                        last = nc.tensor.matmul(B[:, 0:b - a], h, w, start=k == 0, stop=k == K8 - 1)
                elif kind == "latT":
                    t = args[0]
                    pe.wait_ge(drained_v, drains("V", place(0, "zlat", t)))
                    row = lat[:, LAT_ORDER.index(t) % 2, :]
                    if t < T:
                        for i in range(2):
                            transpose(B[:, i * 128:(i + 1) * 128], row[:, i * 128:(i + 1) * 128])
                    transpose(B[:, 256:384], row[:, QL:QL + KVL])
                    last = transpose(B[0:64, 384:512], row[:, QL + KVL:LROW])
                elif kind == "band":
                    g = args[0]
                    drained_through(place(0, "zpool", T - 1), "S")
                    if g == 0:
                        wait_granule(G_BAND)
                    bands = slot(G_BAND)[:, 0:20 * 128].rearrange("p (g b n) -> p g b n", g=4, b=5)
                    for o in range(T):
                        near = [i for i in (o - 1, o, o + 1) if 0 <= i < T]
                        for i in near:
                            b = i - o + 1 if i != o else 3 if o == 0 else 4 if o == T - 1 else 1
                            last = nc.tensor.matmul(B[:, o * 128:(o + 1) * 128], u_pool[:, i, g * 128:(g + 1) * 128],
                                                    bands[:, g, b, :], start=i == near[0], stop=i == near[-1])
                elif kind == "poolw":
                    g = args[0]
                    pe.wait_ge(drained_v, drains("V", place(0, "band", g)))
                    w = slot(G_BAND)[:, 20 * 128:24 * 128].rearrange("p (g n) -> p g n", g=4)
                    last = nc.tensor.matmul(B, w[:, g, :], diffT[:, g % 2, :], start=True, stop=True)
                elif kind == "value":
                    kt = args[0]
                    drained_through(place(0, "latT", 3), "S")
                    pe.wait_ge(attn_w_in, 16 * 4)
                    w = ukv.rearrange("p (h e) -> p h e", h=HEADS)[:, :, NOPE:NOPE + VD]
                    last = nc.tensor.matmul(B, kvT[:, kt * 128:(kt + 1) * 128], w, start=True, stop=True)
                elif kind == "row":
                    s, half = args
                    pe.wait_ge(diag_ready, 2 * l + (1 if s == 2 else 2))
                    diag = diags[(int(l), s)]
                    last = nc.tensor.matmul(B, ones[:, :], diag[:, 4 * half:4 * half + 4, :].rearrange("p a b -> p (a b)"),
                                            start=True, stop=True)
                elif kind == "mix":
                    if args[0]:
                        mix_part(n, 0, K8 - 1)
                    pe.wait_ge(o_done, HEADS)
                    last = mix_part(n, K8 - 1, K8)
                elif kind in ("hT", "h1T"):
                    t, half = args
                    m = NORM[("n2", int(l))] if kind == "hT" else NORM[("n1", 1)]
                    pe.wait_ge(xn_ready, m + t + 1)
                    for i in range(4):
                        last = transpose(B[:, i * 128:(i + 1) * 128], xn[:, t, 4 * half + i::K8])
                elif kind == "logit":
                    t = args[0]
                    drained_through(place(l, "hT", t, 1))
                    for k in range(K8):
                        last = nc.tensor.matmul(B[:, 0:EXPERTS], hT[:, k, t * 128:(t + 1) * 128],
                                                router[:, int(l), k, :], start=k == 0, stop=k == K8 - 1)
                elif kind == "affT":
                    pe.wait_ge(aff_ready, T * (1 + l))
                    for t in range(T):
                        last = transpose(B[0:EXPERTS, t * 128:(t + 1) * 128], aff[:, t, :])
                elif kind == "slotT":
                    pe.wait_ge(slots_ready, 1 + l)
                    for t in range(T):
                        last = transpose(B[:, t * EXPERTS:(t + 1) * EXPERTS],
                                         left[0:EXPERTS, t * 128:(t + 1) * 128], EXPERTS)
                elif kind in ("pwg", "pwa"):
                    c = args[0]
                    drained_through(place(1, "h1T", T - 1, 1))
                    g = G_PW1 + c // 2
                    wait_granule(g)
                    w = slot(g).rearrange("p (k h c) -> p k h c", k=K8, h=2)
                    for k in range(K8):
                        last = nc.tensor.matmul(B, w[:, k, int(kind == "pwg"), (c % 2) * 128:(c % 2) * 128 + 128],
                                                hT[:, k, :], start=k == 0, stop=k == K8 - 1)
                elif kind == "taps":
                    c = args[0]
                    pe.wait_ge(drained_v, drains("V", place(1, "pwa", c)))
                    pe.wait_ge(tap_diag_ready, c + 2 if c < K8 - 1 else 1)
                    for b in {3: (0, 1), K8 - 1: ()}.get(c, (c - 2,) if c > 3 else ()):
                        moments(b)
                    many = pe_taps(c)
                    for i in range(many):
                        j = CONVW - many + i
                        w = last_diag[:, i, :] if c == K8 - 1 else tap_diag[:, c % 2, i, :]
                        last = nc.tensor.matmul(B, w, u_pad[:, c % 2, j:j + N], start=i == 0, stop=i == many - 1)
                elif kind == "shift":
                    pe.wait_ge(conv_done, 1)
                    last = nc.tensor.matmul(B, ones[:, :], conv[:, 0, :], start=True, stop=True)
                elif kind == "moments":
                    moments(K8 - 3)
                    moments(K8 - 2)
                    last = moments(K8 - 1)
                elif kind == "pw2":
                    t, half = args
                    wait_granule(G_PW2)
                    wait_granule(G_PW2 + 1)
                    for k in range(K8):
                        pe.wait_ge(swish_done, K8 * t + k + 1)
                        w = slot(G_PW2 + k // 4)[:, (k % 4) * D + half * N:(k % 4) * D + half * N + N]
                        last = nc.tensor.matmul(B, conv[:, k, t * 128:(t + 1) * 128], w, start=k == 0, stop=k == K8 - 1)
                last.then_inc(filled, 1)

            pe.wait_ge(ones_set, 3)
            for n in range(len(L0)):
                fill(n)

            drained_through(len(L0) - 1)
            S = [PS[:, 2 * b:2 * b + 2, :].rearrange("p a b -> p (a b)") for b in range(2)]
            PT = PS[:, 4:6, :].rearrange("p a b -> p (a b)")

            def project_queries(h):
                pe.wait_ge(q_staged, h + 1)
                if not isinstance(h, int) or 0 < h <= LATE:
                    pe.wait_ge(late_added, h)
                elif h > LATE:
                    pe.wait_ge(q_nope_done, h)
                    pe.wait_ge(q_rope_done, h)
                for k in range(2):
                    last = nc.tensor.matmul(PS[:, 7, :], wq_stage[:, k, :], qlatT[:, k, :], start=k == 0, stop=k == 1)
                last.then_inc(q_projected, 1)

            def project_keys(j):
                pe.wait_ge(k_staged, j + 1)
                if not isinstance(j, int) or j > 0:
                    pe.wait_ge(exp_done, 8 * j - 1)
                nc.tensor.matmul(S[0][:, 0:512], wk_stage, kvT[:, 0:512], start=True, stop=True)
                nc.tensor.matmul(S[0][:, 512:768], wk_stage, kvT[:, 512:768], start=True, stop=True)\
                  .then_inc(k_projected, 1)

            def score(h, odd, qt):
                if not (isinstance(h, int) and h == 0 and qt < 2):
                    pe.wait_ge(exp_done, 4 * h + qt - 1)
                pe.wait_ge(q_nope_done, h + 1)
                pe.wait_ge(q_rope_done, h + 1)
                pe.wait_ge(k_nope_done, h + 1 if odd or qt else h + 2)
                for a, b in ((0, 512), (512, 768)):
                    last = nc.tensor.matmul(S[qt % 2][:, a:b], qT[:, qt * 128:(qt + 1) * 128], keys[odd][:, a:b],
                                            start=True, stop=True)
                last.then_inc(scores_ready, 1)

            def turn(h, qt):
                pe.wait_ge(exp_scaled, 4 * h + qt + 1)
                if not (isinstance(h, int) and h == 0 and qt == 0):
                    pe.wait_ge(pT_drained, 4 * h + qt)
                for k in range(KT):
                    last = transpose(PT[:, k * 128:(k + 1) * 128], exps[:, qt % 2, k * 128:(k + 1) * 128])
                last.then_inc(pT_ready, 1)

            def weigh(h, odd):
                pe.wait_ge(v_staged, h + 1)
                pe.wait_ge(pT_drained, 4 * h + 4)
                if not (isinstance(h, int) and h == 0):
                    pe.wait_ge(o_done, h)
                for k in range(KT):
                    for i in range(2):
                        last = nc.tensor.matmul(PS[64 * i:64 * i + 64, 6, 0:256], v_stage[odd][:, k, :],
                                                pT[:, 2 * i:2 * i + 2, k * 128:(k + 1) * 128],
                                                start=k == 0, stop=k == KT - 1)
                last.then_inc(o_ready, 1)

            def late_block(h, b):
                g = G_LATE + b
                pe.wait_ge(slot_in[g % SLOTS], arrivals(g) - 16 * (LATE - 1) + 16 * h)
                if b == 0:
                    pe.wait_ge(q_nope_done, h + 1)
                    pe.wait_ge(q_rope_done, h + 1)
                else:
                    pe.wait_ge(late_rows, 2 * h + 1)
                ada_block(slot(g).rearrange("p (k n) -> p k n", k=K8), 7).then_inc(late_filled, 1)

            def late_select(h):
                pe.wait_ge(late_rows, 2 * h + 2)
                ada_select(7).then_inc(late_selected, 1)

            def head(h, odd, first, more, late):
                if late:
                    late_block(h, 0)
                score(h, odd, 0)
                if not first:
                    turn(h - 1, 2)
                score(h, odd, 1)
                if not first:
                    turn(h - 1, 3)
                if late:
                    late_block(h, 1)
                score(h, odd, 2)
                if not first:
                    weigh(h - 1, 1 - odd)
                turn(h, 0)
                if late:
                    late_select(h)
                score(h, odd, 3)
                turn(h, 1)
                if more:
                    project_queries(h + 1)

            def two_heads(j, first=False, more=True):
                head(2 * j, 0, first, True, more)
                head(2 * j + 1, 1, False, more, more)
                if more:
                    project_keys(j + 1)

            project_queries(0)
            project_keys(0)
            pe.wait_ge(odd_keys_set, 1)
            two_heads(0, first=True)
            with pe.Fori(1, HEADS // 2 - 1, 1) as j:
                two_heads(j)
            two_heads(HEADS // 2 - 1, more=False)
            pe.wait_ge(exp_done, UNITS - 1)
            mix_part(len(L0), 0, K8 // 2)
            turn(HEADS - 1, 2)
            mix_part(len(L0), K8 // 2, K8 - 1)
            turn(HEADS - 1, 3)
            mix_part(len(L0) + 1, 0, K8 - 1)
            weigh(HEADS - 1, 1)
            pe.wait_ge(pT_drained, UNITS)
            pe.wait_ge(o_done, HEADS)
            for n in range(len(L0), IN_L1):
                fill(n)

            def gather(g):
                pe.wait_ge(onehot_built, g + 1)
                for k in range(K8):
                    for t in range(T):
                        last = nc.tensor.matmul(PS[:, k // 4, (k % 4) * 128:(k % 4 + 1) * 128], xn[:, t, k::K8],
                                                onehot[:, t, :], start=t == 0, stop=t == T - 1)
                    if k % 4 == 3:
                        last.then_inc(xs_filled, 1)

            def turn_gated(g):
                pe.wait_ge(gated_built, g + 1)
                for t in range(T):
                    last = transpose(PS[:, 2, t * 128:(t + 1) * 128], gated[:, t, :])
                last.then_inc(gT_filled, 1)

            def half_products(l, j, q0, lhs, bank):
                for q in range(4):
                    if isinstance(j, int) and j == 0 and q0 + q in SPARE:
                        i = q0 + q - SPARE[0]
                        pe.wait_ge(spare_in[i], 16 * (l + 1))
                        weights = spare[i]
                    elif isinstance(j, int) and j == 0:
                        n = GRANULE[(f"moe{l}", q0 + q)]
                        wait_granule(n)
                        weights = slot(n)
                    else:
                        n = GRANULE[(f"moe{l}", 12 + q0 + q)]
                        pe.wait_ge(slot_in[n % SLOTS], j * 32 + (arrivals(n) - 32))
                        weights = slot(n)
                    w = weights.rearrange("p (e k n) -> p e k n", e=2, k=2)
                    for kk in range(2):
                        k = 2 * q + kk
                        for half in range(2):
                            for e in range(2):
                                last = nc.tensor.matmul(PS[64 * e:64 * e + 64, bank + half, :],
                                                        lhs[:, k, 64 * e:64 * e + 64],
                                                        w[:, e, kk, half * N:(half + 1) * N],
                                                        start=k == 0, stop=k == K8 - 1)
                    last.then_inc(moe_used, 1)

            def pair(l, j, more):
                g = j + PAIRS * l
                pe.wait_ge(xs_drained_v, g + 1)
                pe.wait_ge(xs_drained_s, g + 1)
                half_products(l, j, 0, xsT, 0)
                pe.wait_ge(gT_drained, g + 1)
                half_products(l, j, 4, xsT, 2)
                pe.wait_ge(act_done, 2 * g + 2)
                for k in range(K8):
                    last = transpose(PS[:, 6 + k // 4, (k % 4) * 128:(k % 4 + 1) * 128], act[:, k::K8])
                    if k % 4 == 3:
                        last.then_inc(aT_filled, 1)
                pe.wait_ge(aT_drained_v, g + 1)
                pe.wait_ge(aT_drained_s, g + 1)
                half_products(l, j, 8, actT, 4)
                if more:
                    gather(g + 1)
                pe.wait_ge(y_done, 2 * g + 2)
                for i in range(2 * T):
                    if i >= 2:
                        pe.wait_ge(scat_added, g * 8 + i - 1)
                    nc.tensor.matmul(PS[:, 6 + i % 2, :], gatedT[:, (i // 2) * 128:(i // 2 + 1) * 128],
                                     y_rows[:, (i % 2) * N:(i % 2 + 1) * N], start=True, stop=True)\
                      .then_inc(scat_filled, 1)
                if more:
                    turn_gated(g + 1)
                pe.wait_ge(scat_added, g * 8 + 8)

            def mixture(l):
                gather(PAIRS * l)
                turn_gated(PAIRS * l)
                pair(l, 0, True)
                with pe.Fori(1, PAIRS - 1, 1) as j:
                    pair(l, j, True)
                pair(l, PAIRS - 1, False)

            drained_through(IN_L1 - 1)
            mixture(0)
            for n in range(IN_L1, len(ITEMS)):
                fill(n)
            drained_through(len(ITEMS) - 1)
            mixture(1)

        @block.scalar
        def _(act_e):
            sc = nc.scalar

            def square(m, source, junk):
                sc.activation(junk, source, ACT.Square, accum_out=ssq[:, m:m + 1]).then_inc(ssq_ready, 1)

            def drain(n):
                l = int(n >= IN_L1)
                kind, args, engine = ITEMS[n]
                B = PS[:, bank_of(n)[0], :]
                if engine == "S":
                    act_e.wait_ge(filled, n + 1)
                    if drains("S", n - 1):
                        act_e.wait_ge(drained_s, drains("S", n - 1))
                if kind == "zlat":
                    t = args[0]
                    act_e.wait_ge(filled, n + 1)
                    if t != LAT_ORDER[0]:
                        act_e.wait_ge(lat_ssq_ready, LAT_ORDER.index(t))
                    off = 0
                    if t < T:
                        sc.activation(lat_junk[:, 0:QL], B[:, 0:QL], ACT.Square, accum_out=lat_ssq[:, t, 0:1])
                        off = QL
                    sc.activation(lat_junk2, B[:, off:off + KVL], ACT.Square, accum_out=lat_ssq[:, t, 1:2])\
                      .then_inc(lat_ssq_ready, 1)
                    return
                if kind in ("mix", "pw2") and args[1] == 1:
                    t = args[0]
                    act_e.wait_ge(x_updated, 8 * l + 2 * t + 2)
                    if l and t == 2:
                        act_e.wait_ge(bias_added, T)
                    m = NORM[("n2", l)] + t
                    square(m, x[:, t, :], xn[:, t, :])
                    return
                if kind == "logit":
                    t = args[0]
                    act_e.wait_ge(drained_v, drains("V", n))
                    sc.activation(shifted[:, t, :], shifted[:, t, :], ACT.Exp, accum_out=aff_cols[:, 1, t:t + 1])\
                      .then_inc(aff_exp_done, 1)
                    return
                ready = ()
                if kind == "moments":
                    ready = (K8 - 1,)
                elif kind == "taps" and args[0] >= 2:
                    ready = (0, 1) if args[0] == 2 else (args[0] - 1,)
                for c in ready:
                    act_e.wait_ge(centred, c + 1)
                    if c >= 2:
                        act_e.wait_ge(moments_added, c - 1)
                    sc.activation(ln_sq[:, c % 2, :], conv[:, c, :], ACT.Square).then_inc(sq_ready, 1)
                if kind == "pwa":
                    c = args[0]
                    act_e.wait_ge(drained_v, drains("V", n))
                    if c >= 2:
                        act_e.wait_ge(conv_done, c - 1)
                    for i in range(POOL_TAPS):
                        j = dve_taps(c) + i
                        k = (POOL_TAPS - 1) * c + i - 1
                        if i and k >= 2:
                            act_e.wait_ge(product_added, k - 1)
                        sc.activation(products[k % 2] if i else pool_taps[:, c % 2, :], u_pad[:, c % 2, j:j + N],
                                      ACT.Copy, scale=dwT[:, c, j:j + 1]).then_inc(product_ready, 1)
                    return
                if kind == "moments":
                    act_e.wait_ge(drained_v, drains("V", n))
                    sc.activation(ln_rstd, ln_rstd, ACT.Sqrt).then_inc(ln_root_done, 1)
                    for t in range(T):
                        act_e.wait_ge(scaled, t + 1)
                        for c in range(K8):
                            part = conv[:, c, t * 128:(t + 1) * 128]
                            sc.activation(part, part, ACT.Silu, bias=lnb[:, c:c + 1], scale=lng[:, c:c + 1])\
                              .then_inc(swish_done, 1)
                    return
                if engine != "S":
                    return
                if kind == "ada":
                    last = sc.activation(ada_rows[:, args[0] % 2, :], B, ACT.Copy)
                elif kind == "xT":
                    act_e.wait_ge(drained_v, drains("V", place(0, "sel", 1)))
                    k = args[0]
                    last = sc.activation(hT[:, k, :], B, ACT.Identity, bias=cols[:, 0, 0, 0, k:k + 1],
                                         scale=amp[:, 0, 0, 0, k:k + 1])
                elif kind == "cT":
                    act_e.wait_ge(drained_v, drains("V", place(0, "sel", 1)))
                    for i in range(2):
                        k = 2 * args[0] + i
                        last = sc.activation(hcT[:, k, :], B[:, i * NCTX:(i + 1) * NCTX], ACT.Identity,
                                             bias=cols[:, 0, 0, 1, k:k + 1], scale=amp[:, 0, 0, 1, k:k + 1])
                elif kind == "zpool":
                    last = sc.activation(u_pool[:, args[0], :], B, ACT.Copy)
                elif kind == "latT":
                    t = args[0]
                    act_e.wait_ge(attn_w_in, 16 * 4)
                    if t < T:
                        for i in range(2):
                            sc.activation(qlatT[:, i, t * 128:(t + 1) * 128], B[:, i * 128:(i + 1) * 128], ACT.Copy,
                                          scale=qg[:, i:i + 1])
                    at = (t - T if t >= T else CT + t) * 128
                    sc.activation(kvT[:, at:at + 128], B[:, 256:384], ACT.Copy, scale=kvg[:, 0:1])
                    last = sc.activation(kT[64:128, at:at + 128], B[0:64, 384:512], ACT.Copy)
                elif kind == "poolw":
                    last = sc.activation(catT[:, args[0], :], B, ACT.Copy, scale=pscale[:, args[0]:args[0] + 1])
                elif kind == "value":
                    last = sc.activation(values[:, args[0], :], B, ACT.Copy)
                elif kind == "row":
                    s, half = args
                    row = (g1_row if s == 2 else g2_row)[:, :].rearrange("p (n k) -> p k n", k=K8)
                    last = sc.activation(row[:, 4 * half:4 * half + 4, :], B.rearrange("p (k n) -> p k n", k=4), ACT.Copy)
                elif kind in ("hT", "h1T"):
                    t, half = args
                    norm = int(kind == "hT")
                    if l:
                        act_e.wait_ge(cols_ready, 1)
                    for i in range(4):
                        k = 4 * half + i
                        last = sc.activation(hT[:, k, t * 128:(t + 1) * 128], B[:, i * 128:(i + 1) * 128],
                                             ACT.Identity, bias=cols[:, l, 3 * norm, 0, k:k + 1],
                                             scale=amp[:, l, norm, 0, k:k + 1])
                elif kind == "affT":
                    last = sc.activation(affT[0:EXPERTS, :], B[0:EXPERTS, :], ACT.Copy)
                elif kind == "pwg":
                    c = args[0]
                    if c >= 2:
                        act_e.wait_ge(drained_v, drains("V", place(1, "pwa", c - 2)))
                    last = sc.activation(sig[:, c % 2, :], B, ACT.Sigmoid, bias=g_bias[:, c:c + 1])
                last.then_inc(drained_s, 1)
                if (kind, args) == ("pwg", (0,)):
                    act_e.dma_start(bias_row, b_pw2[0, :].unsqueeze(0).to_broadcast([128, D])).then_inc(bias_in, 16)

            act_e.wait_ge(cond_in, 32)
            for v in range(2):
                sc.activation(cond[:, :, 16 * v:16 * v + 16], cond_raw[:, v, :].unsqueeze(2).to_broadcast([128, K8, 16]),
                              ACT.Silu).then_inc(cond_ready, 1)
            act_e.wait_ge(x_arrived, 16)
            for t in range(T):
                square(t, x[:, t, :], xn[:, t, :])
            act_e.wait_ge(ctx_arrived, 16)
            for t in range(CT):
                square(NORM["ctx"] + t, ctx_x[:, t, :], hT_flat[:, t * D:(t + 1) * D])
            for n in range(len(L0)):
                drain(n)

            S = [PS[:, 2 * b:2 * b + 2, :].rearrange("p a b -> p (a b)") for b in range(2)]

            def queries(h):
                act_e.wait_ge(q_projected, h + 1)
                if not isinstance(h, int) or h > 0:
                    act_e.wait_ge(scores_ready, 4 * h)
                sc.activation(qT[0:NOPE, :], PS[0:NOPE, 7, :], ACT.Copy).then_inc(q_nope_done, 1)

            def two_keys(j):
                act_e.wait_ge(k_projected, j + 1)
                if not isinstance(j, int) or j > 0:
                    act_e.wait_ge(scores_ready, 8 * j)
                for odd in range(2):
                    sc.activation(keys[odd][0:NOPE, :], S[0][64 * odd:64 * odd + NOPE, 0:768], ACT.Copy)\
                      .then_inc(k_nope_done, 1)

            def output(j, odd):
                act_e.wait_ge(o_ready, 2 * j + odd + 1)
                for i in range(2):
                    last = sc.activation(hT_flat[64 * odd:64 * odd + VD, bass.ds(j * N + (4 * N + 256 * i), 256)],
                                         PS[64 * i:64 * i + VD, 6, 0:256], ACT.Copy)
                last.then_inc(o_done, 1)

            def late_rows_out(h, b):
                act_e.wait_ge(late_filled, 2 * h + b + 1)
                sc.activation(ada_rows[:, b, :], PS[:, 7, :], ACT.Copy).then_inc(late_rows, 1)

            def head(j, odd, first, more, late):
                h = 2 * j + odd
                for qt in range(T):
                    if late and qt == 0:
                        late_rows_out(h, 0)
                    act_e.wait_ge(bias_ready, 4 * h + qt + 1)
                    if not (first and qt < 2):
                        act_e.wait_ge(pT_ready, 4 * h + qt - 1)
                    sc.activation(exps[:, qt % 2, :], S[qt % 2][:, 0:768], ACT.Exp, bias=biases[:, qt:qt + 1],
                                  scale=SCALE, accum_out=sums[:, qt:qt + 1]).then_inc(exp_done, 1)
                    if late and qt == 1:
                        late_rows_out(h, 1)
                    if qt == 2 and not first:
                        output(*((j, 0) if odd else (j - 1, 1)))
                if more:
                    queries(h + 1)

            def two_heads(j, first=False, more=True):
                head(j, 0, first, True, more)
                head(j, 1, False, more, more)
                if more:
                    two_keys(j + 1)

            act_e.wait_ge(drained_s, drains("S", len(L0) - 1))
            sc.activation(kT_odd[64:128, :], kT[64:128, :], ACT.Copy).then_inc(odd_keys_set, 1)
            queries(0)
            two_keys(0)
            two_heads(0, first=True)
            with act_e.Fori(1, HEADS // 2 - 1, 1) as j:
                two_heads(j)
            two_heads(HEADS // 2 - 1, more=False)
            output(HEADS // 2 - 1, 1)
            for n in range(len(L0), IN_L1):
                drain(n)

            def gathered(l, g):
                act_e.wait_ge(xs_filled, g * 2 + 2)
                for i in range(4):
                    k = 4 + i
                    last = sc.activation(xsT[:, k, :], PS[:, 1, i * 128:(i + 1) * 128], ACT.Identity,
                                         bias=cols[:, l, 3, 0, k:k + 1], scale=amp[:, l, 1, 0, k:k + 1])
                last.then_inc(xs_drained_s, 1)

            def pair(l, j, more):
                g = j + PAIRS * l
                act_e.wait_ge(moe_used, g * 12 + 4)
                for half in range(2):
                    sc.activation(silu_g[:, half, :], PS[:, half, :], ACT.Silu).then_inc(silu_done, 1)
                act_e.wait_ge(aT_filled, g * 2 + 2)
                sc.activation(actT[:, 4:8, :].rearrange("p a b -> p (a b)"), PS[:, 7, :], ACT.Copy)\
                  .then_inc(aT_drained_s, 1)
                if more:
                    gathered(l, g + 1)

            def mixture(l):
                gathered(l, PAIRS * l)
                with act_e.Fori(0, PAIRS - 1, 1) as j:
                    pair(l, j, True)
                pair(l, PAIRS - 1, False)

            mixture(0)
            for t in range(T):
                act_e.wait_ge(scat_added, 8 * PAIRS - 8 + 2 * t + 2)
                square(NORM[("n1", 1)] + t, x[:, t, :], xn[:, t, :])
            for n in range(IN_L1, len(ITEMS)):
                drain(n)
            act_e.wait_ge(x_updated, 16)
            act_e.dma_start(g1_row[:, :], final_g.unsqueeze(0).to_broadcast([128, D])).then_inc(final_in, 16)
            mixture(1)
            for t in range(T):
                act_e.wait_ge(scat_added, 16 * PAIRS - 8 + 2 * t + 2)
                square(NORM["final"] + t, x[:, t, :], xn[:, t, :])

        @block.vector
        def _(dve):
            v = nc.vector
            chain = Chain(dve, v_chain)

            def normalise(m, dst, src):
                dve.wait_ge(rstd_ready, m + 1)
                v.tensor_scalar(dst, src, rstd[:, m:m + 1], None, ALU.mult).then_inc(xn_ready, 1)

            def amplitude(l, norm, samples=1):
                for i in range(samples):
                    last = v.scalar_tensor_tensor(amp[:, l, norm, i, :], cols[:, l, 3 * norm + 1, i, :], 1.0,
                                                  ng[:, l, norm, :], ALU.add, ALU.mult)
                return last

            cols_flat = cols[:, :, :, :, :].rearrange("p a b v k -> p (a b v k)")
            bias_flat = ada_bias[:, :, :, :].rearrange("p a b k -> p (a b k)")

            def section(n, B):
                return v.tensor_tensor(cols_flat[:, bass.ds(n * 2 * K8, 2 * K8)].rearrange("p (v k) -> p v k", v=2),
                                       B[:, 0:2 * K8].rearrange("p (k v) -> p v k", v=2),
                                       bias_flat[:, bass.ds(n * K8, K8)].unsqueeze(1).to_broadcast([128, 2, K8]), ALU.add)

            def make_diag(l, s):
                v.tensor_tensor(diags[(l, s)], ident.unsqueeze(1).to_broadcast([128, K8, 128]),
                                cols[:, l, s, 0, :].unsqueeze(2).to_broadcast([128, K8, 128]), ALU.mult)\
                 .then_inc(diag_ready, 1)

            def residual(l, t, half, B):
                tmp = (odd_taps if l else ada_rows)[:, half, :]
                if t == 0 and half == 0:
                    dve.wait_ge(drained_s, drains("S", place(l, "row", 2, 1)))
                v.tensor_tensor(tmp, B, g1_row[:, half * N:(half + 1) * N], ALU.mult).then_inc(drained_v, 1)
                dve.wait_ge(drained_v, drains("V", place(l, "pw2" if l else "mix", t, half)))
                if l:
                    dve.wait_ge(bias_added, t + 1)
                v.tensor_tensor(x[:, t, half * N:(half + 1) * N], x[:, t, half * N:(half + 1) * N], tmp, ALU.add)\
                 .then_inc(x_updated, 1)

            def choose(l):
                dve.wait_ge(drained_s, drains("S", place(l, "affT")))
                src = affT[0:EXPERTS, :]
                for r in range(CAP // 8):
                    chain(v.max(top8[0:EXPERTS, :], src))
                    chain(v.match_replace(left[0:EXPERTS, :], top8[0:EXPERTS, :], src, -1.0))
                    src = left[0:EXPERTS, :]
                mask = affT[0:EXPERTS, :]
                chain(v.tensor_scalar(mask, src, 0.0, None, ALU.is_lt))
                chain(v.tensor_tensor_scan(running[0:EXPERTS, :], mask, mask, 0.0, ALU.add, ALU.max))
                chain(v.tensor_tensor(running[0:EXPERTS, :], running[0:EXPERTS, :], mask, ALU.mult))
                v.tensor_scalar(left[0:EXPERTS, :], running[0:EXPERTS, :], -1.0, None, ALU.add)\
                 .then_inc(slots_ready, 1)

            def drain(n):
                l = int(n >= IN_L1)
                kind, args, engine = ITEMS[n]
                B = PS[:, bank_of(n)[0], :]
                if kind == "affT":
                    choose(l)
                    return
                if engine != "V":
                    return
                dve.wait_ge(filled, n + 1)
                if n:
                    dve.wait_ge(drained_v, drains("V", n - 1))
                if kind == "params":
                    v.tensor_copy(dwT[:, :, :].rearrange("p a b -> p (a b)"), B[:, 0:K8 * CONVW])
                    last = v.tensor_copy(vecT[:, :], B[:, 256:256 + VEC_ROWS])
                elif kind == "sel":
                    s = args[0]
                    if s == 0:
                        dve.wait_ge(small_in, 16 * 8)
                    if s == 1:
                        chain(section(s, B))
                        amplitude(0, 0, 2).then_inc(drained_v, 1)
                    else:
                        section(s, B).then_inc(drained_v, 1)
                    dve.wait_ge(drained_v, drains("V", n))
                    if s == 2:
                        make_diag(0, 2)
                    return
                elif kind in ("xT", "cT"):
                    i = int(kind == "cT")
                    for j in range(1 + i):
                        k = 2 * args[0] + j if i else args[0]
                        dst, src = (hcT[:, k, :], B[:, j * NCTX:(j + 1) * NCTX]) if i else (hT[:, k, :], B)
                        last = v.tensor_scalar(dst, src, amp[:, 0, 0, i, k:k + 1], cols[:, 0, 0, i, k:k + 1],
                                               ALU.mult, ALU.add)
                elif kind == "zlat":
                    t = args[0]
                    seq = LAT_ORDER.index(t)
                    row = lat[:, seq % 2, :]
                    dve.wait_ge(lat_rstd_ready, seq + 1)
                    if seq >= 2:
                        dve.wait_ge(filled, place(0, "latT", LAT_ORDER[seq - 2]) + 1)
                    off = 0
                    if t < T:
                        v.tensor_scalar(row[:, 0:QL], B[:, 0:QL], lat_rstd[:, t, 0:1], None, ALU.mult)
                        off = QL
                    v.tensor_scalar(row[:, QL:QL + KVL], B[:, off:off + KVL], lat_rstd[:, t, 1:2], None, ALU.mult)
                    kr = B[:, off + KVL:off + KVL + ROPE]
                    if t < T:
                        if t == 0:
                            dve.wait_ge(attn_w_in, 16 * 4)
                        v.tensor_tensor(kr_tmp[:, 0, :], kr, rope_k[:, 0, t, :], ALU.mult)
                        kr4 = kr.rearrange("p (a h f) -> p a h f", a=2, h=2)
                        to4 = kr_tmp[:, 1, :].rearrange("p (a h f) -> p a h f", a=2, h=2)
                        sin4 = rope_k[:, 1, t, :].rearrange("p (a h f) -> p a h f", a=2, h=2)
                        for h in range(2):
                            last = v.tensor_tensor(to4[:, :, h, :], kr4[:, :, 1 - h, :], sin4[:, :, h, :], ALU.mult)
                        chain(last)
                        for h in range(2):
                            last = v.tensor_tensor(row[:, QL + KVL + h * ROPE:QL + KVL + (h + 1) * ROPE],
                                                   kr_tmp[:, 0, :], kr_tmp[:, 1, :], ALU.add)
                    else:
                        for h in range(2):
                            last = v.tensor_copy(row[:, QL + KVL + h * ROPE:QL + KVL + (h + 1) * ROPE], kr)
                elif kind == "band":
                    if args[0] >= 2:
                        dve.wait_ge(filled, place(0, "poolw", args[0] - 2) + 1)
                    last = v.tensor_copy(diffT[:, args[0] % 2, :], B)
                elif kind == "value":
                    last = v.tensor_copy(values[:, args[0], :], B)
                elif kind == "row":
                    s, half = args
                    row = (g1_row if s == 2 else g2_row)[:, :].rearrange("p (n k) -> p k n", k=K8)
                    last = v.tensor_copy(row[:, 4 * half:4 * half + 4, :], B.rearrange("p (k n) -> p k n", k=4))
                elif kind in ("mix", "pw2"):
                    t, half = args
                    residual(l, t, half, B)
                    if half and t == 0:
                        normalise(NORM[("n2", l)], xn[:, 0, :], x[:, 0, :])
                    return
                elif kind in ("hT", "h1T"):
                    t, half = args
                    norm = int(kind == "hT")
                    for i in range(4):
                        k = 4 * half + i
                        last = v.tensor_scalar(hT[:, k, t * 128:(t + 1) * 128], B[:, i * 128:(i + 1) * 128],
                                               amp[:, l, norm, 0, k:k + 1], cols[:, l, 3 * norm, 0, k:k + 1],
                                               ALU.mult, ALU.add)
                elif kind == "logit":
                    t = args[0]
                    chain(v.reduce_max(aff_cols[:, 0, t:t + 1], B[:, 0:EXPERTS], AX.X))
                    v.tensor_scalar(shifted[:, t, :], B[:, 0:EXPERTS], aff_cols[:, 0, t:t + 1], None, ALU.subtract)\
                     .then_inc(drained_v, 1)
                    if t < T - 1:
                        normalise(NORM[("n2", l)] + t + 1, xn[:, t + 1, :], x[:, t + 1, :])
                    dve.wait_ge(aff_exp_done, T * l + t + 1)
                    chain(v.reciprocal(aff_cols[:, 2, t:t + 1], aff_cols[:, 1, t:t + 1]))
                    v.tensor_scalar(aff[:, t, :], shifted[:, t, :], aff_cols[:, 2, t:t + 1], None, ALU.mult)\
                     .then_inc(aff_ready, 1)
                    return
                elif kind == "slotT":
                    v.tensor_copy(slot_of.rearrange("p a b -> p (a b)"), B[:, 0:T * EXPERTS]).then_inc(drained_v, 1)
                    return
                elif kind == "pwa":
                    c = args[0]
                    dve.wait_ge(drained_s, drains("S", place(1, "pwg", c)))
                    if c == 0:
                        dve.wait_ge(halo_set, 4)
                    if c >= 2:
                        dve.wait_ge(filled, place(1, "taps", c - 2) + 1)
                        dve.wait_ge(product_ready, POOL_TAPS * (c - 1))
                    v.scalar_tensor_tensor(u_pad[:, c % 2, HALO:HALO + N], B, a_bias[:, c:c + 1], sig[:, c % 2, :],
                                           ALU.add, ALU.mult).then_inc(drained_v, 1)
                    dve.wait_ge(drained_v, drains("V", n))
                    if c > 1:
                        dve.wait_ge(conv_done, c - 1)
                    for j in range(dve_taps(c)):
                        to = (conv[:, c, :], odd_taps[:, c % 2, :])[j % 2]
                        step = (even_step, odd_step)[j % 2]
                        u = u_pad[:, c % 2, j:j + N]
                        if j == 0:
                            ins = v.tensor_scalar(to, u, dwT[:, c, 0:1], dw_bias[:, c:c + 1], ALU.mult, ALU.add)
                        elif j == 1:
                            ins = v.tensor_scalar(to, u, dwT[:, c, 1:2], None, ALU.mult)
                        else:
                            dve.wait_ge(step, dve_steps(j % 2, c) + j // 2)
                            ins = v.scalar_tensor_tensor(to, u, dwT[:, c, j:j + 1], to, ALU.mult, ALU.add)
                        ins.then_inc(step, 1)
                    return
                elif kind == "taps":
                    c = args[0]
                    dve.wait_ge(odd_step, dve_steps(1, c + 1))
                    last = v.tensor_tensor(odd_taps[:, c % 2, :], odd_taps[:, c % 2, :], B, ALU.add)
                    if c == K8 - 1:
                        last.then_inc(drained_v, 1)
                        dve.wait_ge(drained_v, drains("V", n))
                        dve.wait_ge(even_step, dve_steps(0, c + 1))
                        chain(v.tensor_tensor(conv[:, c, :], conv[:, c, :], odd_taps[:, c % 2, :], ALU.add))
                        dve.wait_ge(product_added, (POOL_TAPS - 1) * (c + 1))
                        chain(v.tensor_tensor(conv[:, c, :], conv[:, c, :], pool_taps[:, c % 2, :], ALU.add))
                        dve.wait_ge(centred, c)
                        v.tensor_tensor(conv[:, c, :], conv[:, c, :], shift, ALU.subtract).then_inc(centred, 1)
                        return
                elif kind == "shift":
                    last = v.tensor_scalar(shift, B, 1.0 / 128, None, ALU.mult)
                elif kind == "moments":
                    dve.wait_ge(centred, K8)
                    chain(v.tensor_copy(ln_mean, PS[:, 6, :]))
                    chain(v.tensor_tensor(shift, ln_mean, ln_mean, ALU.mult))
                    v.scalar_tensor_tensor(ln_rstd, PS[:, 7, :], EPS, shift, ALU.add, ALU.subtract)\
                     .then_inc(drained_v, 1)
                    dve.wait_ge(ln_root_done, 1)
                    for t in range(T):
                        chain(v.reciprocal(ln_rstd[:, t * 128:(t + 1) * 128], ln_rstd[:, t * 128:(t + 1) * 128]))
                        part = conv[:, :, t * 128:(t + 1) * 128]
                        mean, root = (a[:, t * 128:(t + 1) * 128].unsqueeze(1).to_broadcast([128, K8, 128])
                                      for a in (ln_mean, ln_rstd))
                        chain(v.tensor_tensor(part, part, mean, ALU.subtract))
                        v.tensor_tensor(part, part, root, ALU.mult).then_inc(scaled, 1)
                    return
                last.then_inc(drained_v, 1)

            v.memset(ones[:, :], 1.0).then_inc(ones_set, 1)
            v.memset(one_dth[:, :], 1.0 / D).then_inc(ones_set, 1)
            v.memset(minus_half[:, :], -0.5).then_inc(ones_set, 1)
            for t in range(T):
                normalise(t, xn[:, t, :], x[:, t, :])
            for t in range(CT):
                normalise(NORM["ctx"] + t, ctx_x[:, t, :], ctx_x[:, t, :])
            for n in range(len(L0)):
                drain(n)

            S = [PS[:, 2 * b:2 * b + 2, :].rearrange("p a b -> p (a b)") for b in range(2)]
            PT = PS[:, 4:6, :].rearrange("p a b -> p (a b)")

            def rotate(h):
                dve.wait_ge(q_projected, h + 1)
                if not isinstance(h, int) or h > 0:
                    dve.wait_ge(scores_ready, 4 * h)
                v.tensor_tensor(qT[64:128, :], PS[64:128, 7, :], rope_q[64:128, :], ALU.mult).then_inc(q_rope_done, 1)

            def turned(h, qt):
                dve.wait_ge(pT_ready, 4 * h + qt + 1)
                if not (isinstance(h, int) and h == 0):
                    dve.wait_ge(o_ready, h)
                v.tensor_copy(pT[:, qt, :], PT[:, 0:768]).then_inc(pT_drained, 1)

            def divide(h, qt):
                unit = 4 * h + qt
                dve.wait_ge(exp_done, unit + 1)
                v.reciprocal(recips[:, qt:qt + 1], sums[:, qt:qt + 1]).then_inc(recip_done, 1)
                dve.wait_ge(recip_done, unit + 1)
                v.tensor_scalar(exps[:, qt % 2, :], exps[:, qt % 2, :], recips[:, qt:qt + 1], None, ALU.mult)\
                 .then_inc(exp_scaled, 1)

            def head(h, first, more, late):
                for qt in range(T):
                    if late and qt == 3:
                        dve.wait_ge(late_selected, h + 1)
                        section(h + EARLY, PS[:, 7, :]).then_inc(late_added, 1)
                    unit = 4 * h + qt
                    dve.wait_ge(scores_ready, unit + 1)
                    v.reduce_max(maxima[:, qt:qt + 1], S[qt % 2][:, 0:768], AX.X).then_inc(max_step, 1)
                    dve.wait_ge(max_step, unit + 1)
                    v.tensor_scalar(biases[:, qt:qt + 1], maxima[:, qt:qt + 1], -SCALE, None, ALU.mult)\
                     .then_inc(bias_ready, 1)
                    if qt:
                        divide(h, qt - 1)
                    if not (first and qt < 2):
                        turned(*((h, qt - 2) if qt > 1 else (h - 1, qt + 2)))
                if more:
                    rotate(h + 1)
                divide(h, 3)

            rotate(0)
            head(0, True, True, True)
            with dve.Fori(1, LATE, 1) as h:
                head(h, False, True, True)
            head(HEADS - 2, False, True, False)
            head(HEADS - 1, False, False, False)
            turned(HEADS - 1, 2)
            turned(HEADS - 1, 3)
            dve.wait_ge(late_added, LATE)
            make_diag(0, 5)
            chain(amplitude(0, 1))
            for n in range(len(L0), IN_L1):
                drain(n)

            def choose_pair(g, j):
                for dst, scaled_by, built in ((onehot, False, onehot_built), (gated, True, gated_built)):
                    for t in range(T):
                        for e in range(2):
                            s = slot_of[:, t, bass.ds(j * 2 + e, 1)]
                            if scaled_by:
                                last = v.tensor_scalar(dst[:, t, 64 * e:64 * e + 64], iota, s,
                                                       aff[:, t, bass.ds(j * 2 + e, 1)], ALU.is_equal, ALU.mult)
                            else:
                                last = v.tensor_scalar(dst[:, t, 64 * e:64 * e + 64], iota, s, None, ALU.is_equal)
                    last.then_inc(built, 1)

            def gathered(l, g):
                dve.wait_ge(xs_filled, g * 2 + 1)
                for k in range(4):
                    last = v.tensor_scalar(xsT[:, k, :], PS[:, 0, k * 128:(k + 1) * 128], amp[:, l, 1, 0, k:k + 1],
                                           cols[:, l, 3, 0, k:k + 1], ALU.mult, ALU.add)
                last.then_inc(xs_drained_v, 1)

            def gated_turned(g):
                dve.wait_ge(gT_filled, g + 1)
                v.tensor_copy(gatedT, PS[:, 2, :]).then_inc(gT_drained, 1)

            def pair(l, j, more):
                g = j + PAIRS * l
                if more:
                    dve.wait_ge(xs_filled, g * 2 + 2)
                    choose_pair(g + 1, j + 1)
                dve.wait_ge(moe_used, g * 12 + 8)
                for half in range(2):
                    dve.wait_ge(silu_done, g * 2 + half + 1)
                    v.tensor_tensor(act[:, half * N:(half + 1) * N], silu_g[:, half, :], PS[:, 2 + half, :], ALU.mult)\
                     .then_inc(act_done, 1)
                dve.wait_ge(aT_filled, g * 2 + 1)
                v.tensor_copy(actT[:, 0:4, :].rearrange("p a b -> p (a b)"), PS[:, 6, :]).then_inc(aT_drained_v, 1)
                dve.wait_ge(moe_used, g * 12 + 12)
                for half in range(2):
                    v.tensor_tensor(y_rows[:, half * N:(half + 1) * N], PS[:, 4 + half, :],
                                    g2_row[:, half * N:(half + 1) * N], ALU.mult).then_inc(y_done, 1)
                if more:
                    gathered(l, g + 1)
                for i in range(2 * T):
                    dve.wait_ge(scat_filled, g * 8 + i + 1)
                    part = x[:, i // 2, (i % 2) * N:(i % 2 + 1) * N]
                    v.tensor_tensor(part, part, PS[:, 6 + i % 2, :], ALU.add).then_inc(scat_added, 1)
                if more:
                    gated_turned(g + 1)

            def mixture(l):
                choose_pair(PAIRS * l, 0)
                gathered(l, PAIRS * l)
                gated_turned(PAIRS * l)
                with dve.Fori(0, PAIRS - 1, 1) as j:
                    pair(l, j, True)
                pair(l, PAIRS - 1, False)

            dve.wait_ge(drained_v, drains("V", IN_L1 - 1))
            mixture(0)
            amplitude(1, 0)
            amplitude(1, 1).then_inc(cols_ready, 1)
            dve.wait_ge(cols_ready, 1)
            for t in range(T):
                normalise(NORM[("n1", 1)] + t, xn[:, t, :], x[:, t, :])
            for n in range(IN_L1, len(ITEMS)):
                drain(n)
            dve.wait_ge(drained_v, drains("V", len(ITEMS) - 1))
            mixture(1)
            dve.wait_ge(final_in, 16)
            for t in range(T):
                m = NORM["final"] + t
                dve.wait_ge(rstd_ready, m + 1)
                v.scalar_tensor_tensor(xn[:, t, :], x[:, t, :], rstd[:, m:m + 1], g1_row[:, :], ALU.mult, ALU.mult)\
                 .then_inc(out_ready, 1)

        @block.gpsimd
        def _(pool):
            p = nc.gpsimd
            chain = Chain(pool, p_chain)

            def reciprocal_root(m):
                pool.wait_ge(ssq_ready, m + 1)
                chain(p.tensor_scalar(ms[:, m:m + 1], ssq[:, m:m + 1], 1.0 / D, EPS, ALU.mult, ALU.add))
                p.tensor_tensor(rstd[:, m:m + 1], ms[:, m:m + 1], minus_half[:, :], ALU.pow).then_inc(rstd_ready, 1)

            pool.wait_ge(ones_set, 3)
            for m in range(6):
                reciprocal_root(m)
            for seq, t in enumerate(LAT_ORDER):
                pool.wait_ge(lat_ssq_ready, seq + 1)
                a = 0 if t < T else 1
                if t < T:
                    p.tensor_scalar(lat_ms[:, t, 0:1], lat_ssq[:, t, 0:1], 1.0 / QL, EPS, ALU.mult, ALU.add)
                chain(p.tensor_scalar(lat_ms[:, t, 1:2], lat_ssq[:, t, 1:2], 1.0 / KVL, EPS, ALU.mult, ALU.add))
                p.tensor_tensor(lat_rstd[:, t, a:2], lat_ms[:, t, a:2], minus_half[:, :].to_broadcast([128, 2 - a]),
                                ALU.pow).then_inc(lat_rstd_ready, 1)

            pool.wait_ge(attn_w_in, 16 * 4)

            def stage_queries(h):
                if not isinstance(h, int) or h > 0:
                    pool.wait_ge(q_projected, h)
                p.tensor_copy(wq_stage[:, :, 0:QK], uq[:, :, bass.ds(h * QK, QK)])
                for half in range(2):
                    for axis in range(2):
                        to = QK + axis * 16 + half * 8
                        fr = NOPE + axis * 16 + (1 - half) * 8
                        last = p.tensor_copy(wq_stage[:, :, to:to + 8], uq[:, :, bass.ds(h * QK + fr, 8)])
                last.then_inc(q_staged, 1)

            def stage_values(h, odd):
                if not isinstance(h, int) or h > 1:
                    pool.wait_ge(o_ready, h - 1)
                p.tensor_copy(v_stage[odd], values[:, :, bass.ds(h * VD, VD)]).then_inc(v_staged, 1)

            def stage_two_heads(j):
                stage_queries(2 * j)
                if not isinstance(j, int) or j > 0:
                    pool.wait_ge(k_projected, j)
                p.tensor_copy(wk_stage.rearrange("p (a b) -> p a b", a=2),
                              ukv_heads[:, bass.ds(2 * j, 2), 0:NOPE]).then_inc(k_staged, 1)
                if isinstance(j, int):
                    pool.wait_ge(drained_v, drains("V", len(L0) - 1))
                    pool.wait_ge(drained_s, drains("S", len(L0) - 1))
                stage_values(2 * j, 0)
                stage_queries(2 * j + 1)
                stage_values(2 * j + 1, 1)

            ukv_heads = ukv.rearrange("p (h e) -> p h e", h=HEADS)
            stage_two_heads(0)
            with pool.Fori(1, HEADS // 2, 1) as j:
                stage_two_heads(j)
            for t in range(T):
                reciprocal_root(NORM[("n2", 0)] + t)
            for t in range(T):
                reciprocal_root(NORM[("n1", 1)] + t)
            for b in range(2):
                for a in (0, HALO + N):
                    p.memset(u_pad[:, b, a:a + HALO], 0.0).then_inc(halo_set, 1)
            pool.wait_ge(filled, place(1, "h1T", T - 1, 1) + 1)

            def whole(c):
                pool.wait_ge(drained_v, drains("V", place(1, "taps", c)))
                pool.wait_ge(even_step, dve_steps(0, c + 1))
                pool.wait_ge(product_added, (POOL_TAPS - 1) * (c + 1))
                chain(p.tensor_tensor(conv[:, c, :], conv[:, c, :], odd_taps[:, c % 2, :], ALU.add))
                p.tensor_tensor(conv[:, c, :], conv[:, c, :], pool_taps[:, c % 2, :], ALU.add).then_inc(conv_done, 1)
                pool.wait_ge(conv_done, c + 1)

            def centre(c):
                pool.wait_ge(drained_v, drains("V", place(1, "shift")))
                p.tensor_tensor(conv[:, c, :], conv[:, c, :], shift, ALU.subtract).then_inc(centred, 1)

            def taps(c):
                for i in range(1, POOL_TAPS):
                    k = (POOL_TAPS - 1) * c + i - 1
                    pool.wait_ge(product_ready, POOL_TAPS * c + i + 1)
                    if k:
                        pool.wait_ge(product_added, k)
                    to = pool_taps[:, c % 2, :]
                    p.tensor_tensor(to, to, products[k % 2], ALU.add).then_inc(product_added, 1)

            def make_diag(s):
                p.tensor_tensor(diags[(1, s)], ident.unsqueeze(1).to_broadcast([128, K8, 128]),
                                cols[:, 1, s, 0, :].unsqueeze(2).to_broadcast([128, K8, 128]), ALU.mult)\
                 .then_inc(diag_ready, 1)

            make_diag(2)
            for c in [K8 - 1] + list(range(K8 - 1)):
                many = pe_taps(c)
                if 2 <= c < K8 - 1:
                    pool.wait_ge(filled, place(1, "taps", c - 2) + 1)
                for i in range(many):
                    j = CONVW - many + i
                    w = last_diag[:, i, :] if c == K8 - 1 else tap_diag[:, c % 2, i, :]
                    last = p.tensor_scalar(w, ident, dwT[:, c, j:j + 1], None, ALU.mult)
                last.then_inc(tap_diag_ready, 1)
                if 2 <= c < K8 - 1:
                    whole(c - 2)
                if c == 3:
                    centre(0)
                if 3 <= c < K8 - 1:
                    centre(c - 2)
                if c < K8 - 1:
                    taps(c)
            whole(K8 - 3)
            centre(K8 - 3)
            taps(K8 - 1)
            whole(K8 - 2)
            centre(K8 - 2)
            make_diag(5)
            pool.wait_ge(bias_in, 16)
            pool.wait_ge(drained_s, drains("S", place(1, "row", 2, 1)))
            chain(p.tensor_tensor(bias_row, bias_row, g1_row[:, :], ALU.mult))
            for t in range(T):
                p.tensor_tensor(x[:, t, :], x[:, t, :], bias_row, ALU.add).then_inc(bias_added, 1)
            for t in range(T):
                reciprocal_root(NORM[("n2", 1)] + t)
            for t in range(T):
                reciprocal_root(NORM["final"] + t)


_INS = ["x", "c", "ctx", "c_ctx", "ada_w", "ada_b", "norm1_g", "norm2_g", "mix_w_in", "pool_w", "pool_scale",
        "q_norm_g", "kv_norm_g", "w_uq", "w_ukv", "mix_w_out", "conv_w_pw1", "conv_b_pw1", "conv_w_dw", "conv_b_dw",
        "conv_ln_g", "conv_ln_b", "conv_w_pw2", "conv_b_pw2", "router_w", "exp_wg", "exp_wu", "exp_wd", "final_g"]


def tables():
    import numpy as np
    small = np.zeros((128, 194), np.float32)
    small[:, 0:128] = np.eye(128, dtype=np.float32)
    small[:, 128:192] = np.arange(64, dtype=np.float32)
    small[0::32, 192] = 1.0
    small[16::32, 193] = 1.0
    tok = np.arange(N)
    inv = (1.0 / (10000.0 ** (np.arange(0, 16, 2, dtype=np.float32) / 16))).astype(np.float32)
    pos = np.stack([tok // 64, tok % 64], 1).astype(np.float32)
    ang = (pos[:, :, None] * inv).astype(np.float32)
    cos = np.repeat(np.cos(ang)[:, :, None, :], 2, axis=2).reshape(N, ROPE).astype(np.float32)
    sin = (np.repeat(np.sin(ang)[:, :, None, :], 2, axis=2)
           * np.array([-1.0, 1.0])[None, None, :, None]).reshape(N, ROPE).astype(np.float32)
    rope = np.zeros((128, N + 2 * T * ROPE), np.float32)
    rope[64:96, 0:N] = cos.T
    rope[96:128, 0:N] = sin.T
    rope[:, N:N + T * ROPE] = cos.reshape(T, 128, ROPE).transpose(1, 0, 2).reshape(128, T * ROPE)
    rope[:, N + T * ROPE:] = sin.reshape(T, 128, ROPE).transpose(1, 0, 2).reshape(128, T * ROPE)
    band = np.zeros((128, 4, 5, 128), np.float32)
    for g, w in enumerate((2, 4, 8, 16)):
        lo, hi = np.clip(tok - w // 2, 0, N), np.clip(tok - w // 2 + w, 0, N)
        inside = (tok[:, None] >= lo) & (tok[:, None] < hi)
        full = inside / (hi - lo).astype(np.float32) - np.eye(N)
        for b, (i, o) in enumerate(((0, 1), (1, 1), (2, 1), (0, 0), (3, 3))):
            band[:, g, b, :] = full[i * 128:(i + 1) * 128, o * 128:(o + 1) * 128]
    return {"small_tab": small, "rope_tab": rope, "band_tab": band.reshape(128, 20 * 128)}


def kernel(**inputs):
    import numpy as _np
    import concourse.bacc as _bacc
    from concourse import mybir as _mybir
    from concourse.bass_utils import run_bass_kernel_spmd as _run

    nc = _bacc.Bacc("TRN2", target_bir_lowering=False, num_devices=1)
    given = {n: _np.ascontiguousarray(inputs[n]) for n in _INS}
    given.update(tables())
    arrays, args = {}, []
    for name, a in given.items():
        arrays[f"in_{name}_dram"] = a
        args.append(nc.dram_tensor(f"in_{name}_dram", a.shape, _mybir.dt.from_np(a.dtype), kind="ExternalInput").ap())
    args.append(nc.dram_tensor("out_0_dram", (1, N, D), _mybir.dt.float32, kind="ExternalOutput").ap())
    build(nc, *args)
    r = _run(nc, [arrays], core_ids=[0])
    return r.results[0]["out_0_dram"]
```
